# Optimizing a Trainium2 kernel written in Bass

```python
import jax, jax.numpy as jnp
from jax import lax
import numpy as np

D_MODEL = 1024
BATCH = 1
SEQ = 256
DEPTH = 2

POOL_GROUPS = 4
POOL_GROUP_DIM = 64
POOL_WINDOWS = (2, 4, 8, 16)
POOL_DIM = POOL_GROUPS * POOL_GROUP_DIM
ATT_HEADS = 8
HEAD_DIM = 64
ATT_DIM = ATT_HEADS * HEAD_DIM
MOBA_BLOCK = 256
MOBA_TOPK = 3
MOBA_Q_CHUNK = 64
ROPE_THETA = 10000.0
SGU_GROUPS = 4
SGU_GROUP_DIM = 64
SGU_DIM = SGU_GROUPS * SGU_GROUP_DIM
SGU_CHUNK = 128
CONV_DIM = 256
CONV_WIDTH = 31
N_BRANCH = 4
FF_DIM = -(-8 * D_MODEL // (3 * 256)) * 256
IN_DIM = POOL_DIM + 3 * ATT_DIM + 2 * SGU_DIM + 2 * CONV_DIM
EPS = 1e-6
NEG = -1e30

kernel_name = 'hybrid_pool_moba_sgu_conv_gated_block'

def rms_norm(x, g):
    xf = x.astype(jnp.float32)
    y = xf * lax.rsqrt(jnp.mean(xf * xf, axis=-1, keepdims=True) + EPS)
    return (y * g.astype(jnp.float32)).astype(x.dtype)

def layer_norm(x, g, b):
    xf = x.astype(jnp.float32)
    mu = jnp.mean(xf, axis=-1, keepdims=True)
    var = jnp.mean(jnp.square(xf - mu), axis=-1, keepdims=True)
    y = (xf - mu) * lax.rsqrt(var + EPS)
    return (y * g.astype(jnp.float32) + b.astype(jnp.float32)).astype(x.dtype)

def rope(x, positions):
    half = HEAD_DIM // 2
    inv_freq = 1.0 / (ROPE_THETA ** (jnp.arange(half, dtype=jnp.float32) / half))
    ang = positions.astype(jnp.float32)[..., None] * inv_freq
    cos = jnp.cos(ang)[:, :, None, :]
    sin = jnp.sin(ang)[:, :, None, :]
    xf = x.astype(jnp.float32)
    x1, x2 = xf[..., :half], xf[..., half:]
    out = jnp.concatenate([x1 * cos - x2 * sin, x2 * cos + x1 * sin], axis=-1)
    return out.astype(x.dtype)

def pool_mixer(xa, pool_w, pool_scale):
    B, S, _ = xa.shape
    xf = xa.astype(jnp.float32).reshape(B, S, POOL_GROUPS, POOL_GROUP_DIM)
    cs = jnp.cumsum(xf, axis=1)
    t = jnp.arange(S)
    outs = []
    for g, w in enumerate(POOL_WINDOWS):
        c = cs[:, :, g]
        lagged = jnp.pad(c, ((0, 0), (w, 0), (0, 0)))[:, :S]
        cnt = jnp.minimum(t + 1, w).astype(jnp.float32)[None, :, None]
        outs.append((c - lagged) / cnt - xf[:, :, g])
    pooled = jnp.stack(outs, axis=2)
    mixed = jnp.einsum('bsgc,gcd->bsgd', pooled, pool_w.astype(jnp.float32))
    return (mixed.reshape(B, S, POOL_DIM) * pool_scale.astype(jnp.float32)).astype(xa.dtype)

def moba_attention(q, k, v):
    B, S, H, Dh = q.shape
    s_pad = -(-S // MOBA_BLOCK) * MOBA_BLOCK
    pad = ((0, 0), (0, s_pad - S), (0, 0), (0, 0))
    q, k, v = jnp.pad(q, pad), jnp.pad(k, pad), jnp.pad(v, pad)
    nb = s_pad // MOBA_BLOCK
    nq = s_pad // MOBA_Q_CHUNK
    top = min(MOBA_TOPK, nb)
    scale = HEAD_DIM ** -0.5
    kb = k.transpose(0, 2, 1, 3).reshape(B, H, nb, MOBA_BLOCK, Dh)
    vb = v.transpose(0, 2, 1, 3).reshape(B, H, nb, MOBA_BLOCK, Dh)
    kmean = jnp.mean(kb.astype(jnp.float32), axis=3)
    q_chunks = q.transpose(0, 2, 1, 3).reshape(B, H, nq, MOBA_Q_CHUNK, Dh).transpose(2, 0, 1, 3, 4)
    b_idx = jnp.arange(B)[:, None, None, None]
    h_idx = jnp.arange(H)[None, :, None, None]
    blk_ids = jnp.arange(nb)
    key_off = jnp.arange(MOBA_BLOCK)
    q_off = jnp.arange(MOBA_Q_CHUNK)

    def one_chunk(args):
        c, qc = args
        qf = qc.astype(jnp.float32)
        blk = (c * MOBA_Q_CHUNK) // MOBA_BLOCK
        gate = jnp.einsum('bhqd,bhnd->bhqn', qf, kmean)
        gate = jnp.where(blk_ids < blk, gate, NEG)
        _, sel = lax.top_k(gate, top)
        sel_valid = sel < blk
        ks = kb[b_idx, h_idx, sel].astype(jnp.float32)
        vs = vb[b_idx, h_idx, sel].astype(jnp.float32)
        s_sel = jnp.einsum('bhqd,bhqnkd->bhqnk', qf, ks) * scale
        s_sel = jnp.where(sel_valid[..., None], s_sel, NEG).reshape(B, H, MOBA_Q_CHUNK, top * MOBA_BLOCK)
        k_own = lax.dynamic_index_in_dim(kb, blk, axis=2, keepdims=False).astype(jnp.float32)
        v_own = lax.dynamic_index_in_dim(vb, blk, axis=2, keepdims=False).astype(jnp.float32)
        s_own = jnp.einsum('bhqd,bhkd->bhqk', qf, k_own) * scale
        q_pos = c * MOBA_Q_CHUNK + q_off
        k_pos = blk * MOBA_BLOCK + key_off
        s_own = jnp.where(k_pos[None, :] <= q_pos[:, None], s_own, NEG)
        p = jax.nn.softmax(jnp.concatenate([s_sel, s_own], axis=-1), axis=-1)
        p_sel = p[..., :top * MOBA_BLOCK].reshape(B, H, MOBA_Q_CHUNK, top, MOBA_BLOCK)
        p_own = p[..., top * MOBA_BLOCK:]
        o = jnp.einsum('bhqnk,bhqnkd->bhqd', p_sel, vs) + jnp.einsum('bhqk,bhkd->bhqd', p_own, v_own)
        return o.astype(qc.dtype)

    out = lax.map(one_chunk, (jnp.arange(nq), q_chunks))
    out = out.transpose(1, 0, 3, 2, 4).reshape(B, s_pad, H * Dh)
    return out[:, :S]

def spatial_gating(z, norm_g, norm_b, w_s, b_s):
    B, S, _ = z.shape
    u, v = z[..., :SGU_DIM], z[..., SGU_DIM:]
    v = layer_norm(v, norm_g, norm_b)
    nc = S // SGU_CHUNK
    vc = v.astype(jnp.float32).reshape(B, nc, SGU_CHUNK, SGU_GROUPS, SGU_GROUP_DIM)
    mask = jnp.tril(jnp.ones((SGU_CHUNK, SGU_CHUNK), dtype=bool))
    ws = jnp.where(mask[None], w_s.astype(jnp.float32), 0.0)
    f = jnp.einsum('gts,bnsgc->bntgc', ws, vc) + b_s.astype(jnp.float32).T[None, None, :, :, None]
    return (u.astype(jnp.float32) * f.reshape(B, S, SGU_DIM)).astype(z.dtype)

def conv_module(xd, conv_w, conv_b, norm_g, norm_b):
    a, g = xd[..., :CONV_DIM], xd[..., CONV_DIM:]
    h = a * jax.nn.sigmoid(g)
    h = lax.conv_general_dilated(
        h, conv_w[:, None, :], window_strides=(1,), padding=[(CONV_WIDTH - 1, 0)],
        dimension_numbers=('NWC', 'WIO', 'NWC'), feature_group_count=CONV_DIM) + conv_b
    return jax.nn.silu(layer_norm(h, norm_g, norm_b))

def setup_inputs(seed: int = 0) -> dict:
    key = jax.random.key(seed)
    ks = jax.random.split(key, 32)
    L, D = DEPTH, D_MODEL

    def nrm(k, shape, scale):
        return jax.random.normal(k, shape, jnp.float32) * scale

    x = nrm(ks[0], (BATCH, SEQ, D), 1.0)
    positions = (jax.random.randint(ks[1], (BATCH, 1), 0, 1024) + jnp.arange(SEQ)[None, :]).astype(jnp.int32)
    return {
        'x': x,
        'positions': positions,
        'norm_mix_g': 1.0 + nrm(ks[2], (L, D), 0.05),
        'w_in': nrm(ks[3], (L, D, IN_DIM), D ** -0.5),
        'w_gate': nrm(ks[4], (L, D, N_BRANCH * D), D ** -0.5),
        'b_gate': nrm(ks[5], (L, N_BRANCH * D), 0.1),
        'pool_w': nrm(ks[6], (L, POOL_GROUPS, POOL_GROUP_DIM, POOL_GROUP_DIM), POOL_GROUP_DIM ** -0.5),
        'pool_scale': 1.0 + nrm(ks[7], (L, POOL_DIM), 0.1),
        'sgu_norm_g': 1.0 + nrm(ks[8], (L, SGU_DIM), 0.05),
        'sgu_norm_b': nrm(ks[9], (L, SGU_DIM), 0.02),
        'sgu_w': nrm(ks[10], (L, SGU_GROUPS, SGU_CHUNK, SGU_CHUNK), SGU_CHUNK ** -0.5),
        'sgu_b': 1.0 + nrm(ks[11], (L, SGU_GROUPS, SGU_CHUNK), 0.1),
        'conv_w': nrm(ks[12], (L, CONV_WIDTH, CONV_DIM), CONV_WIDTH ** -0.5),
        'conv_b': nrm(ks[13], (L, CONV_DIM), 0.02),
        'conv_norm_g': 1.0 + nrm(ks[14], (L, CONV_DIM), 0.05),
        'conv_norm_b': nrm(ks[15], (L, CONV_DIM), 0.02),
        'w_proj_a': nrm(ks[16], (L, POOL_DIM, D), POOL_DIM ** -0.5),
        'w_proj_b': nrm(ks[17], (L, ATT_DIM, D), ATT_DIM ** -0.5),
        'w_proj_c': nrm(ks[18], (L, SGU_DIM, D), SGU_DIM ** -0.5),
        'w_proj_d': nrm(ks[19], (L, CONV_DIM, D), CONV_DIM ** -0.5),
        'w_o': nrm(ks[20], (L, D, D), D ** -0.5),
        'norm_ffn_g': 1.0 + nrm(ks[21], (L, D), 0.05),
        'w_ffn_in': nrm(ks[22], (L, D, 2 * FF_DIM), D ** -0.5),
        'w_ffn_out': nrm(ks[23], (L, FF_DIM, D), FF_DIM ** -0.5),
        'final_norm_g': 1.0 + nrm(ks[24], (D,), 0.05),
    }

def reference(x, positions, norm_mix_g, w_in, w_gate, b_gate, pool_w, pool_scale,
              sgu_norm_g, sgu_norm_b, sgu_w, sgu_b, conv_w, conv_b, conv_norm_g, conv_norm_b,
              w_proj_a, w_proj_b, w_proj_c, w_proj_d, w_o, norm_ffn_g, w_ffn_in, w_ffn_out,
              final_norm_g):
    B, S, D = x.shape
    splits = np.cumsum([POOL_DIM, ATT_DIM, ATT_DIM, ATT_DIM, 2 * SGU_DIM]).tolist()
    for l in range(DEPTH):
        xn = rms_norm(x, norm_mix_g[l])
        proj = xn @ w_in[l]
        xa, q, k, v, zc, xd = jnp.split(proj, splits, axis=-1)
        q = rope(q.reshape(B, S, ATT_HEADS, HEAD_DIM), positions)
        k = rope(k.reshape(B, S, ATT_HEADS, HEAD_DIM), positions)
        v = v.reshape(B, S, ATT_HEADS, HEAD_DIM)
        ya = pool_mixer(xa, pool_w[l], pool_scale[l])
        yb = moba_attention(q, k, v)
        yc = spatial_gating(jax.nn.gelu(zc), sgu_norm_g[l], sgu_norm_b[l], sgu_w[l], sgu_b[l])
        yd = conv_module(xd, conv_w[l], conv_b[l], conv_norm_g[l], conv_norm_b[l])
        gates = jax.nn.sigmoid((xn @ w_gate[l] + b_gate[l]).astype(jnp.float32)).reshape(B, S, N_BRANCH, D)
        merged = (gates[:, :, 0] * (ya @ w_proj_a[l]) + gates[:, :, 1] * (yb @ w_proj_b[l])
                  + gates[:, :, 2] * (yc @ w_proj_c[l]) + gates[:, :, 3] * (yd @ w_proj_d[l]))
        x = x + merged.astype(x.dtype) @ w_o[l]
        hn = rms_norm(x, norm_ffn_g[l])
        gu = hn @ w_ffn_in[l]
        x = x + (jax.nn.silu(gu[..., :FF_DIM]) * gu[..., FF_DIM:]) @ w_ffn_out[l]
    return rms_norm(x, final_norm_g)


_drawn_inputs = setup_inputs


def setup_inputs(seed=0):
    import zlib

    import numpy as np

    out = dict(_drawn_inputs(seed))
    spreads = {}
    factors = {'sgu_norm_g': 3.877,
     'sgu_norm_b': 8.0,
     'conv_b': 3.351,
     'conv_norm_b': 6.914,
     'conv_norm_g': 3.013}
    for name, (base, spread) in spreads.items():
        noise = np.random.default_rng([zlib.crc32(name.encode()), seed]).standard_normal(out[name].shape)
        drawn = base * np.exp(spread * noise) if base else spread * noise
        out[name] = __import__('jax').numpy.asarray(drawn.astype(out[name].dtype))
    for name, factor in factors.items():
        out[name] = (out[name] * factor).astype(out[name].dtype)
    return out
```

```python
from contextlib import ExitStack

import numpy as np

import concourse.bass as bass
from concourse import mybir

ALU = mybir.AluOpType
ACT = mybir.ActivationFunctionType
AX = mybir.AxisListType
F32 = mybir.dt.float32
F32R = mybir.dt.float32r
BF16 = mybir.dt.bfloat16
I32 = mybir.dt.int32

P = 128
EPS = 1e-6
NEG = -1e30
WINDOWS = (2, 4, 8, 16)
HEAD_DIM = 64
ROPE_THETA = 10000.0
PAD = 16

RING = 3
UC = 256
W_IN_UNITS = (("q", 256), ("q", 512), ("k", 768), ("k", 1024), ("v", 1280), ("v", 1536),
              ("glu_gate", 2560), ("glu_in", 2304), ("sgu_v", 2048), ("sgu_u", 1792), ("pool", 0))
N_IN = len(W_IN_UNITS)
U_GATE = N_IN
U_PROJ_A = U_GATE + 16
U_PROJ_C = U_PROJ_A + 1
U_PROJ_D = U_PROJ_A + 2
U_PROJ_B = U_PROJ_A + 3
U_WO = U_PROJ_A + 5
U_FFN = U_WO + 4
FF_STEPS = 11
UNITS = U_FFN + 3 * FF_STEPS
USES = UNITS // RING
FF_ITERS = 4
U_LOOP = U_FFN + 2
U_TAIL = U_LOOP + 6 * FF_ITERS
J_TAIL = 1 + 2 * FF_ITERS
GATE_BRANCH = (0, 2, 3, 1)

HIGH_USES = {
    4: ["perm0", "S0", "PV0", "S1", "PV1", "S2", "PV2", "S3", "PV3"],
    5: ["perm1", "S0", "F", "S1", "pool", "S2", "cT1", "S3", "cT2"],
    6: ["par", "perm2", "wsT", "PT0", "PT1", "PT2", "PT3"],
    7: ["stat1", "perm3", "PT0", "PT1", "PT2", "PT3", "stat2"],
}
LOW_MIX = [[u for u in range(U_PROJ_A) if u % 4 == b] for b in range(4)]
FF_USES = [len(range(b // 2, FF_STEPS, 2)) for b in range(4)]
PROJ_ORDER = ("A", "C", "D", "B")
BANK_USES = {b: len(LOW_MIX[b]) + 4 + FF_USES[b] for b in range(4)}
BANK_USES.update({b: len(v) for b, v in HIGH_USES.items()})

ROWS = {"norm_mix_g": (0, 8), "norm_ffn_g": (8, 8), "b_gate": (16, 32), "pool_scale": (48, 2),
        "conv_b": (50, 2), "conv_norm_g": (52, 2), "conv_norm_b": (54, 2), "conv_w": (56, 62)}
N_ROWS = 118
DVE_CHAIN_PER_LAYER = 75
POOL_CHAIN_PER_LAYER = 8
PRE_DVE_ROPE = 18
PRE_DVE_OUT = PRE_DVE_ROPE + 14


def build(nc, T, out, inv_freq, inv_count):
    L, D, IN_DIM = T["w_in"].shape
    S = T["x"].shape[1]
    FF = T["w_ffn_out"].shape[1]
    KT = D // P
    TT = S // P
    CW = T["conv_w"].shape[1]
    HP = 4
    SCALE = float(HEAD_DIM) ** -0.5
    assert FF == FF_STEPS * UC and UNITS % RING == 0 and U_LOOP % RING == 2

    with ExitStack() as ctx:
        def sb(name, shape, dt=F32):
            return ctx.enter_context(nc.sbuf_tensor(name, shape, dt))

        def sem(name):
            return ctx.enter_context(nc.semaphore(name))

        raw = [sb(f"raw{s}", [P, 8 * UC]) for s in range(RING)]
        w_hi = [sb(f"w_hi{s}", [P, 8 * UC], F32R) for s in range(RING)]
        w_lo = [sb(f"w_lo{s}", [P, 8 * UC], F32R) for s in range(RING)]
        x_res = sb("x_res", [P, KT, S])
        sq = sb("sq", [P, KT, S])
        act_hi = sb("act_hi", [P, KT, S], F32R)
        act_lo = sb("act_lo", [P, KT, S], F32R)
        xn = sb("xn", [P, 2, 2, S])
        gates = sb("gates", [P, 4 * KT, S])
        qk = sb("qk", [P, 8, S])
        rot = sb("rot", [P, 2, S])
        v_sb = sb("v_sb", [P, TT, 512])
        y_hi = sb("y_hi", [P, 10, S], F32R)
        y_lo = sb("y_lo", [P, 10, S], F32R)
        conv_h = sb("conv_h", [P, 2, 32 + S])
        xa = sb("xa", [P, 2, PAD + S])
        ff_hi = sb("ff_hi", [P, 2, 2, S], F32R)
        ff_lo = sb("ff_lo", [P, 2, 2, S], F32R)
        yd_f = sb("yd_f", [P, 2, S])

        def part(owner, a, shape):
            flat = owner.rearrange("p k s -> p (k s)") if len(owner.shape) == 3 else owner
            n = int(np.prod(shape))
            return flat[:, a:a + n].rearrange("p (i j) -> p i j", j=shape[-1]) if len(shape) == 2 else flat[:, a:a + n]

        glu_t, conv_a = rot, rot
        probs = part(sq[:, :, :], 0, [2, 3 * P])
        probsT = part(sq[:, :, :], 6 * P, [2, 3 * P])
        conv_n = part(sq[:, :, :], 12 * P, [TT, 256])
        scores = part(xn[:, :, :, :].rearrange("p i f s -> p (i f) s"), 0, [2, 3 * P])
        E = PAD + S
        g_b = gates[:, KT:2 * KT, :]
        s2, s4 = part(g_b, 0, [2, E]), part(g_b, 2 * E, [2, E])
        s8, s16 = part(g_b, 4 * E, [E]), part(g_b, 5 * E, [E])
        g_d = gates[:, 3 * KT:4 * KT, :]
        zv, zu = g_d[:, 0:2, :], g_d[:, 2:4, :]
        yc_f, ya_f, pooled = g_d[:, 4:6, :], g_d[:, 0:2, :], g_d[:, 6:8, :]
        mtmp = part(qk[:, :, :], 0, [2, 2 * S])
        ff_g = part(qk[:, :, :], 0, [2, 2 * S])
        ff_a = part(qk[:, :, :], 4 * S, [2 * S])
        rows = sb("rows", [N_ROWS, P])
        par = sb("par", [P, N_ROWS])
        half_bg = sb("half_bg", [P, 32])
        ln_g = sb("ln_g", [P, 256])
        ln_b = sb("ln_b", [P, 256])
        sgu_bias = sb("sgu_bias", [P, 2, P])
        pool_w = sb("pool_w", [P, 2, P])
        ws_nat = sb("ws_nat", [P, 4, P])
        wsT = sb("wsT", [P, 4, P])
        ident = sb("ident", [P, P])
        ones = sb("ones", [P, P])
        zeros = sb("zeros", [P, 2 * S], BF16)
        rot_perm = sb("rot_perm", [P, P])
        causal = sb("causal", [P, 384])
        cos_t = sb("cos_t", [P, 1, S])
        sin_t = sb("sin_t", [P, 1, S])
        icnt = sb("icnt", [P, 2, S])
        ifreq = sb("ifreq", [P, 1])
        st = sb("st", [P, 16])
        ist = sb("ist", [P, 4], I32)
        diag = sb("diag", [P, TT, P])
        bn6 = sb("bn6", [P, TT, 6])
        mv = sb("mv", [P, TT, 2])
        mx = sb("mx", [P, 4])
        nmx = sb("nmx", [P, 4])
        den = sb("den", [P, 4])
        rden = sb("rden", [P, 4])
        ssq = sb("ssq", [P, 4])

        bank = [ctx.enter_context(nc.psum_tensor(f"bank{b}", [P, 512], F32)) for b in range(8)]

        raw_full = [sem(f"raw_full{s}") for s in range(RING)]
        raw_claimed = sem("raw_claimed")
        hi_ready = [sem(f"hi_ready{s}") for s in range(RING)]
        lo_ready = [sem(f"lo_ready{s}") for s in range(RING)]
        w_used = [sem(f"w_used{s}") for s in range(RING)]
        bank_free = [sem(f"bank_free{b}") for b in range(8)]
        x_ready = sem("x_ready")
        sq_done = sem("sq_done")
        stat_done = sem("stat_done")
        diag_ready = sem("diag_ready")
        rms_done = sem("rms_done")
        xn_ready = sem("xn_ready")
        act_hi_ready = sem("act_hi_ready")
        act_lo_ready = sem("act_lo_ready")
        par_done = sem("par_done")
        perm_done = sem("perm_done")
        rope_ready = sem("rope_ready")
        tri_ready = sem("tri_ready")
        wst_done = sem("wst_done")
        vn_ready = sem("vn_ready")
        f_done = sem("f_done")
        yc_ready = sem("yc_ready")
        pooled_ready = sem("pooled_ready")
        pool_done = sem("pool_done")
        conv_tap = sem("conv_tap")
        ct1_done = sem("ct1_done")
        ct2_done = sem("ct2_done")
        cg_ready = sem("cg_ready")
        yd_ready = sem("yd_ready")
        s_done = sem("s_done")
        nmx_ready = sem("nmx_ready")
        exp_done = sem("exp_done")
        probs_ready = sem("probs_ready")
        pt_done = sem("pt_done")
        pv_done = sem("pv_done")
        yhi_ready = sem("yhi_ready")
        ylo_ready = sem("ylo_ready")
        proj_b_done = sem("proj_b_done")
        merged_ready = sem("merged_ready")
        madd_done = sem("madd_done")
        ffhi_ready = sem("ffhi_ready")
        fflo_ready = sem("fflo_ready")
        y_done = sem("y_done")
        mats_seen = sem("mats_seen")
        rows_in = sem("rows_in")
        mats_in = sem("mats_in")
        params_free = sem("params_free")
        dve_chain = sem("dve_chain")
        pool_chain = sem("pool_chain")
        x_in = sem("x_in")
        pos_in = sem("pos_in")
        icnt_in = sem("icnt_in")
        gfin_in = sem("gfin_in")
        pre_const = sem("pre_const")
        pre_dve = sem("pre_dve")
        pre_act = sem("pre_act")
        pre_pe = sem("pre_pe")
        out_done = sem("out_done")

        def free_at(l, b, idx):
            return l * BANK_USES[b] + (idx + 1)

        def high_use(b, what):
            return HIGH_USES[b].index(what)

        def unit_use(u):
            return u // 4

        def proj_use(b, which):
            return len(LOW_MIX[b]) + PROJ_ORDER.index(which)

        mixed = [len(LOW_MIX[b]) + 4 for b in range(4)]

        def kview(t):
            return t[:, :].rearrange("p (k n) -> p k n", n=UC)

        def wide(t):
            return t[:, :].rearrange("p (k n) -> p k n", n=D)

        def low(b):
            return bank[b][:, :].rearrange("p (f s) -> p f s", f=2)

        x_nat = gates[:, 0:8, :].rearrange("p k s -> p (k s)").rearrange("p (t d) -> p t d", t=TT)
        g_fin = gates[:, 8:12, :].rearrange("p k s -> p (k s)")
        o_nat = gates[:, 16:24, :].rearrange("p k s -> p (k s)").rearrange("p (t d) -> p t d", t=TT)
        junk = gates[:, 24:32, :].rearrange("p k s -> p (k s)").rearrange("p (h n) -> p h n", h=4)

        block = ctx.enter_context(nc.Block())

        @block.sync
        def _(sp):
            sp.dma_start(x_nat, T["x"][0].rearrange("(t p) d -> p t d", p=P)).then_inc(x_in, 16)

            def load(l, slot, use, src, n=UC):
                sp.wait_ge(lo_ready[slot], l * USES + use + 1)
                sp.sem_inc(raw_claimed, 1)
                sp.dma_start(raw[slot][:, :].rearrange("p (k n) -> p k n", n=n), src)\
                    .then_inc(raw_full[slot], 16)

            def cols(w, l, c0):
                return w[l].rearrange("(k p) n -> p k n", p=P)[:, :, c0:c0 + UC]

            def down(l, r0):
                return T["w_ffn_out"][l].rearrange("(j k p) n -> j p k n", p=P, k=2)[r0]

            def ffn_load(l, kind, j, slot, use):
                if kind == "G":
                    load(l, slot, use, T["w_ffn_in"][l].rearrange("(k p) (h j n) -> h j p k n", p=P, h=2, n=UC)[0, j])
                elif kind == "U":
                    load(l, slot, use, T["w_ffn_in"][l].rearrange("(k p) (h j n) -> h j p k n", p=P, h=2, n=UC)[1, j])
                else:
                    load(l, slot, use, down(l, j), n=D)

            with sp.Fori(0, L) as l:
                for u in range(U_FFN):
                    slot, use = u % RING, u // RING
                    if u < U_GATE:
                        load(l, slot, use, cols(T["w_in"], l, W_IN_UNITS[u][1]))
                    elif u < U_PROJ_A:
                        g, dp = divmod(u - U_GATE, 4)
                        load(l, slot, use, cols(T["w_gate"], l, GATE_BRANCH[g] * D + dp * UC))
                    elif u < U_PROJ_B:
                        w = T["w_proj_" + "acd"[u - U_PROJ_A]]
                        load(l, slot, use, w[l].rearrange("(k p) n -> p k n", p=P), n=D)
                    elif u < U_WO:
                        r0 = (u - U_PROJ_B) * 2 * P
                        load(l, slot, use, T["w_proj_b"][l].rearrange("(j k p) n -> j p k n", p=P, k=2)[u - U_PROJ_B], n=D)
                    else:
                        load(l, slot, use, cols(T["w_o"], l, (u - U_WO) * UC))
                ffn_load(l, "G", 0, U_FFN % RING, U_FFN // RING)
                ffn_load(l, "U", 0, (U_FFN + 1) % RING, (U_FFN + 1) // RING)
                with sp.Fori(0, FF_ITERS) as it:
                    for c in range(6):
                        ffn_load(l, "GUO"[c % 3], it * 2 + c // 3 + (c % 3 != 2),
                                 (U_LOOP + c) % RING, it * 2 + (U_LOOP + c) // RING)
                for u in range(U_TAIL, UNITS):
                    c = u - U_TAIL
                    kind = "GUO"[c % 3] if u < UNITS - 1 else "O"
                    j = J_TAIL + c // 3 - (kind == "O") if u < UNITS - 1 else FF_STEPS - 1
                    ffn_load(l, kind, j, u % RING, u // RING)

            sp.wait_ge(x_ready, 8 * L)
            sp.dma_start(g_fin, T["final_norm_g"].partition_broadcast(P)).then_inc(gfin_in, 16)
            for t in range(TT):
                sp.wait_ge(pre_dve, PRE_DVE_OUT + t + 1)
                sp.dma_start(out[0].rearrange("(t p) d -> t p d", p=P)[t], o_nat[:, t, :])\
                    .then_inc(out_done, 16)
            sp.wait_ge(out_done, 16 * TT)

        @block.gpsimd
        def _(pool):
            pool.dma_start(ifreq[:, :], inv_freq).then_inc(pos_in, 16)
            pool.dma_start(xn[:, 0, 0, :].bitcast(I32), T["positions"].to_broadcast([P, S]))\
                .then_inc(pos_in, 16)
            nc.gpsimd.memset(ident[:, :], 0.0).then_inc(pre_const, 1)
            pool.wait_ge(pre_const, 1)
            nc.gpsimd.affine_select(out=ident[:, :], in_=ident[:, :], compare_op=ALU.not_equal, fill=1.0,
                                    base=0, pattern=[[-1, P]], channel_multiplier=1).then_inc(pre_const, 1)
            nc.gpsimd.memset(ones[:, :], 1.0).then_inc(pre_const, 1)
            nc.gpsimd.memset(rot_perm[:, :], 0.0)
            nc.gpsimd.memset(causal[:, :], 0.0)
            nc.gpsimd.memset(zeros[:, :], 0.0)
            nc.gpsimd.memset(conv_h[:, :, :], 0.0)
            nc.gpsimd.memset(pool_w[:, :, :], 0.0)
            nc.gpsimd.memset(xa[:, :, 0:PAD], 0.0).then_inc(pre_const, 1)
            pool.wait_ge(pre_const, 4)
            for m0 in range(0, P, 32):
                first = m0 % HEAD_DIM == 0
                src0 = m0 + 32 if first else m0 - 32
                blk = rot_perm[:, m0:m0 + 32]
                nc.gpsimd.affine_select(out=blk, in_=blk, compare_op=ALU.not_equal, fill=-1.0 if first else 1.0,
                                        base=-src0, pattern=[[-1, 32]], channel_multiplier=1)
            for c0 in (0, 2 * P):
                blk = causal[:, c0:c0 + P]
                last = nc.gpsimd.affine_select(out=blk, in_=blk, compare_op=ALU.is_ge, fill=NEG,
                                               base=0, pattern=[[-1, P]], channel_multiplier=1)
            last.then_inc(pre_const, 1)
            pool.sem_inc(madd_done, 1)
            pool.dma_start(icnt[:, :, :], inv_count).then_inc(icnt_in, 16)

            n = [0]

            def link(l, ins):
                n[0] += 1
                ins.then_inc(pool_chain, 1)
                pool.wait_ge(pool_chain, l * POOL_CHAIN_PER_LAYER + n[0])

            with pool.Fori(0, L) as l:
                pool.wait_ge(params_free, l + 1)
                for name, (r0, k) in ROWS.items():
                    src = T[name][l]
                    if name == "conv_w":
                        src = src.rearrange("w (c p) -> (w c) p", p=P)
                    else:
                        src = src.rearrange("(r p) -> r p", p=P)
                    pool.dma_start(rows[r0:r0 + k, :], src).then_inc(rows_in, 16)
                pool.dma_start(ws_nat[:, :, :], T["sgu_w"][l].rearrange("g t s -> t g s")).then_inc(mats_in, 16)
                pool.dma_start(ln_g[:, :], T["sgu_norm_g"][l].partition_broadcast(P)).then_inc(mats_in, 16)
                pool.dma_start(ln_b[:, :], T["sgu_norm_b"][l].partition_broadcast(P)).then_inc(mats_in, 16)
                for g in range(4):
                    half = slice(64 * (g % 2), 64 * (g % 2) + 64)
                    pool.dma_start(sgu_bias[half, g // 2, :], T["sgu_b"][l, g].partition_broadcast(64))\
                        .then_inc(mats_in, 16)
                    pool.dma_start(pool_w[half, g // 2, half], T["pool_w"][l, g]).then_inc(mats_in, 16)
                pool.wait_ge(mats_in, l * (16 * 11) + 16 * 11)
                pool.sem_inc(mats_seen, 1)
                nc.gpsimd.affine_select(out=ws_nat[:, :, :], in_=ws_nat[:, :, :], compare_op=ALU.is_ge, fill=0.0,
                                        base=0, pattern=[[0, 4], [-1, P]], channel_multiplier=1).then_inc(tri_ready, 1)
                pool.wait_ge(bank_free[2], free_at(l, 2, unit_use(10) + 1))
                pool.wait_ge(icnt_in, 16)
                link(l, nc.gpsimd.tensor_tensor(s2[:, :, 1:E], xa[:, :, 1:E], xa[:, :, 0:E - 1], ALU.add))
                link(l, nc.gpsimd.tensor_tensor(s4[:, :, 4:E], s2[:, :, 4:E], s2[:, :, 2:E - 2], ALU.add))
                link(l, nc.gpsimd.tensor_tensor(s8[:, 8:E], s4[:, 1, 8:E], s4[:, 1, 4:E - 4], ALU.add))
                link(l, nc.gpsimd.tensor_tensor(s16[:, 16:E], s8[:, 16:E], s8[:, 8:E - 8], ALU.add))
                for g, total in enumerate((s2[:, 0], s4[:, 0], s8, s16)):
                    half = slice(64 * (g % 2), 64 * (g % 2) + 64)
                    link(l, nc.gpsimd.tensor_tensor(pooled[half, g // 2, :], total[half, PAD:E],
                                                    icnt[half, g // 2, :], ALU.mult))
                nc.gpsimd.tensor_tensor(pooled[:, :, :], pooled[:, :, :], xa[:, :, PAD:E], ALU.subtract)\
                    .then_inc(pooled_ready, 1)
                for i in range(8):
                    dp = i % 4
                    pool.wait_ge(bank_free[dp], free_at(l, dp, proj_use(dp, "CD"[i // 4]) + 1))
                    m = gates[:, 2 * dp:2 * dp + 2, :].rearrange("p f s -> p (f s)")
                    nc.gpsimd.tensor_tensor(m, m, mtmp[:, i % 2, :], ALU.add).then_inc(madd_done, 1)
            assert n[0] == POOL_CHAIN_PER_LAYER

        @block.scalar
        def _(act):
            for s in range(RING):
                act.sem_inc(w_used[s], 1)
            for b in range(8):
                act.sem_inc(bank_free[b], 1)

            def copy(o, i):
                return nc.scalar.activation(o, i, ACT.Copy)

            def split(l, slot, use):
                act.wait_ge(raw_full[slot], (l * USES + use + 1) * 16)
                act.wait_ge(w_used[slot], l * USES + use + 1)
                copy(w_hi[slot][:, :], raw[slot][:, :]).then_inc(hi_ready[slot], 1)

            def squares(l, n):
                for i in range(4):
                    act.wait_ge(x_ready, l * 8 + (4 * n + i + 1))
                    nc.scalar.activation(sq[:, 2 * i:2 * i + 2, :], x_res[:, 2 * i:2 * i + 2, :], ACT.Square)\
                        .then_inc(sq_done, 1)

            def split_acts(l, n, i):
                act.wait_ge(xn_ready, l * 8 + (4 * n + i + 1))
                copy(act_hi[:, 2 * i:2 * i + 2, :], xn[:, i % 2, :, :]).then_inc(act_hi_ready, 1)

            def unit_done(l, u):
                act.wait_ge(w_used[u % RING], l * USES + (u // RING + 2))

            def evac(l, u):
                b = u % 4
                if u < 4:
                    unit_done(l, u)
                    copy(qk[:, 2 * u:2 * u + 2, :], low(b)).then_inc(bank_free[b], 1)
                elif u < 6:
                    unit_done(l, u)
                    copy(v_sb[:, :, (u - 4) * UC:(u - 3) * UC], low(b)).then_inc(bank_free[b], 1)
                elif u == 6:
                    act.wait_ge(rope_ready, l * 4 + 4)
                    unit_done(l, u)
                    nc.scalar.activation(glu_t[:, :, :], low(b), ACT.Tanh, scale=0.5).then_inc(bank_free[b], 1)
                elif u == 8:
                    unit_done(l, u)
                    nc.scalar.activation(zv[:, :, :], low(b), ACT.Gelu_apprx_tanh).then_inc(bank_free[b], 1)
                elif u == 9:
                    unit_done(l, u)
                    nc.scalar.activation(zu[:, :, :], low(b), ACT.Gelu_apprx_tanh).then_inc(bank_free[b], 1)
                elif u == 10:
                    unit_done(l, u)
                    copy(xa[:, :, PAD:PAD + S], low(b)).then_inc(bank_free[b], 1)
                elif U_GATE <= u < U_PROJ_A:
                    g, dp = divmod(u - U_GATE, 4)
                    unit_done(l, u)
                    for f in range(2):
                        k = GATE_BRANCH[g] * KT + 2 * dp + f
                        last = nc.scalar.activation(gates[:, k, :], low(b)[:, f, :], ACT.Tanh, scale=0.5,
                                                    bias=half_bg[:, k:k + 1])
                    last.then_inc(bank_free[b], 1)

            def misc(l, u):
                if u == 6:
                    act.wait_ge(wst_done, l + 1)
                    copy(wsT[:, :, :], bank[6][:, :].rearrange("p (g s) -> p g s", g=4)).then_inc(bank_free[6], 1)
                if u in (10, 14, 18, 22):
                    hp = (u - 10) // 4
                    act.wait_ge(nmx_ready, l * HP + hp + 1)
                    for i in range(2):
                        for q, (a, b) in enumerate(((0, P), (P, 3 * P))):
                            c = 2 * q + i
                            last = nc.scalar.activation(probs[:, i, a:b], scores[:, i, a:b], ACT.Exp, scale=SCALE,
                                                        bias=nmx[:, c:c + 1], accum_out=den[:, c:c + 1])
                    last.then_inc(exp_done, 1)
                if u in (12, 16, 20, 24):
                    hp = (u - 12) // 4
                    for i in range(2):
                        act.wait_ge(pt_done, l * 2 * HP + 2 * hp + i + 1)
                        copy(probsT[:, i, :], bank[6 + i][:, 0:3 * P]).then_inc(bank_free[6 + i], 1)
                if u in (13, 17, 21, 25):
                    hp = (u - 13) // 4
                    act.wait_ge(pv_done, l * HP + hp + 1)
                    copy(y_hi[:, 2 + hp, :], bank[4][:, 0:S]).then_inc(yhi_ready, 1)
                if u == 14:
                    act.wait_ge(yc_ready, l + 1)
                    copy(y_hi[:, 6:8, :], yc_f).then_inc(yhi_ready, 1)
                if u == 16:
                    act.wait_ge(pool_done, l + 1)
                    for f in range(2):
                        c = ROWS["pool_scale"][0] + f
                        last = nc.scalar.activation(ya_f[:, f, :], bank[5][:, f * S:(f + 1) * S], ACT.Copy,
                                                    scale=par[:, c:c + 1])
                    last.then_inc(bank_free[5], 1)
                    act.wait_ge(bank_free[5], free_at(l, 5, high_use(5, "pool") + 1))
                    copy(y_hi[:, 0:2, :], ya_f).then_inc(yhi_ready, 1)
                if u == 24:
                    act.wait_ge(ct2_done, l + 1)
                    for f in range(2):
                        cg, cb = ROWS["conv_norm_g"][0] + f, ROWS["conv_norm_b"][0] + f
                        last = nc.scalar.activation(yd_f[:, f, :], bank[5][:, f * S:(f + 1) * S], ACT.Identity,
                                                    scale=par[:, cg:cg + 1], bias=par[:, cb:cb + 1])
                    last.then_inc(bank_free[5], 1)
                    act.wait_ge(bank_free[5], free_at(l, 5, high_use(5, "cT2") + 1))
                    nc.scalar.activation(glu_t[:, :, :], yd_f[:, :, :], ACT.Tanh, scale=0.5).then_inc(cg_ready, 1)
                if u == 26:
                    act.wait_ge(yd_ready, l + 1)
                    copy(y_hi[:, 8:10, :], yd_f[:, :, :]).then_inc(yhi_ready, 1)
                if u == U_WO - 1:
                    for i in range(4):
                        act.wait_ge(merged_ready, l * 4 + i + 1)
                        copy(act_hi[:, 2 * i:2 * i + 2, :], gates[:, 2 * i:2 * i + 2, :]).then_inc(act_hi_ready, 1)

            def ffn_gate(l, slot, use, even, it):
                act.wait_ge(w_used[slot], l * USES + (use + 2))
                if it is not None:
                    b = 3 if even else 1
                    act.wait_ge(bank_free[b], l * BANK_USES[b] + (it + (mixed[b] + 2)))
                b = 0 if even else 2
                nc.scalar.activation(ff_g[:, 0 if even else 1, :], bank[b][:, :], ACT.Silu).then_inc(bank_free[b], 1)

            def ffn_hi(l, even, it):
                b = 1 if even else 3
                act.wait_ge(bank_free[b], l * BANK_USES[b] + (it + (mixed[b] + (2 if not even else 3))))
                copy(ff_hi[:, 0 if even else 1, :, :].rearrange("p f s -> p (f s)"), ff_a).then_inc(ffhi_ready, 1)

            act.wait_ge(pre_dve, PRE_DVE_ROPE)
            nc.scalar.activation(sin_t[:, 0, :], xn[:, 1, 0, :], ACT.Sin)
            nc.scalar.activation(cos_t[:, 0, :], xn[:, 1, 1, :], ACT.Sin).then_inc(pre_act, 1)

            with act.Fori(0, L) as l:
                split(l, 0, 0)
                squares(l, 0)
                split(l, 1, 0)
                act.wait_ge(par_done, l + 1)
                copy(par[:, :], bank[6][:, 0:N_ROWS])
                r0, k = ROWS["b_gate"]
                nc.scalar.activation(half_bg[:, :], bank[6][:, r0:r0 + k], ACT.Copy, scale=0.5)\
                    .then_inc(bank_free[6], 1)
                act.wait_ge(bank_free[6], free_at(l, 6, high_use(6, "par") + 1))
                split_acts(l, 0, 0)
                split_acts(l, 0, 1)
                split_acts(l, 0, 2)
                split_acts(l, 0, 3)
                for u in range(U_FFN):
                    split(l, (u + 2) % RING, (u + 2) // RING)
                    evac(l, u)
                    misc(l, u)
                squares(l, 1)
                for i in range(4):
                    split_acts(l, 1, i)
                split(l, (U_FFN + 2) % RING, (U_FFN + 2) // RING)
                ffn_gate(l, U_FFN % RING, U_FFN // RING, True, None)
                split(l, (U_FFN + 3) % RING, (U_FFN + 3) // RING)
                ffn_hi(l, True, -1)

                def ffn_unit(l, base_u, use0, it, c):
                    ahead = c + 2
                    split(l, (base_u + ahead) % RING, use0 + ((base_u + ahead) // RING - base_u // RING))
                    if c % 3 == 0:
                        ffn_gate(l, base_u % RING, use0 + c // 3, c == 3, it)
                    elif c % 3 == 1:
                        ffn_hi(l, c == 4, it)

                with act.Fori(0, FF_ITERS) as it:
                    for c in range(6):
                        ffn_unit(l, U_LOOP, it * 2 + U_LOOP // RING, it, c)
                for c in range(5):
                    ffn_unit(l, U_TAIL, U_TAIL // RING, FF_ITERS, c)

            for h in range(4):
                act.wait_ge(pre_pe, 5 + h)
                nc.scalar.activation(junk[:, h, :], bank[h][:, :], ACT.Square, accum_out=ssq[:, h:h + 1]).then_inc(pre_act, 1)

        @block.tensor
        def _(pe):
            def mm3(o, whi, wlo, ahi, alo, first, last, skip=False):
                nc.tensor.matmul(o, whi, ahi, start=first, stop=False, skip_group_check=skip)
                nc.tensor.matmul(o, whi, alo, start=False, stop=False, skip_group_check=skip)
                return nc.tensor.matmul(o, wlo, ahi, start=False, stop=last, skip_group_check=skip)

            def weights(l, slot, use):
                pe.wait_ge(lo_ready[slot], l * USES + use + 2)

            def bank_wait(l, b, idx):
                pe.wait_ge(bank_free[b], free_at(l, b, idx))

            def unit(l, slot, b, wait_k=None):
                hi, lo = kview(w_hi[slot]), kview(w_lo[slot])
                for f in range(2):
                    fs = slice(f * P, f * P + P)
                    for k in range(KT):
                        if wait_k is not None and f == 0 and k % 2 == 0:
                            pe.wait_ge(act_lo_ready, wait_k + (k // 2 + 1))
                        last = mm3(low(b)[:, f, :], hi[:, k, fs], lo[:, k, fs], act_hi[:, k, :], act_lo[:, k, :],
                                   k == 0, k == KT - 1)
                last.then_inc(w_used[slot], 1)

            def unit_natural(slot, b):
                hi, lo = kview(w_hi[slot]), kview(w_lo[slot])
                for t in range(TT):
                    ts = slice(t * P, t * P + P)
                    for k in range(KT):
                        o = low(b)[:, t, :]
                        nc.tensor.matmul(o, act_hi[:, k, ts], hi[:, k, :], start=(k == 0), stop=False)
                        nc.tensor.matmul(o, act_hi[:, k, ts], lo[:, k, :], start=False, stop=False)
                        last = nc.tensor.matmul(o, act_lo[:, k, ts], hi[:, k, :], start=False, stop=(k == KT - 1))
                last.then_inc(w_used[slot], 1)

            def unit_rows(slot, b0, hi_in, lo_in, first, last_k, done=None, start_banks=True):
                hi, lo = wide(w_hi[slot]), wide(w_lo[slot])
                for dp in range(4):
                    for f in range(2):
                        fs = slice((2 * dp + f) * P, (2 * dp + f + 1) * P)
                        for k in range(2):
                            last = mm3(low(b0 + dp)[:, f, :], hi[:, k, fs], lo[:, k, fs], hi_in[k], lo_in[k],
                                       first and start_banks and f == 0 and k == 0, last_k and k == 1, skip=True)
                    if done is not None and dp < 3:
                        last.then_inc(done, 1)
                last.then_inc(w_used[slot], 1)

            def norm(l, n, tag):
                bank_wait(l, 7, high_use(7, "stat" + tag))
                for t in range(TT):
                    for k in range(KT):
                        if t == 0 and k % 2 == 0:
                            pe.wait_ge(sq_done, l * 8 + (4 * n + k // 2 + 1))
                        last = nc.tensor.matmul(bank[7][:, t:t + 1], sq[:, k, t * P:t * P + P], ones[:, 0:1],
                                                start=(k == 0), stop=(k == KT - 1))
                last.then_inc(stat_done, 1)
                pe.wait_ge(diag_ready, l * 2 + n + 1)
                pe.wait_ge(bank_free[7], free_at(l, 7, high_use(7, "stat" + tag) + 1))
                for t in range(TT):
                    last = nc.tensor.matmul(bank[7][:, t * P:t * P + P], ones[:, :], diag[:, t, :], start=True, stop=True)
                last.then_inc(rms_done, 1)

            def misc(l, u):
                if 1 <= u <= 4:
                    i = u - 1
                    bank_wait(l, 4 + i, high_use(4 + i, f"perm{i}"))
                    if i == 3:
                        pe.wait_ge(xn_ready, l * 8 + 4)
                    pe.wait_ge(bank_free[i], free_at(l, i, 1))
                    nc.tensor.matmul(bank[4 + i][:, :], rot_perm[:, :],
                                     qk[:, 2 * i:2 * i + 2, :].rearrange("p f s -> p (f s)"),
                                     start=True, stop=True).then_inc(perm_done, 1)
                if u == 6:
                    bank_wait(l, 6, high_use(6, "wsT"))
                    pe.wait_ge(tri_ready, l + 1)
                    for g in range(4):
                        last = nc.tensor.transpose(bank[6][:, g * P:(g + 1) * P], ws_nat[:, g, :], ident[:, :])
                    last.then_inc(wst_done, 1)
                if u in (10, 14, 18, 22):
                    hp = (u - 10) // 4
                    if hp == 0:
                        pe.wait_ge(rope_ready, l * 4 + 4)
                    for i in range(2):
                        bank_wait(l, 4 + i, high_use(4 + i, f"S{hp}"))
                        h = slice(64 * i, 64 * i + 64)
                        nc.tensor.matmul(bank[4 + i][:, 0:P], qk[h, hp, 0:P], qk[h, 4 + hp, 0:P], start=True, stop=True)
                        nc.tensor.matmul(bank[4 + i][:, P:3 * P], qk[h, hp, P:2 * P], qk[h, 4 + hp, :],
                                         start=True, stop=True).then_inc(s_done, 1)
                if u in (12, 16, 20, 24):
                    hp = (u - 12) // 4
                    pe.wait_ge(probs_ready, l * HP + hp + 1)
                    for i in range(2):
                        bank_wait(l, 6 + i, high_use(6 + i, f"PT{hp}"))
                        for c in range(3):
                            last = nc.tensor.transpose(bank[6 + i][:, c * P:(c + 1) * P], probs[:, i, c * P:(c + 1) * P],
                                                       ident[:, :])
                        last.then_inc(pt_done, 1)
                if u in (13, 17, 21, 25):
                    hp = (u - 13) // 4
                    bank_wait(l, 4, high_use(4, f"PV{hp}"))
                    for i in range(2):
                        pe.wait_ge(bank_free[6 + i], free_at(l, 6 + i, high_use(6 + i, f"PT{hp}") + 1))
                        o = bank[4][64 * i:64 * i + 64, :]
                        c0 = (2 * hp + i) * HEAD_DIM
                        nc.tensor.matmul(o[:, 0:S], v_sb[:, 0, c0:c0 + HEAD_DIM], probsT[:, i, 0:2 * P],
                                         start=True, stop=False, skip_group_check=True)
                        last = nc.tensor.matmul(o[:, P:S], v_sb[:, 1, c0:c0 + HEAD_DIM], probsT[:, i, 2 * P:3 * P],
                                                start=False, stop=True, skip_group_check=True)
                    last.then_inc(pv_done, 1)
                if u == 13:
                    bank_wait(l, 5, high_use(5, "F"))
                    pe.wait_ge(vn_ready, l + 1)
                    pe.wait_ge(bank_free[6], free_at(l, 6, high_use(6, "wsT") + 1))
                    for g in range(4):
                        for t in range(TT):
                            c0 = (g // 2) * S + t * P
                            last = nc.tensor.matmul(bank[5][64 * (g % 2):64 * (g % 2) + 64, c0:c0 + P],
                                                    zv[:, t, g * 64:(g + 1) * 64], wsT[:, g, :], start=True, stop=True)
                    last.then_inc(f_done, 1)
                if u == 16:
                    bank_wait(l, 5, high_use(5, "pool"))
                    pe.wait_ge(pooled_ready, l + 1)
                    for f in range(2):
                        last = nc.tensor.matmul(bank[5][:, f * S:(f + 1) * S], pool_w[:, f, :], pooled[:, f, :],
                                                start=True, stop=True)
                    last.then_inc(pool_done, 1)
                if u == 20:
                    bank_wait(l, 5, high_use(5, "cT1"))
                    pe.wait_ge(conv_tap, l * (2 * CW) + 2 * CW)
                    for t in range(TT):
                        for f in range(2):
                            last = nc.tensor.transpose(bank[5][:, t * 256 + f * P:t * 256 + (f + 1) * P],
                                                       conv_a[:, f, t * P:(t + 1) * P], ident[:, :])
                    last.then_inc(ct1_done, 1)
                if u == 24:
                    bank_wait(l, 5, high_use(5, "cT2"))
                    pe.wait_ge(bank_free[5], free_at(l, 5, high_use(5, "cT1") + 1))
                    for t in range(TT):
                        for f in range(2):
                            last = nc.tensor.transpose(bank[5][:, f * S + t * P:f * S + (t + 1) * P],
                                                       conv_n[:, t, f * P:(f + 1) * P], ident[:, :])
                    last.then_inc(ct2_done, 1)

            def ffn_in(l, slot, use, b, idx, wait_k=None):
                weights(l, slot, use)
                pe.wait_ge(bank_free[b], l * BANK_USES[b] + idx + 1)
                unit(l, slot, b, wait_k)

            def ffn_out(l, slot, use, even, n, last_k=False):
                weights(l, slot, use)
                pe.wait_ge(fflo_ready, n + 1)
                e = 0 if even else 1
                unit_rows(slot, 4, [ff_hi[:, e, k, :] for k in range(2)], [ff_lo[:, e, k, :] for k in range(2)],
                          False, last_k)

            pe.wait_ge(pre_const, 3)
            pe.wait_ge(x_in, 16)
            for i in range(4):
                for f in range(2):
                    for t in range(TT):
                        k = 2 * i + f
                        last = nc.tensor.transpose(low(i)[:, f, t * P:(t + 1) * P], x_nat[:, t, k * P:(k + 1) * P],
                                                   ident[:, :])
                last.then_inc(pre_pe, 1)

            with pe.Fori(0, L) as l:
                pe.wait_ge(rows_in, l * (16 * len(ROWS)) + 16 * len(ROWS))
                pe.wait_ge(x_ready, l * 8 + 4)
                bank_wait(l, 6, high_use(6, "par"))
                nc.tensor.transpose(bank[6][:, 0:N_ROWS], rows[:, :], ident[0:N_ROWS, 0:N_ROWS]).then_inc(par_done, 1)
                norm(l, 0, "1")
                for u in range(U_PROJ_A):
                    weights(l, u % RING, u // RING)
                    bank_wait(l, u % 4, unit_use(u))
                    if W_IN_UNITS[min(u, N_IN - 1)][0] in ("v", "sgu_v") and u < N_IN:
                        unit_natural(u % RING, u % 4)
                    else:
                        unit(l, u % RING, u % 4, l * 12 if u == 0 else None)
                    misc(l, u)
                for u, which, k0 in ((U_PROJ_A, "A", 0), (U_PROJ_C, "C", 6), (U_PROJ_D, "D", 8),
                                     (U_PROJ_B, "B", 2), (U_PROJ_B + 1, "", 4)):
                    weights(l, u % RING, u // RING)
                    if which:
                        pe.wait_ge(ylo_ready, l + 1)
                        for b in range(4):
                            bank_wait(l, b, proj_use(b, which))
                    unit_rows(u % RING, 0, [y_hi[:, k0 + k, :] for k in range(2)], [y_lo[:, k0 + k, :] for k in range(2)],
                              bool(which), which != "B", done=proj_b_done if not which else None)
                for i in range(4):
                    u = U_WO + i
                    weights(l, u % RING, u // RING)
                    bank_wait(l, i, proj_use(i, "B") + 1)
                    unit(l, u % RING, i, l * 12 + 4 if i == 0 else None)
                norm(l, 1, "2")
                pe.wait_ge(xn_ready, l * 8 + 8)
                for b in range(4, 8):
                    bank_wait(l, b, len(HIGH_USES[b]))
                    nc.tensor.matmul(bank[b][:, :], zeros[:, 0:P], zeros[:, :], start=True, stop=False,
                                     skip_group_check=True)
                pe.wait_ge(x_ready, l * 8 + 8)
                ffn_in(l, U_FFN % RING, U_FFN // RING, 0, mixed[0], l * 12 + 8)
                ffn_in(l, (U_FFN + 1) % RING, (U_FFN + 1) // RING, 1, mixed[1])
                with pe.Fori(0, FF_ITERS) as it:
                    for h in range(2):
                        b = 0 if h else 2
                        c = U_LOOP + 3 * h
                        ffn_in(l, c % RING, it * 2 + c // RING, b, it + (mixed[b] + h))
                        ffn_in(l, (c + 1) % RING, it * 2 + (c + 1) // RING, b + 1, it + (mixed[b + 1] + h))
                        ffn_out(l, (c + 2) % RING, it * 2 + (c + 2) // RING, h == 0, l * FF_STEPS + (it * 2 + h))
                for h in range(2):
                    b = 0 if h else 2
                    c = U_TAIL + 3 * h
                    ffn_in(l, c % RING, c // RING, b, FF_ITERS + mixed[b] + h)
                    ffn_in(l, (c + 1) % RING, (c + 1) // RING, b + 1, FF_ITERS + mixed[b + 1] + h)
                    ffn_out(l, (c + 2) % RING, (c + 2) // RING, h == 0, l * FF_STEPS + (J_TAIL + h - 1))
                u = UNITS - 1
                ffn_out(l, u % RING, u // RING, True, l * FF_STEPS + (FF_STEPS - 1), last_k=True)

            pe.wait_ge(x_ready, 8 * L + 4)
            for h in range(4):
                for c in range(4):
                    k = 4 * (h % 2) + c
                    last = nc.tensor.transpose(bank[h][:, c * P:(c + 1) * P], x_res[:, k, (h // 2) * P:(h // 2 + 1) * P],
                                               ident[:, :])
                last.then_inc(pre_pe, 1)

        @block.vector
        def _(dve):
            for s in range(RING):
                dve.sem_inc(lo_ready[s], 1)
            dve.sem_inc(params_free, 1)
            V = nc.vector
            n = [0]
            pre = [0]

            def link(l, ins):
                if l is None:
                    pre[0] += 1
                    ins.then_inc(pre_dve, 1)
                    dve.wait_ge(pre_dve, pre[0])
                else:
                    n[0] += 1
                    ins.then_inc(dve_chain, 1)
                    dve.wait_ge(dve_chain, l * DVE_CHAIN_PER_LAYER + n[0])

            def rsqrt(l, o, v, tmp, bits):
                link(l, V.tensor_scalar(bits, v.bitcast(I32), 1, None, ALU.logical_shift_right))
                link(l, V.tensor_scalar(v, v, -0.5, None, ALU.mult))
                link(l, V.tensor_scalar(o.bitcast(I32), bits, -1.0, float(0x5F3759DF), ALU.mult, ALU.add))
                for _ in range(3):
                    link(l, V.tensor_tensor(tmp, o, o, ALU.mult))
                    link(l, V.tensor_tensor(tmp, tmp, v, ALU.mult))
                    link(l, V.scalar_tensor_tensor(o, tmp, 1.5, o, ALU.add, ALU.mult))

            def split(l, slot, use):
                dve.wait_ge(hi_ready[slot], l * USES + use + 1)
                V.tensor_tensor(w_lo[slot][:, :], raw[slot][:, :], w_hi[slot][:, :].bitcast(F32), ALU.subtract)\
                    .then_inc(lo_ready[slot], 1)

            def norm_scale(l, k):
                dve.wait_ge(stat_done, l * 2 + k + 1)
                ins = V.tensor_scalar(st[:, 0:2], bank[7][:, 0:2], 1.0 / D, EPS, ALU.mult, ALU.add)
                ins.then_inc(bank_free[7], 1)
                tag = high_use(7, "stat1" if k == 0 else "stat2")
                dve.wait_ge(bank_free[7], free_at(l, 7, tag + 1))
                rsqrt(l, st[:, 2:4], st[:, 0:2], st[:, 4:6], ist[:, 0:2])
                for t in range(TT):
                    last = V.tensor_scalar(diag[:, t, :], ident[:, :], st[:, 2 + t:3 + t], None, ALU.mult)
                last.then_inc(diag_ready, 1)

            def norm_apply(l, k, i):
                if i == 0:
                    dve.wait_ge(rms_done, l * 2 + k + 1)
                    dve.wait_ge(bank_free[6], free_at(l, 6, high_use(6, "par") + 1))
                if i >= 2:
                    dve.wait_ge(act_lo_ready, l * 12 + (8 * k + i - 1))
                g0 = ROWS["norm_mix_g" if k == 0 else "norm_ffn_g"][0]
                for f in range(2):
                    last = V.scalar_tensor_tensor(xn[:, i % 2, f, :], x_res[:, 2 * i + f, :],
                                                  par[:, g0 + 2 * i + f:g0 + 2 * i + f + 1], bank[7][:, 0:S],
                                                  ALU.mult, ALU.mult)
                last.then_inc(xn_ready, 1)

            def norm_lo(l, k, i):
                dve.wait_ge(act_hi_ready, l * 12 + (8 * k + i + 1))
                V.tensor_tensor(act_lo[:, 2 * i:2 * i + 2, :], xn[:, i % 2, :, :],
                                act_hi[:, 2 * i:2 * i + 2, :].bitcast(F32), ALU.subtract).then_inc(act_lo_ready, 1)

            def norm_all(l, k):
                norm_apply(l, k, 0)
                for i in range(4):
                    if i < 3:
                        norm_apply(l, k, i + 1)
                    norm_lo(l, k, i)

            def unit_done(l, u):
                dve.wait_ge(w_used[u % RING], l * USES + (u // RING + 2))

            def lo_of(o_lo, src, o_hi, count, l):
                dve.wait_ge(yhi_ready, l * 7 + count)
                return V.tensor_tensor(o_lo, src, o_hi.bitcast(F32), ALU.subtract)

            def conv_taps(l, w0, w1):
                for w in range(w0, w1):
                    for f in range(2):
                        c = ROWS["conv_w"][0] + 2 * w + f
                        src = conv_h[:, f, 32 - (CW - 1) + w:32 - (CW - 1) + w + S]
                        if w == 0:
                            cb = ROWS["conv_b"][0] + f
                            ins = V.tensor_scalar(conv_a[:, f, :], src, par[:, c:c + 1], par[:, cb:cb + 1],
                                                  ALU.mult, ALU.add)
                        else:
                            dve.wait_ge(conv_tap, l * (2 * CW) + (2 * (w - 1) + f + 1))
                            ins = V.scalar_tensor_tensor(conv_a[:, f, :], src, par[:, c:c + 1], conv_a[:, f, :],
                                                         ALU.mult, ALU.add)
                        ins.then_inc(conv_tap, 1)

            def misc(l, u):
                if 1 <= u <= 4:
                    i = u - 1
                    r = rot[:, :, :]
                    src = qk[:, 2 * i:2 * i + 2, :]
                    dst = qk[:, 2 * i:2 * i + 2, :]
                    if i >= 1:
                        dve.wait_ge(rope_ready, l * 4 + i)
                    dve.wait_ge(perm_done, l * 4 + i + 1)
                    V.tensor_tensor(r, bank[4 + i][:, :].rearrange("p (f s) -> p f s", f=2),
                                    sin_t[:, :, :].to_broadcast([P, 2, S]), ALU.mult).then_inc(bank_free[4 + i], 1)
                    link(l, V.tensor_tensor(dst, src, cos_t[:, :, :].to_broadcast([P, 2, S]), ALU.mult))
                    dve.wait_ge(bank_free[4 + i], free_at(l, 4 + i, high_use(4 + i, f"perm{i}") + 1))
                    V.tensor_tensor(dst, dst, r, ALU.add).then_inc(rope_ready, 1)
                if u == 7:
                    dve.wait_ge(bank_free[2], free_at(l, 2, unit_use(6) + 1))
                    link(l, V.tensor_scalar(glu_t[:, :, :], glu_t[:, :, :], 0.5, 0.5, ALU.mult, ALU.add))
                    unit_done(l, 7)
                    V.tensor_tensor(conv_h[:, :, 32:32 + S], glu_t[:, :, :], low(3), ALU.mult)\
                        .then_inc(bank_free[3], 1)
                    dve.wait_ge(bank_free[3], free_at(l, 3, unit_use(7) + 1))
                if u == 9:
                    dve.wait_ge(bank_free[0], free_at(l, 0, unit_use(8) + 1))
                    for t in range(TT):
                        link(l, V.bn_stats(bn6[:, t, :], zv[:, t, :]))
                        V.memset(st[:, 14:15], 0.0)
                        link(l, V.bn_aggr(mv[:, t, :], bn6[:, t, :]))
                    link(l, V.tensor_scalar(st[:, 8:10], mv[:, :, 1], EPS, None, ALU.add))
                    rsqrt(l, st[:, 10:12], st[:, 8:10], st[:, 12:14], ist[:, 2:4])
                    for t in range(TT):
                        link(l, V.tensor_scalar(zv[:, t, :], zv[:, t, :], mv[:, t, 0:1], st[:, 10 + t:11 + t],
                                                ALU.subtract, ALU.mult))
                    dve.wait_ge(mats_seen, l + 1)
                    link(l, V.tensor_tensor(zv[:, :, :], zv[:, :, :],
                                            ln_g[:, :].unsqueeze(1).to_broadcast([P, TT, 256]), ALU.mult))
                    V.tensor_tensor(zv[:, :, :], zv[:, :, :],
                                    ln_b[:, :].unsqueeze(1).to_broadcast([P, TT, 256]), ALU.add).then_inc(vn_ready, 1)
                if 8 <= u <= 18:
                    conv_taps(l, 3 * (u - 8), min(3 * (u - 7), CW))
                if u in (10, 14, 18, 22):
                    hp = (u - 10) // 4
                    for i in range(2):
                        dve.wait_ge(s_done, l * 2 * HP + 2 * hp + i + 1)
                        V.tensor_tensor(scores[:, i, :], bank[4 + i][:, 0:3 * P], causal[:, :], ALU.add)\
                            .then_inc(bank_free[4 + i], 1)
                    for i in range(2):
                        dve.wait_ge(bank_free[4 + i], free_at(l, 4 + i, high_use(4 + i, f"S{hp}") + 1))
                    V.tensor_reduce(mx[:, 0:2], scores[:, :, 0:P], AX.X, ALU.max)
                    link(l, V.tensor_reduce(mx[:, 2:4], scores[:, :, P:3 * P], AX.X, ALU.max))
                    V.tensor_scalar(nmx[:, :], mx[:, :], -SCALE, None, ALU.mult).then_inc(nmx_ready, 1)
                if u in (11, 15, 19, 23):
                    hp = (u - 11) // 4
                    dve.wait_ge(exp_done, l * HP + hp + 1)
                    link(l, V.reciprocal(rden[:, :], den[:, :]))
                    V.tensor_tensor(probs[:, :, 0:P], probs[:, :, 0:P],
                                    rden[:, 0:2].unsqueeze(2).to_broadcast([P, 2, P]), ALU.mult)
                    V.tensor_tensor(probs[:, :, P:3 * P], probs[:, :, P:3 * P],
                                    rden[:, 2:4].unsqueeze(2).to_broadcast([P, 2, 2 * P]), ALU.mult)\
                        .then_inc(probs_ready, 1)
                if u == 13:
                    dve.wait_ge(f_done, l + 1)
                    for f in range(2):
                        last = V.tensor_tensor(yc_f[:, f, :].rearrange("p (t s) -> p t s", t=TT),
                                               bank[5][:, f * S:(f + 1) * S].rearrange("p (t s) -> p t s", t=TT),
                                               sgu_bias[:, f:f + 1, :].to_broadcast([P, TT, P]), ALU.add)
                    last.then_inc(bank_free[5], 1)
                    dve.wait_ge(bank_free[5], free_at(l, 5, high_use(5, "F") + 1))
                    dve.wait_ge(bank_free[1], free_at(l, 1, unit_use(9) + 1))
                    V.tensor_tensor(yc_f, yc_f, zu[:, :, :], ALU.mult).then_inc(yc_ready, 1)
                if u in (13, 17, 21, 25):
                    hp = (u - 13) // 4
                    count = (1, 4, 5, 6)[hp]
                    lo_of(y_lo[:, 2 + hp, :], bank[4][:, 0:S], y_hi[:, 2 + hp, :], count, l).then_inc(bank_free[4], 1)
                if u == 15:
                    lo_of(y_lo[:, 6:8, :], yc_f, y_hi[:, 6:8, :], 2, l)
                if u == 16:
                    lo_of(y_lo[:, 0:2, :], ya_f, y_hi[:, 0:2, :], 3, l).then_inc(params_free, 1)
                if u == 20:
                    dve.wait_ge(ct1_done, l + 1)
                    nat = bank[5][:, :].rearrange("p (t c) -> p t c", t=TT)
                    for t in range(TT):
                        link(l, V.bn_stats(bn6[:, t, :], nat[:, t, :]))
                        V.memset(st[:, 14:15], 0.0)
                        link(l, V.bn_aggr(mv[:, t, :], bn6[:, t, :]))
                    link(l, V.tensor_scalar(st[:, 8:10], mv[:, :, 1], EPS, None, ALU.add))
                    rsqrt(l, st[:, 10:12], st[:, 8:10], st[:, 12:14], ist[:, 2:4])
                    for t in range(TT):
                        last = V.tensor_scalar(conv_n[:, t, :], nat[:, t, :], mv[:, t, 0:1], st[:, 10 + t:11 + t],
                                               ALU.subtract, ALU.mult)
                    last.then_inc(bank_free[5], 1)
                if u == 25:
                    dve.wait_ge(cg_ready, l + 1)
                    link(l, V.tensor_scalar(glu_t[:, :, :], glu_t[:, :, :], 0.5, 0.5, ALU.mult, ALU.add))
                    V.tensor_tensor(yd_f[:, :, :], yd_f[:, :, :], glu_t[:, :, :], ALU.mult).then_inc(yd_ready, 1)
                if u == 26:
                    lo_of(y_lo[:, 8:10, :], yd_f[:, :, :], y_hi[:, 8:10, :], 7, l).then_inc(ylo_ready, 1)

            def gated(l, which, b, o):
                br = {"A": 0, "B": 1, "C": 2, "D": 3}[which]
                return V.scalar_tensor_tensor(o, gates[:, br * KT + 2 * b:br * KT + 2 * b + 2, :]
                                              .rearrange("p f s -> p (f s)"), 1.0, bank[b][:, :], ALU.add, ALU.mult)

            def merge(l, u):
                if u == U_PROJ_A:
                    unit_done(l, u)
                    for b in range(4):
                        m = gates[:, 2 * b:2 * b + 2, :].rearrange("p f s -> p (f s)")
                        gated(l, "A", b, m).then_inc(bank_free[b], 1)
                if u in (U_PROJ_C, U_PROJ_D):
                    which = "C" if u == U_PROJ_C else "D"
                    unit_done(l, u)
                    for b in range(4):
                        i = 4 * (u - U_PROJ_C) + b
                        if i >= 1:
                            dve.wait_ge(madd_done, l * 8 + i)
                        gated(l, which, b, mtmp[:, i % 2, :]).then_inc(bank_free[b], 1)
                if u == U_PROJ_B + 1:
                    dve.wait_ge(madd_done, l * 8 + 9)
                    for b in range(4):
                        if b < 3:
                            dve.wait_ge(proj_b_done, l * 3 + b + 1)
                        else:
                            unit_done(l, u)
                        m = gates[:, 2 * b:2 * b + 2, :].rearrange("p f s -> p (f s)")
                        if b >= 2:
                            dve.wait_ge(merged_ready, l * 4 + b - 1)
                        gated(l, "B", b, mtmp[:, b % 2, :]).then_inc(bank_free[b], 1)
                        dve.wait_ge(bank_free[b], free_at(l, b, proj_use(b, "B") + 1))
                        V.tensor_tensor(m, m, mtmp[:, b % 2, :], ALU.add).then_inc(merged_ready, 1)
                        if b >= 1:
                            merged_lo(l, b - 1)
                    merged_lo(l, 3)
                if U_WO <= u < U_FFN:
                    b = u - U_WO
                    unit_done(l, u)
                    xv = x_res[:, 2 * b:2 * b + 2, :]
                    V.scalar_tensor_tensor(xv, low(b), 0.5, xv, ALU.mult, ALU.add).then_inc(x_ready, 1)

            def merged_lo(l, i):
                dve.wait_ge(act_hi_ready, l * 12 + (4 + i + 1))
                V.tensor_tensor(act_lo[:, 2 * i:2 * i + 2, :], gates[:, 2 * i:2 * i + 2, :],
                                act_hi[:, 2 * i:2 * i + 2, :].bitcast(F32), ALU.subtract).then_inc(act_lo_ready, 1)

            def ffn_up(l, slot, use, even, gate_free, j):
                if j is not None:
                    dve.wait_ge(fflo_ready, l * FF_STEPS + j)
                e, b = (0, 1) if even else (1, 3)
                dve.wait_ge(w_used[slot], l * USES + (use + 2))
                dve.wait_ge(bank_free[b - 1], gate_free)
                V.tensor_tensor(ff_a, ff_g[:, e, :], bank[b][:, :], ALU.mult).then_inc(bank_free[b], 1)

            def ffn_lo(l, even, cnt):
                e = 0 if even else 1
                dve.wait_ge(ffhi_ready, cnt + 1)
                V.tensor_tensor(ff_lo[:, e, :, :].rearrange("p f s -> p (f s)"), ff_a,
                                ff_hi[:, e, :, :].rearrange("p f s -> p (f s)").bitcast(F32), ALU.subtract)\
                    .then_inc(fflo_ready, 1)

            dve.wait_ge(pos_in, 16 * 2)
            posf, ang, turns, red_s, red_c = (sq[:, 0, :], sq[:, 1, :], sq[:, 2, :], xn[:, 1, 0, :], xn[:, 1, 1, :])
            magic = 1.5 * 2.0 ** 23
            c1 = 6.28125
            c2 = float(np.float32(np.round((2 * np.pi - c1) * 2 ** 20) / 2 ** 20))
            c3 = float(np.float32(2 * np.pi - c1 - c2))
            link(None, V.tensor_copy(posf, xn[:, 0, 0, :].bitcast(I32)))
            link(None, V.tensor_scalar(ang, posf, ifreq[:, 0:1], None, ALU.mult))
            for red, quarter in ((red_s, 0.0), (red_c, 0.25)):
                link(None, V.tensor_scalar(turns, ang, 1.0 / (2 * np.pi), quarter, ALU.mult, ALU.add))
                link(None, V.tensor_scalar(turns, turns, magic, None, ALU.add))
                link(None, V.tensor_scalar(turns, turns, magic, None, ALU.subtract))
                link(None, V.scalar_tensor_tensor(red, turns, -c1, ang, ALU.mult, ALU.add))
                link(None, V.scalar_tensor_tensor(red, turns, -c2, red, ALU.mult, ALU.add))
                link(None, V.scalar_tensor_tensor(red, turns, -c3, red, ALU.mult, ALU.add))
                link(None, V.tensor_scalar(red, red, quarter * 2 * np.pi, 3.1415925, ALU.add, ALU.min))
                link(None, V.tensor_scalar(red, red, -3.1415925, None, ALU.max))
            assert pre[0] == PRE_DVE_ROPE
            for i in range(4):
                dve.wait_ge(pre_pe, i + 1)
                V.tensor_copy(x_res[:, 2 * i:2 * i + 2, :], low(i)).then_inc(x_ready, 1)
            dve.wait_ge(pre_act, 1)
            dve.wait_ge(pre_const, 5)

            with dve.Fori(0, L) as l:
                split(l, 0, 0)
                norm_scale(l, 0)
                norm_all(l, 0)
                split(l, 1, 0)
                for u in range(U_FFN):
                    split(l, (u + 2) % RING, (u + 2) // RING)
                    misc(l, u)
                    merge(l, u)
                norm_scale(l, 1)
                norm_all(l, 1)
                split(l, (U_FFN + 2) % RING, (U_FFN + 2) // RING)
                split(l, (U_FFN + 3) % RING, (U_FFN + 3) // RING)
                ffn_up(l, (U_FFN + 1) % RING, (U_FFN + 1) // RING, True, free_at(l, 0, mixed[0] + 1), None)
                ffn_lo(l, True, l * FF_STEPS)

                def ffn_unit(l, base_u, use0, it, j0, c):
                    ahead = c + 2
                    split(l, (base_u + ahead) % RING, use0 + ((base_u + ahead) // RING - base_u // RING))
                    if c % 3 == 1:
                        h = c // 3
                        b = 0 if h else 2
                        ffn_up(l, (base_u + c) % RING, use0 + ((base_u + c) // RING - base_u // RING), h == 1,
                               l * BANK_USES[b] + (it + (mixed[b] + h + 2)), j0 + h)
                    if c % 3 == 2:
                        ffn_lo(l, c == 5, l * FF_STEPS + (j0 + c // 3))

                with dve.Fori(0, FF_ITERS) as it:
                    for c in range(6):
                        ffn_unit(l, U_LOOP, it * 2 + U_LOOP // RING, it, it * 2 + 1, c)
                for c in range(5):
                    ffn_unit(l, U_TAIL, U_TAIL // RING, FF_ITERS, J_TAIL, c)
                ffn_lo(l, True, l * FF_STEPS + (FF_STEPS - 1))
                u = UNITS - 1
                dve.wait_ge(w_used[u % RING], l * USES + (u // RING + 2))
                for b in range(4):
                    xv = x_res[:, 2 * b:2 * b + 2, :]
                    V.tensor_tensor(xv, low(4 + b), xv, ALU.add).then_inc(x_ready, 1)
            assert n[0] == DVE_CHAIN_PER_LAYER, n[0]

            dve.wait_ge(gfin_in, 16)
            dve.wait_ge(pre_act, 5)
            pre[0] = PRE_DVE_ROPE
            link(None, V.tensor_tensor(st[:, 0:2], ssq[:, 0:4:2], ssq[:, 1:4:2], ALU.add))
            link(None, V.tensor_scalar(st[:, 0:2], st[:, 0:2], 1.0 / D, EPS, ALU.mult, ALU.add))
            rsqrt(None, st[:, 2:4], st[:, 0:2], st[:, 4:6], ist[:, 0:2])
            assert pre[0] == PRE_DVE_OUT, pre[0]
            for h in range(4):
                ins = V.scalar_tensor_tensor(o_nat[:, h // 2, 512 * (h % 2):512 * (h % 2) + 512], bank[h][:, :],
                                             st[:, 2 + h // 2:3 + h // 2], g_fin[:, 512 * (h % 2):512 * (h % 2) + 512],
                                             ALU.mult, ALU.mult)
                if h % 2:
                    ins.then_inc(pre_dve, 1)


_INS = ["x", "positions", "norm_mix_g", "w_in", "w_gate", "b_gate", "pool_w", "pool_scale", "sgu_norm_g",
        "sgu_norm_b", "sgu_w", "sgu_b", "conv_w", "conv_b", "conv_norm_g", "conv_norm_b", "w_proj_a",
        "w_proj_b", "w_proj_c", "w_proj_d", "w_o", "norm_ffn_g", "w_ffn_in", "w_ffn_out", "final_norm_g"]


def kernel(**inputs):
    import numpy as _np
    import concourse.bacc as _bacc
    from concourse import mybir as _mybir
    from concourse.bass_utils import run_bass_kernel_spmd as _run

    nc = _bacc.Bacc("TRN2", target_bir_lowering=False, num_devices=1)
    arrays, T = {}, {}
    for name in _INS:
        a = _np.ascontiguousarray(inputs[name])
        arrays[f"in_{name}"] = a
        T[name] = nc.dram_tensor(f"in_{name}", a.shape, _mybir.dt.from_np(a.dtype), kind="ExternalInput").ap()
    S = inputs["x"].shape[1]
    half = HEAD_DIM // 2
    freq = (1.0 / (_np.float32(ROPE_THETA) ** (_np.arange(half, dtype=_np.float32) / half))).astype(_np.float32)
    consts = {
        "inv_freq": _np.tile(freq, P // half).reshape(P, 1),
        "inv_count": _np.stack([_np.repeat([1.0 / _np.minimum(_np.arange(S) + 1, w) for w in WINDOWS[2 * f:2 * f + 2]],
                                           P // 2, axis=0) for f in range(2)], axis=1).astype(_np.float32),
    }
    aps = {}
    for name, a in consts.items():
        arrays[name] = _np.ascontiguousarray(a)
        aps[name] = nc.dram_tensor(name, a.shape, _mybir.dt.float32, kind="ExternalInput").ap()
    out = nc.dram_tensor("out", inputs["x"].shape, _mybir.dt.float32, kind="ExternalOutput").ap()
    build(nc, T, out, aps["inv_freq"], aps["inv_count"])
    r = _run(nc, [arrays], core_ids=[0])
    return r.results[0]["out"]
```

```python
from contextlib import ExitStack

import numpy as np

import concourse.bass as bass
from concourse import mybir

ALU = mybir.AluOpType
ACT = mybir.ActivationFunctionType
AX = mybir.AxisListType
F32 = mybir.dt.float32
F32R = mybir.dt.float32r
BF16 = mybir.dt.bfloat16
I32 = mybir.dt.int32

P = 128
EPS = 1e-6
NEG = -1e30
WINDOWS = (2, 4, 8, 16)
HEAD_DIM = 64
ROPE_THETA = 10000.0
PAD = 16

RING = 3
UC = 256
W_IN_UNITS = (("q", 256), ("q", 512), ("k", 768), ("k", 1024), ("sgu_v", 2048), ("glu_gate", 2560),
              ("glu_in", 2304), ("v", 1280), ("v", 1536), ("sgu_u", 1792), ("pool", 0))
N_IN = len(W_IN_UNITS)
U_GATE = N_IN
U_PROJ_A = U_GATE + 16
U_PROJ_C = U_PROJ_A + 1
U_PROJ_B = U_PROJ_A + 2
U_PROJ_D = U_PROJ_A + 4
U_WO = U_PROJ_A + 5
U_FFN = U_WO + 4
FF_STEPS = 11
UNITS = U_FFN + 3 * FF_STEPS
USES = UNITS // RING
FF_ITERS = 4
U_LOOP = U_FFN + 2
U_TAIL = U_LOOP + 6 * FF_ITERS
J_TAIL = 1 + 2 * FF_ITERS
GATE_BRANCH = (0, 2, 3, 1)

BANKS = {b: [f"unit{u}" for u in range(U_PROJ_A) if u % 4 == b] + ["A", "B"] for b in range(4)}
BANKS[2] += ["stat2"]
BANKS[3] += ["R2"]
FFN_FROM = [len(BANKS[b]) for b in range(4)]
for b in range(4):
    BANKS[b] += [f"ffn{j}" for j in range(b // 2, FF_STEPS, 2)]
BANKS[4] = ["perm0", "S0", "PV0", "S1", "PV1", "S2", "PV2", "S3", "PV3", "C", "D"]
BANKS[5] = ["perm1", "S0", "F", "S1", "pool", "S2", "cT1", "S3", "cT2", "C", "D"]
BANKS[6] = ["par", "R1", "perm2", "wsT", "PT0", "PT1", "PT2", "PT3", "C", "D"]
BANKS[7] = ["stat1", "perm3", "PT0", "PT1", "PT2", "PT3", "C", "D"]
TAPS = {8: 4, 9: 3, 10: 1, 11: 4, 12: 4, 14: 2, 15: 2, 16: 2, 17: 4, 18: 2, 19: 3}

ROWS = {"b_gate": (0, 32), "pool_scale": (32, 2), "conv_b": (34, 2), "conv_norm_g": (36, 2),
        "conv_norm_b": (38, 2), "conv_w": (40, 62)}
N_ROWS = 102
DVE_CHAIN_PER_LAYER = 80
POOL_CHAIN_PER_LAYER = 8
PRE_DVE_ROPE = 18
PRE_DVE_OUT = PRE_DVE_ROPE + 14


def build(nc, T, out, inv_freq, inv_count):
    L, D, IN_DIM = T["w_in"].shape
    S = T["x"].shape[1]
    FF = T["w_ffn_out"].shape[1]
    KT = D // P
    TT = S // P
    CW = T["conv_w"].shape[1]
    HP = 4
    SCALE = float(HEAD_DIM) ** -0.5
    assert FF == FF_STEPS * UC and UNITS % RING == 0 and U_LOOP % RING == 2

    with ExitStack() as ctx:
        def sb(name, shape, dt=F32):
            return ctx.enter_context(nc.sbuf_tensor(name, shape, dt))

        def sem(name):
            return ctx.enter_context(nc.semaphore(name))

        raw = [sb(f"raw{s}", [P, 8 * UC]) for s in range(RING)]
        w_hi = [sb(f"w_hi{s}", [P, 8 * UC], F32R) for s in range(RING)]
        w_lo = [sb(f"w_lo{s}", [P, 8 * UC], F32R) for s in range(RING)]
        x_res = sb("x_res", [P, KT, S])
        sq = sb("sq", [P, KT, S])
        act_hi = sb("act_hi", [P, KT, S], F32R)
        act_lo = sb("act_lo", [P, KT, S], F32R)
        gates = sb("gates", [P, 4 * KT, S])
        qk = sb("qk", [P, 8, S])
        rot = sb("rot", [P, 2, S])
        v_sb = sb("v_sb", [P, TT, 512])
        y_hi = sb("y_hi", [P, 10, S], F32R)
        y_lo = sb("y_lo", [P, 10, S], F32R)
        conv_h = sb("conv_h", [P, 2, 32 + S])
        xa = sb("xa", [P, 2, PAD + S])
        ff_hi = sb("ff_hi", [P, 2, 2, S], F32R)
        ff_lo = sb("ff_lo", [P, 2, 2, S], F32R)
        yd_f = sb("yd_f", [P, 2, S])
        rms_b = sb("rms_b", [P, 1, S])
        cos_r = sb("cos_r", [P, 1, S])
        sin_r = sb("sin_r", [P, 1, S])

        def part(owner, a, shape):
            flat = owner.rearrange("p k s -> p (k s)") if len(owner.shape) == 3 else owner
            n = int(np.prod(shape))
            return flat[:, a:a + n].rearrange("p (i j) -> p i j", j=shape[-1]) if len(shape) == 2 else flat[:, a:a + n]

        conv_a, swish_t = rot, rot
        glu_t = yd_f
        probs = part(sq[:, :, :], 0, [2, 3 * P])
        probsT = part(sq[:, :, :], 6 * P, [2, 3 * P])
        conv_n = part(sq[:, :, :], 12 * P, [TT, 256])
        E = PAD + S
        g_b = gates[:, KT:2 * KT, :]
        s2, s4 = part(g_b, 0, [2, E]), part(g_b, 2 * E, [2, E])
        s8, s16 = part(g_b, 4 * E, [E]), part(g_b, 5 * E, [E])
        g_d = gates[:, 3 * KT:4 * KT, :]
        zv, zu = g_d[:, 0:2, :], g_d[:, 2:4, :]
        yc_f, ya_f, pooled = g_d[:, 4:6, :], g_d[:, 0:2, :], g_d[:, 6:8, :]
        mtmp = part(qk[:, :, :], 0, [2, 2 * S])
        ff_g, ff_u, ff_a = (qk[:, 2 * i:2 * i + 2, :] for i in range(3))
        rows = sb("rows", [N_ROWS, P])
        gain_rows = sb("gain_rows", [2 * L * KT, P])
        gains = sb("gains", [P, 2 * L * KT])
        par = sb("par", [P, N_ROWS])
        half_bg = sb("half_bg", [P, 32])
        ln_g = sb("ln_g", [P, 256])
        ln_b = sb("ln_b", [P, 256])
        sgu_bias = sb("sgu_bias", [P, 2, P])
        pool_w = sb("pool_w", [P, 2, P])
        ws_nat = sb("ws_nat", [P, 4, P])
        wsT = sb("wsT", [P, 4, P])
        ident = sb("ident", [P, P])
        ones = sb("ones", [P, P])
        zeros = sb("zeros", [P, 2 * S], BF16)
        rot_perm = sb("rot_perm", [P, P])
        causal = sb("causal", [P, 384], BF16)
        ident16 = sb("ident16", [P, P], BF16)
        cos_t = sb("cos_t", [P, 1, S])
        sin_t = sb("sin_t", [P, 1, S])
        icnt = sb("icnt", [P, 2, S])
        ifreq = sb("ifreq", [P, 1])
        st = sb("st", [P, 16])
        ist = sb("ist", [P, 4], I32)
        rms_t = sb("rms_t", [P, TT])
        diag = sb("diag", [P, TT, P])
        bn6 = sb("bn6", [P, TT, 6])
        mv = sb("mv", [P, TT, 2])
        mx = sb("mx", [P, 4])
        nmx = sb("nmx", [P, 4])
        den = sb("den", [P, 4])
        rden = sb("rden", [P, 4])
        ssq = sb("ssq", [P, 4])

        bank = [ctx.enter_context(nc.psum_tensor(f"bank{b}", [P, 512], F32)) for b in range(8)]

        raw_full = [sem(f"raw_full{s}") for s in range(RING)]
        raw_claimed = sem("raw_claimed")
        hi_ready = [sem(f"hi_ready{s}") for s in range(RING)]
        lo_ready = [sem(f"lo_ready{s}") for s in range(RING)]
        w_used = [sem(f"w_used{s}") for s in range(RING)]
        bank_free = [sem(f"bank_free{b}") for b in range(8)]
        x_ready = sem("x_ready")
        sq_done = sem("sq_done")
        ssum_ready = sem("ssum_ready")
        stat_done = sem("stat_done")
        diag_ready = sem("diag_ready")
        rms_done = sem("rms_done")
        rms_ready = sem("rms_ready")
        table_ready = sem("table_ready")
        glu_ready = sem("glu_ready")
        gelu_done = sem("gelu_done")
        gate_ready = sem("gate_ready")
        rden_ready = sem("rden_ready")
        pj_done = sem("pj_done")
        ydp_done = sem("ydp_done")
        swish_ready = sem("swish_ready")
        silu_done = sem("silu_done")
        ffa_ready = sem("ffa_ready")
        act_hi_ready = sem("act_hi_ready")
        act_lo_ready = sem("act_lo_ready")
        par_done = sem("par_done")
        perm_done = sem("perm_done")
        rope_ready = sem("rope_ready")
        tri_ready = sem("tri_ready")
        wst_done = sem("wst_done")
        vn_ready = sem("vn_ready")
        f_done = sem("f_done")
        yc_ready = sem("yc_ready")
        pooled_ready = sem("pooled_ready")
        pool_done = sem("pool_done")
        conv_tap = sem("conv_tap")
        ct1_done = sem("ct1_done")
        ct2_done = sem("ct2_done")
        yd_ready = sem("yd_ready")
        s_done = sem("s_done")
        nmx_ready = sem("nmx_ready")
        probs_ready = sem("probs_ready")
        pt_done = sem("pt_done")
        pv_done = sem("pv_done")
        yhi_ready = sem("yhi_ready")
        ylo_ready = sem("ylo_ready")
        merged_ready = sem("merged_ready")
        madd_done = sem("madd_done")
        ffhi_ready = sem("ffhi_ready")
        fflo_ready = sem("fflo_ready")
        mats_seen = sem("mats_seen")
        rows_in = sem("rows_in")
        mats_in = sem("mats_in")
        params_free = sem("params_free")
        dve_chain = sem("dve_chain")
        pool_chain = sem("pool_chain")
        x_in = [sem(f"x_in{i}") for i in range(4)]
        gain_in = sem("gain_in")
        pos_in = sem("pos_in")
        icnt_in = sem("icnt_in")
        gfin_in = sem("gfin_in")
        pre_const = sem("pre_const")
        pre_x0 = sem("pre_x0")
        pre_dve = sem("pre_dve")
        pre_act = sem("pre_act")
        pre_pe = sem("pre_pe")
        out_done = sem("out_done")

        def free_at(l, b, what, after=False):
            return l * len(BANKS[b]) + (BANKS[b].index(what) + (2 if after else 1))

        def kview(t):
            return t[:, :].rearrange("p (k n) -> p k n", n=UC)

        def wide(t):
            return t[:, :].rearrange("p (k n) -> p k n", n=D)

        def low(b):
            return bank[b][:, :].rearrange("p (f s) -> p f s", f=2)

        x_nat = gates[:, 0:8, :].rearrange("p k s -> p (k s)").rearrange("p (t d) -> p t d", t=TT)
        g_fin = gates[:, 8:12, :].rearrange("p k s -> p (k s)")
        o_nat = gates[:, 16:24, :].rearrange("p k s -> p (k s)").rearrange("p (t d) -> p t d", t=TT)
        pos_i = gates[:, 8, :].bitcast(I32)
        red_s, red_c = gates[:, 9, :], gates[:, 10, :]
        junk = gates[:, 24:32, :].rearrange("p k s -> p (k s)").rearrange("p (h n) -> p h n", h=4)

        block = ctx.enter_context(nc.Block())

        @block.sync
        def _(sp):
            for i in range(4):
                cs = slice(i * 2 * P, (i + 1) * 2 * P)
                sp.dma_start(x_nat[:, :, cs], T["x"][0].rearrange("(t p) d -> p t d", p=P)[:, :, cs])\
                    .then_inc(x_in[i], 16)

            def load(l, slot, use, src, n=UC):
                sp.wait_ge(lo_ready[slot], l * USES + use + 1)
                sp.sem_inc(raw_claimed, 1)
                sp.dma_start(raw[slot][:, :].rearrange("p (k n) -> p k n", n=n), src)\
                    .then_inc(raw_full[slot], 16)

            def cols(w, l, c0):
                return w[l].rearrange("(k p) n -> p k n", p=P)[:, :, c0:c0 + UC]

            def down(l, r0):
                return T["w_ffn_out"][l].rearrange("(j k p) n -> j p k n", p=P, k=2)[r0]

            def ffn_load(l, kind, j, slot, use):
                if kind == "G":
                    load(l, slot, use, T["w_ffn_in"][l].rearrange("(k p) (h j n) -> h j p k n", p=P, h=2, n=UC)[0, j])
                elif kind == "U":
                    load(l, slot, use, T["w_ffn_in"][l].rearrange("(k p) (h j n) -> h j p k n", p=P, h=2, n=UC)[1, j])
                else:
                    load(l, slot, use, down(l, j), n=D)

            with sp.Fori(0, L) as l:
                for u in range(U_FFN):
                    slot, use = u % RING, u // RING
                    if u < U_GATE:
                        load(l, slot, use, cols(T["w_in"], l, W_IN_UNITS[u][1]))
                    elif u < U_PROJ_A:
                        g, dp = divmod(u - U_GATE, 4)
                        load(l, slot, use, cols(T["w_gate"], l, GATE_BRANCH[g] * D + dp * UC))
                    elif u in (U_PROJ_A, U_PROJ_C, U_PROJ_D):
                        w = T["w_proj_" + {U_PROJ_A: "a", U_PROJ_C: "c", U_PROJ_D: "d"}[u]]
                        load(l, slot, use, w[l].rearrange("(k p) n -> p k n", p=P), n=D)
                    elif u < U_WO:
                        load(l, slot, use, T["w_proj_b"][l].rearrange("(j k p) n -> j p k n", p=P, k=2)[u - U_PROJ_B],
                             n=D)
                    else:
                        load(l, slot, use, cols(T["w_o"], l, (u - U_WO) * UC))
                ffn_load(l, "G", 0, U_FFN % RING, U_FFN // RING)
                ffn_load(l, "U", 0, (U_FFN + 1) % RING, (U_FFN + 1) // RING)
                with sp.Fori(0, FF_ITERS) as it:
                    for c in range(6):
                        ffn_load(l, "GUO"[c % 3], it * 2 + c // 3 + (c % 3 != 2),
                                 (U_LOOP + c) % RING, it * 2 + (U_LOOP + c) // RING)
                for u in range(U_TAIL, UNITS):
                    c = u - U_TAIL
                    kind = "GUO"[c % 3] if u < UNITS - 1 else "O"
                    j = J_TAIL + c // 3 - (kind == "O") if u < UNITS - 1 else FF_STEPS - 1
                    ffn_load(l, kind, j, u % RING, u // RING)

            sp.wait_ge(x_ready, 8 * L)
            sp.dma_start(g_fin, T["final_norm_g"].partition_broadcast(P)).then_inc(gfin_in, 16)
            for t in range(TT):
                sp.wait_ge(pre_dve, PRE_DVE_OUT + t + 1)
                sp.dma_start(out[0].rearrange("(t p) d -> t p d", p=P)[t], o_nat[:, t, :])\
                    .then_inc(out_done, 16)
            sp.wait_ge(out_done, 16 * TT)

        @block.gpsimd
        def _(pool):
            pool.dma_start(ifreq[:, :], inv_freq).then_inc(pos_in, 16)
            pool.dma_start(pos_i, T["positions"].to_broadcast([P, S]))\
                .then_inc(pos_in, 16)
            nc.gpsimd.memset(ident[:, :], 0.0).then_inc(pre_const, 1)
            pool.wait_ge(pre_const, 1)
            nc.gpsimd.affine_select(out=ident[:, :], in_=ident[:, :], compare_op=ALU.not_equal, fill=1.0,
                                    base=0, pattern=[[-1, P]], channel_multiplier=1).then_inc(pre_const, 1)
            nc.gpsimd.memset(ones[:, :], 1.0).then_inc(pre_const, 1)
            nc.gpsimd.memset(rot_perm[:, :], 0.0)
            nc.gpsimd.memset(causal[:, :], 0.0)
            nc.gpsimd.memset(zeros[:, :], 0.0)
            nc.gpsimd.memset(conv_h[:, :, :], 0.0)
            nc.gpsimd.memset(pool_w[:, :, :], 0.0)
            nc.gpsimd.memset(xa[:, :, 0:PAD], 0.0).then_inc(pre_const, 1)
            pool.wait_ge(pre_const, 4)
            nc.gpsimd.tensor_copy(ident16[:, :], ident[:, :])
            for m0 in range(0, P, 32):
                first = m0 % HEAD_DIM == 0
                src0 = m0 + 32 if first else m0 - 32
                blk = rot_perm[:, m0:m0 + 32]
                nc.gpsimd.affine_select(out=blk, in_=blk, compare_op=ALU.not_equal, fill=-1.0 if first else 1.0,
                                        base=-src0, pattern=[[-1, 32]], channel_multiplier=1)
            for c0 in (0, 2 * P):
                blk = causal[:, c0:c0 + P]
                last = nc.gpsimd.affine_select(out=blk, in_=blk, compare_op=ALU.is_ge, fill=NEG,
                                               base=0, pattern=[[-1, P]], channel_multiplier=1)
            last.then_inc(pre_const, 1)
            pool.sem_inc(madd_done, 1)
            pool.dma_start(icnt[:, :, :], inv_count).then_inc(icnt_in, 16)

            n = [0]

            def link(l, ins):
                n[0] += 1
                ins.then_inc(pool_chain, 1)
                pool.wait_ge(pool_chain, l * POOL_CHAIN_PER_LAYER + n[0])

            with pool.Fori(0, L) as l:
                pool.wait_ge(params_free, l + 1)
                for name, (r0, k) in ROWS.items():
                    src = T[name][l]
                    if name == "conv_w":
                        src = src.rearrange("w (c p) -> (w c) p", p=P)
                    else:
                        src = src.rearrange("(r p) -> r p", p=P)
                    pool.dma_start(rows[r0:r0 + k, :], src).then_inc(rows_in, 16)
                pool.dma_start(ws_nat[:, :, :], T["sgu_w"][l].rearrange("g t s -> t g s")).then_inc(mats_in, 16)
                pool.dma_start(ln_g[:, :], T["sgu_norm_g"][l].partition_broadcast(P)).then_inc(mats_in, 16)
                pool.dma_start(ln_b[:, :], T["sgu_norm_b"][l].partition_broadcast(P)).then_inc(mats_in, 16)
                for g in range(4):
                    half = slice(64 * (g % 2), 64 * (g % 2) + 64)
                    pool.dma_start(sgu_bias[half, g // 2, :], T["sgu_b"][l, g].partition_broadcast(64))\
                        .then_inc(mats_in, 16)
                    pool.dma_start(pool_w[half, g // 2, half], T["pool_w"][l, g]).then_inc(mats_in, 16)
                pool.wait_ge(mats_in, l * (16 * 11) + 16 * 11)
                pool.sem_inc(mats_seen, 1)
                nc.gpsimd.affine_select(out=ws_nat[:, :, :], in_=ws_nat[:, :, :], compare_op=ALU.is_ge, fill=0.0,
                                        base=0, pattern=[[0, 4], [-1, P]], channel_multiplier=1).then_inc(tri_ready, 1)
                pool.wait_ge(bank_free[2], free_at(l, 2, "unit10", True))
                pool.wait_ge(icnt_in, 16)
                link(l, nc.gpsimd.tensor_tensor(s2[:, :, 1:E], xa[:, :, 1:E], xa[:, :, 0:E - 1], ALU.add))
                link(l, nc.gpsimd.tensor_tensor(s4[:, :, 4:E], s2[:, :, 4:E], s2[:, :, 2:E - 2], ALU.add))
                link(l, nc.gpsimd.tensor_tensor(s8[:, 8:E], s4[:, 1, 8:E], s4[:, 1, 4:E - 4], ALU.add))
                link(l, nc.gpsimd.tensor_tensor(s16[:, 16:E], s8[:, 16:E], s8[:, 8:E - 8], ALU.add))
                for g, total in enumerate((s2[:, 0], s4[:, 0], s8, s16)):
                    half = slice(64 * (g % 2), 64 * (g % 2) + 64)
                    link(l, nc.gpsimd.tensor_tensor(pooled[half, g // 2, :], total[half, PAD:E],
                                                    icnt[half, g // 2, :], ALU.mult))
                nc.gpsimd.tensor_tensor(pooled[:, :, :], pooled[:, :, :], xa[:, :, PAD:E], ALU.subtract)\
                    .then_inc(pooled_ready, 1)
                for i in range(8):
                    dp = i % 4
                    b, which = (4 + dp, "C") if i < 4 else (dp, "B")
                    pool.wait_ge(bank_free[b], free_at(l, b, which, True))
                    m = gates[:, 2 * dp:2 * dp + 2, :].rearrange("p f s -> p (f s)")
                    nc.gpsimd.tensor_tensor(m, m, mtmp[:, i % 2, :], ALU.add).then_inc(madd_done, 1)
            assert n[0] == POOL_CHAIN_PER_LAYER

        @block.scalar
        def _(act):
            for i, name in enumerate(("norm_mix_g", "norm_ffn_g")):
                act.dma_start(gain_rows[i * L * KT:(i + 1) * L * KT, :], T[name].rearrange("l (r p) -> (l r) p", p=P))\
                    .then_inc(gain_in, 16)
            for s in range(RING):
                act.sem_inc(w_used[s], 1)
            for b in range(8):
                act.sem_inc(bank_free[b], 1)

            def copy(o, i):
                return nc.scalar.activation(o, i, ACT.Copy)

            def split(l, slot, use):
                act.wait_ge(raw_full[slot], (l * USES + use + 1) * 16)
                act.wait_ge(w_used[slot], l * USES + use + 1)
                copy(w_hi[slot][:, :], raw[slot][:, :]).then_inc(hi_ready[slot], 1)

            def xg_hi(l, n, i):
                act.wait_ge(x_ready, l * 8 + (4 * n + i + 1))
                for f in range(2):
                    k = 2 * i + f
                    last = nc.scalar.activation((act_hi, y_hi)[n][:, k, :], x_res[:, k, :], ACT.Copy,
                                                scale=gains[:, bass.ds(l * KT + (n * L * KT + k), 1)])
                last.then_inc(act_hi_ready, 1)

            def square(l, n, i):
                act.wait_ge(x_ready, l * 8 + (4 * n + i + 1))
                nc.scalar.activation(sq[:, 2 * i:2 * i + 2, :], x_res[:, 2 * i:2 * i + 2, :], ACT.Square)\
                    .then_inc(sq_done, 1)

            def rms_copy(l, n):
                b, what = (6, "R1") if n == 0 else (3, "R2")
                act.wait_ge(rms_done, l * 2 + (n + 1))
                copy(rms_b[:, 0, :], bank[b][:, 0:S]).then_inc(bank_free[b], 1)

            def unit_done(l, u):
                act.wait_ge(w_used[u % RING], l * USES + (u // RING + 2))

            def evac(l, u):
                b = u % 4
                if u < 4:
                    unit_done(l, u)
                    copy(qk[:, 2 * u:2 * u + 2, :], low(b)).then_inc(bank_free[b], 1)
                elif u in (4, 7, 8):
                    unit_done(l, u)
                    act.wait_ge(diag_ready, l * 2 + 1)
                    for t in range(TT):
                        if u == 4:
                            last = nc.scalar.activation(zv[:, t, :], low(b)[:, t, :], ACT.Gelu_apprx_tanh,
                                                        scale=rms_t[:, t:t + 1])
                        else:
                            last = nc.scalar.activation(v_sb[:, t, (u - 7) * UC:(u - 6) * UC], low(b)[:, t, :],
                                                        ACT.Copy, scale=rms_t[:, t:t + 1])
                    last.then_inc(bank_free[b], 1)
                elif u == 5:
                    act.wait_ge(bank_free[b], free_at(l, b, "unit5", True))
                    nc.scalar.activation(glu_t[:, :, :], glu_t[:, :, :], ACT.Tanh, scale=0.5).then_inc(glu_ready, 1)
                elif u == 9:
                    act.wait_ge(bank_free[b], free_at(l, b, "unit9", True))
                    nc.scalar.activation(zu, zu, ACT.Gelu_apprx_tanh).then_inc(gelu_done, 1)
                elif U_GATE <= u < U_PROJ_A:
                    g, dp = divmod(u - U_GATE, 4)
                    act.wait_ge(bank_free[b], free_at(l, b, f"unit{u}", True))
                    for f in range(2):
                        k = GATE_BRANCH[g] * KT + 2 * dp + f
                        last = nc.scalar.activation(gates[:, k, :], gates[:, k, :], ACT.Tanh, scale=0.5,
                                                    bias=half_bg[:, k:k + 1])
                    last.then_inc(gate_ready, 1)

            def misc(l, u):
                if u == 0:
                    act.wait_ge(par_done, l + 1)
                    copy(par[:, :], bank[6][:, 0:N_ROWS])
                    r0, k = ROWS["b_gate"]
                    nc.scalar.activation(half_bg[:, :], bank[6][:, r0:r0 + k], ACT.Copy, scale=0.5)\
                        .then_inc(bank_free[6], 1)
                    act.wait_ge(bank_free[6], free_at(l, 6, "par", True))
                if u == 1:
                    rms_copy(l, 0)
                if u == 6:
                    act.wait_ge(wst_done, l + 1)
                    copy(wsT[:, :, :], bank[6][:, :].rearrange("p (g s) -> p g s", g=4)).then_inc(bank_free[6], 1)
                if u in (10, 14, 18, 22):
                    hp = (u - 10) // 4
                    act.wait_ge(nmx_ready, l * HP + hp + 1)
                    for i in range(2):
                        for q, (a, b) in enumerate(((0, P), (P, 3 * P))):
                            c = 2 * q + i
                            last = nc.scalar.activation(probs[:, i, a:b], bank[4 + i][:, a:b], ACT.Exp, scale=SCALE,
                                                        bias=nmx[:, c:c + 1], accum_out=den[:, c:c + 1])
                        last.then_inc(bank_free[4 + i], 1)
                if u in (11, 15, 19, 23):
                    hp = (u - 11) // 4
                    act.wait_ge(rden_ready, l * HP + hp + 1)
                    for i in range(2):
                        for q, (a, b) in enumerate(((0, P), (P, 3 * P))):
                            c = 2 * q + i
                            last = nc.scalar.activation(probs[:, i, a:b], probs[:, i, a:b], ACT.Copy,
                                                        scale=rden[:, c:c + 1])
                    last.then_inc(probs_ready, 1)
                if u in (12, 16, 20, 24):
                    hp = (u - 12) // 4
                    for i in range(2):
                        act.wait_ge(pt_done, l * 2 * HP + 2 * hp + i + 1)
                        copy(probsT[:, i, :], bank[6 + i][:, 0:3 * P]).then_inc(bank_free[6 + i], 1)
                if u in (13, 17, 21, 25):
                    hp = (u - 13) // 4
                    act.wait_ge(pv_done, l * HP + hp + 1)
                    copy(y_hi[:, 2 + hp, :], bank[4][:, 0:S]).then_inc(yhi_ready, 1)
                if u == 14:
                    act.wait_ge(yc_ready, l + 1)
                    copy(y_hi[:, 6:8, :], yc_f).then_inc(yhi_ready, 1)
                if u == 16:
                    act.wait_ge(pool_done, l + 1)
                    for f in range(2):
                        c = ROWS["pool_scale"][0] + f
                        last = nc.scalar.activation(ya_f[:, f, :], bank[5][:, f * S:(f + 1) * S], ACT.Copy,
                                                    scale=par[:, c:c + 1])
                    last.then_inc(bank_free[5], 1)
                    act.wait_ge(bank_free[5], free_at(l, 5, "pool", True))
                    copy(y_hi[:, 0:2, :], ya_f).then_inc(yhi_ready, 1)
                if u == 24:
                    act.wait_ge(ct2_done, l + 1)
                    for f in range(2):
                        cg, cb = ROWS["conv_norm_g"][0] + f, ROWS["conv_norm_b"][0] + f
                        last = nc.scalar.activation(yd_f[:, f, :], bank[5][:, f * S:(f + 1) * S], ACT.Identity,
                                                    scale=par[:, cg:cg + 1], bias=par[:, cb:cb + 1])
                    last.then_inc(bank_free[5], 1)
                    act.wait_ge(bank_free[5], free_at(l, 5, "cT2", True))
                    nc.scalar.activation(swish_t[:, :, :], yd_f[:, :, :], ACT.Tanh, scale=0.5).then_inc(swish_ready, 1)
                if u == 26:
                    act.wait_ge(yd_ready, l + 1)
                    copy(y_hi[:, 8:10, :], yd_f[:, :, :]).then_inc(yhi_ready, 1)
                if u == U_PROJ_D:
                    for i in range(4):
                        act.wait_ge(merged_ready, l * 4 + i + 1)
                        copy(act_hi[:, 2 * i:2 * i + 2, :], gates[:, 2 * i:2 * i + 2, :]).then_inc(act_hi_ready, 1)
                if U_WO <= u < U_FFN:
                    xg_hi(l, 1, u - U_WO)
                    square(l, 1, u - U_WO)

            def ffn_silu(l, even, it):
                b = 0 if even else 2
                act.wait_ge(bank_free[b], l * len(BANKS[b]) + (it + (FFN_FROM[b] + (3 if even else 2))))
                nc.scalar.activation(ff_g, ff_g, ACT.Silu).then_inc(silu_done, 1)

            def ffn_hi(l, even, j):
                act.wait_ge(ffa_ready, l * FF_STEPS + (j + 1))
                copy(ff_hi[:, 0 if even else 1, :, :], ff_a).then_inc(ffhi_ready, 1)

            act.wait_ge(pre_dve, PRE_DVE_ROPE)
            nc.scalar.activation(sin_t[:, 0, :], red_s, ACT.Sin)
            nc.scalar.activation(cos_t[:, 0, :], red_c, ACT.Sin).then_inc(pre_act, 1)
            act.wait_ge(pre_pe, 1)
            copy(gains[:, :], bank[0][:, 0:2 * L * KT]).then_inc(pre_act, 1)
            act.wait_ge(pre_act, 2)

            with act.Fori(0, L) as l:
                split(l, 0, 0)
                split(l, 1, 0)
                for i in range(4):
                    xg_hi(l, 0, i)
                for i in range(4):
                    square(l, 0, i)
                for u in range(U_FFN):
                    split(l, (u + 2) % RING, (u + 2) // RING)
                    evac(l, u)
                    misc(l, u)
                split(l, (U_FFN + 2) % RING, (U_FFN + 2) // RING)
                split(l, (U_FFN + 3) % RING, (U_FFN + 3) // RING)
                rms_copy(l, 1)
                ffn_silu(l, True, -1)
                ffn_hi(l, True, 0)

                def ffn_unit(l, base_u, use0, it, c):
                    ahead = c + 2
                    split(l, (base_u + ahead) % RING, use0 + ((base_u + ahead) // RING - base_u // RING))
                    if c % 3 == 0:
                        ffn_silu(l, c == 3, it)
                    elif c % 3 == 1:
                        ffn_hi(l, c == 4, it * 2 + (c // 3 + 1))

                with act.Fori(0, FF_ITERS) as it:
                    for c in range(6):
                        ffn_unit(l, U_LOOP, it * 2 + U_LOOP // RING, it, c)
                for c in range(5):
                    ffn_unit(l, U_TAIL, U_TAIL // RING, FF_ITERS, c)

            for h in range(4):
                act.wait_ge(pre_pe, 2 + h)
                nc.scalar.activation(junk[:, h, :], bank[h][:, :], ACT.Square, accum_out=ssq[:, h:h + 1]).then_inc(pre_act, 1)

        @block.tensor
        def _(pe):
            def mm3(o, whi, wlo, ahi, alo, first, last, skip=False):
                nc.tensor.matmul(o, whi, ahi, start=first, stop=False, skip_group_check=skip)
                nc.tensor.matmul(o, whi, alo, start=False, stop=False, skip_group_check=skip)
                return nc.tensor.matmul(o, wlo, ahi, start=False, stop=last, skip_group_check=skip)

            def weights(l, slot, use):
                pe.wait_ge(lo_ready[slot], l * USES + use + 2)

            def bank_wait(l, b, what):
                pe.wait_ge(bank_free[b], free_at(l, b, what))

            def unit(l, slot, b, wait_k=None, a_hi=act_hi, a_lo=act_lo):
                hi, lo = kview(w_hi[slot]), kview(w_lo[slot])
                for f in range(2):
                    fs = slice(f * P, f * P + P)
                    for k in range(KT):
                        if wait_k is not None and f == 0 and k % 2 == 0:
                            pe.wait_ge(act_lo_ready, wait_k + (k // 2 + 1))
                        last = mm3(low(b)[:, f, :], hi[:, k, fs], lo[:, k, fs], a_hi[:, k, :], a_lo[:, k, :],
                                   k == 0, k == KT - 1)
                last.then_inc(w_used[slot], 1)

            def unit_natural(slot, b):
                hi, lo = kview(w_hi[slot]), kview(w_lo[slot])
                for t in range(TT):
                    ts = slice(t * P, t * P + P)
                    for k in range(KT):
                        o = low(b)[:, t, :]
                        nc.tensor.matmul(o, act_hi[:, k, ts], hi[:, k, :], start=(k == 0), stop=False)
                        nc.tensor.matmul(o, act_hi[:, k, ts], lo[:, k, :], start=False, stop=False)
                        last = nc.tensor.matmul(o, act_lo[:, k, ts], hi[:, k, :], start=False, stop=(k == KT - 1))
                last.then_inc(w_used[slot], 1)

            def unit_rows(slot, b0, hi_in, lo_in, first, last_k, done=None):
                hi, lo = wide(w_hi[slot]), wide(w_lo[slot])
                for dp in range(4):
                    for f in range(2):
                        fs = slice((2 * dp + f) * P, (2 * dp + f + 1) * P)
                        for k in range(2):
                            last = mm3(low(b0 + dp)[:, f, :], hi[:, k, fs], lo[:, k, fs], hi_in[k], lo_in[k],
                                       first and f == 0 and k == 0, last_k and k == 1, skip=True)
                    if done is not None and dp < 3:
                        last.then_inc(done, 1)
                last.then_inc(w_used[slot], 1)

            def norm_stat(l, n):
                b, what = (7, "stat1") if n == 0 else (2, "stat2")
                bank_wait(l, b, what)
                pe.wait_ge(ssum_ready, l * 2 + (n + 1))
                for t in range(TT):
                    last = nc.tensor.matmul(bank[b][:, t:t + 1], sq[:, 0, t * P:t * P + P], ones[:, 0:1],
                                            start=True, stop=True)
                last.then_inc(stat_done, 1)

            def norm_rms(l, n):
                b, what = (6, "R1") if n == 0 else (3, "R2")
                bank_wait(l, b, what)
                pe.wait_ge(diag_ready, l * 2 + (n + 1))
                for t in range(TT):
                    last = nc.tensor.matmul(bank[b][:, t * P:t * P + P], ones[:, :], diag[:, t, :], start=True, stop=True)
                last.then_inc(rms_done, 1)

            def misc(l, u):
                if u == 0:
                    norm_stat(l, 0)
                    pe.wait_ge(rows_in, l * (16 * len(ROWS)) + 16 * len(ROWS))
                    bank_wait(l, 6, "par")
                    nc.tensor.transpose(bank[6][:, 0:N_ROWS], rows[:, :], ident[0:N_ROWS, 0:N_ROWS])\
                        .then_inc(par_done, 1)
                if u == 1:
                    norm_rms(l, 0)
                if 2 <= u <= 5:
                    i = u - 2
                    bank_wait(l, 4 + i, f"perm{i}")
                    pe.wait_ge(bank_free[i], free_at(l, i, f"unit{i}", True))
                    nc.tensor.matmul(bank[4 + i][:, :], rot_perm[:, :],
                                     qk[:, 2 * i:2 * i + 2, :].rearrange("p f s -> p (f s)"),
                                     start=True, stop=True).then_inc(perm_done, 1)
                if u == 6:
                    bank_wait(l, 6, "wsT")
                    pe.wait_ge(tri_ready, l + 1)
                    for g in range(4):
                        last = nc.tensor.transpose(bank[6][:, g * P:(g + 1) * P], ws_nat[:, g, :], ident[:, :])
                    last.then_inc(wst_done, 1)
                if u in (10, 14, 18, 22):
                    hp = (u - 10) // 4
                    if hp == 0:
                        pe.wait_ge(rope_ready, l * 4 + 4)
                    for i in range(2):
                        bank_wait(l, 4 + i, f"S{hp}")
                        h = slice(64 * i, 64 * i + 64)
                        s_bank = bank[4 + i]
                        nc.tensor.matmul(s_bank[:, 0:3 * P], ident16[:, :], causal[:, :], start=True, stop=False,
                                         skip_group_check=True)
                        nc.tensor.matmul(s_bank[:, 0:P], qk[h, hp, 0:P], qk[h, 4 + hp, 0:P], start=False, stop=False,
                                         skip_group_check=True)
                        nc.tensor.matmul(s_bank[:, P:3 * P], qk[h, hp, P:2 * P], qk[h, 4 + hp, :],
                                         start=False, stop=True, skip_group_check=True).then_inc(s_done, 1)
                if u in (12, 16, 20, 24):
                    hp = (u - 12) // 4
                    pe.wait_ge(probs_ready, l * HP + hp + 1)
                    for i in range(2):
                        bank_wait(l, 6 + i, f"PT{hp}")
                        for c in range(3):
                            last = nc.tensor.transpose(bank[6 + i][:, c * P:(c + 1) * P], probs[:, i, c * P:(c + 1) * P],
                                                       ident[:, :])
                        last.then_inc(pt_done, 1)
                if u in (13, 17, 21, 25):
                    hp = (u - 13) // 4
                    bank_wait(l, 4, f"PV{hp}")
                    for i in range(2):
                        pe.wait_ge(bank_free[6 + i], free_at(l, 6 + i, f"PT{hp}", True))
                        o = bank[4][64 * i:64 * i + 64, :]
                        c0 = (2 * hp + i) * HEAD_DIM
                        nc.tensor.matmul(o[:, 0:S], v_sb[:, 0, c0:c0 + HEAD_DIM], probsT[:, i, 0:2 * P],
                                         start=True, stop=False, skip_group_check=True)
                        last = nc.tensor.matmul(o[:, P:S], v_sb[:, 1, c0:c0 + HEAD_DIM], probsT[:, i, 2 * P:3 * P],
                                                start=False, stop=True, skip_group_check=True)
                    last.then_inc(pv_done, 1)
                if u == 13:
                    bank_wait(l, 5, "F")
                    pe.wait_ge(vn_ready, l + 1)
                    pe.wait_ge(bank_free[6], free_at(l, 6, "wsT", True))
                    for g in range(4):
                        for t in range(TT):
                            c0 = (g // 2) * S + t * P
                            last = nc.tensor.matmul(bank[5][64 * (g % 2):64 * (g % 2) + 64, c0:c0 + P],
                                                    zv[:, t, g * 64:(g + 1) * 64], wsT[:, g, :], start=True, stop=True)
                    last.then_inc(f_done, 1)
                if u == 16:
                    bank_wait(l, 5, "pool")
                    pe.wait_ge(pooled_ready, l + 1)
                    for f in range(2):
                        last = nc.tensor.matmul(bank[5][:, f * S:(f + 1) * S], pool_w[:, f, :], pooled[:, f, :],
                                                start=True, stop=True)
                    last.then_inc(pool_done, 1)
                if u == 20:
                    bank_wait(l, 5, "cT1")
                    pe.wait_ge(conv_tap, l * (2 * CW) + 2 * CW)
                    for t in range(TT):
                        for f in range(2):
                            last = nc.tensor.transpose(bank[5][:, t * 256 + f * P:t * 256 + (f + 1) * P],
                                                       conv_a[:, f, t * P:(t + 1) * P], ident[:, :])
                    last.then_inc(ct1_done, 1)
                if u == 24:
                    bank_wait(l, 5, "cT2")
                    pe.wait_ge(bank_free[5], free_at(l, 5, "cT1", True))
                    for t in range(TT):
                        for f in range(2):
                            last = nc.tensor.transpose(bank[5][:, f * S + t * P:f * S + (t + 1) * P],
                                                       conv_n[:, t, f * P:(f + 1) * P], ident[:, :])
                    last.then_inc(ct2_done, 1)

            def ffn_in(l, slot, use, b, it, wait_k=None):
                weights(l, slot, use)
                pe.wait_ge(bank_free[b], l * len(BANKS[b]) + (it + (FFN_FROM[b] + 1)))
                unit(l, slot, b, wait_k, y_hi, y_lo)

            def ffn_out(l, slot, use, even, j, last_unit=False):
                weights(l, slot, use)
                pe.wait_ge(fflo_ready, l * FF_STEPS + (j + 1))
                e = 0 if even else 1
                unit_rows(slot, 4, [ff_hi[:, e, k, :] for k in range(2)], [ff_lo[:, e, k, :] for k in range(2)],
                          False, last_unit, done=ydp_done if last_unit else None)

            pe.wait_ge(pre_const, 3)
            pe.wait_ge(gain_in, 16 * 2)
            nc.tensor.transpose(bank[0][:, 0:2 * L * KT], gain_rows[:, :], ident[0:2 * L * KT, 0:2 * L * KT])\
                .then_inc(pre_pe, 1)
            for i in range(4):
                pe.wait_ge(x_in[i], 16)
                for f in range(2):
                    for t in range(TT):
                        k = 2 * i + f
                        last = nc.tensor.transpose(low(4 + i)[:, f, t * P:(t + 1) * P], x_nat[:, t, k * P:(k + 1) * P],
                                                   ident[:, :])
                last.then_inc(ydp_done, 1)
            pe.wait_ge(pre_act, 2)
            pe.wait_ge(pre_const, 5)

            with pe.Fori(0, L) as l:
                for u in range(U_PROJ_A):
                    weights(l, u % RING, u // RING)
                    bank_wait(l, u % 4, f"unit{u}")
                    if u < N_IN and W_IN_UNITS[u][0] in ("v", "sgu_v"):
                        unit_natural(u % RING, u % 4)
                    else:
                        unit(l, u % RING, u % 4, l * 12 if u == 0 else None)
                    misc(l, u)
                for u, which, part, b0, k0 in ((U_PROJ_A, "A", 0, 0, 0), (U_PROJ_C, "C", 0, 4, 6),
                                               (U_PROJ_B, "B", 0, 0, 2), (U_PROJ_B + 1, "B", 1, 0, 4),
                                               (U_PROJ_D, "D", 0, 4, 8)):
                    weights(l, u % RING, u // RING)
                    if which == "A":
                        pe.wait_ge(ylo_ready, l + 1)
                    if part == 0:
                        for b in range(b0, b0 + 4):
                            bank_wait(l, b, which)
                    complete = which != "B" or part == 1
                    unit_rows(u % RING, b0, [y_hi[:, k0 + k, :] for k in range(2)], [y_lo[:, k0 + k, :] for k in range(2)],
                              part == 0, complete, done=pj_done if complete else None)
                for i in range(4):
                    u = U_WO + i
                    weights(l, u % RING, u // RING)
                    pe.wait_ge(bank_free[i], free_at(l, i, "B", True))
                    unit(l, u % RING, i, l * 12 + 4 if i == 0 else None)
                pe.wait_ge(x_ready, l * 8 + 6)
                ffn_in(l, U_FFN % RING, U_FFN // RING, 0, 0, l * 12 + 8)
                norm_stat(l, 1)
                ffn_in(l, (U_FFN + 1) % RING, (U_FFN + 1) // RING, 1, 0)
                norm_rms(l, 1)
                for b in range(4, 8):
                    pe.wait_ge(bank_free[b], free_at(l, b, "D", True))
                    nc.tensor.matmul(bank[b][:, :], zeros[:, 0:P], zeros[:, :], start=True, stop=False,
                                     skip_group_check=True)

                def ffn_pair(l, c, use0, it):
                    for h in range(2):
                        b = 0 if h else 2
                        uses = [use0 + ((c + 3 * h + i) // RING - c // RING) for i in range(3)]
                        ffn_in(l, (c + 3 * h) % RING, uses[0], b, it + h)
                        ffn_in(l, (c + 3 * h + 1) % RING, uses[1], b + 1, it + h)
                        ffn_out(l, (c + 3 * h + 2) % RING, uses[2], h == 0, it * 2 + h)

                with pe.Fori(0, FF_ITERS) as it:
                    ffn_pair(l, U_LOOP, it * 2 + U_LOOP // RING, it)
                ffn_pair(l, U_TAIL, U_TAIL // RING, FF_ITERS)
                u = UNITS - 1
                ffn_out(l, u % RING, u // RING, True, FF_STEPS - 1, last_unit=True)

            pe.wait_ge(x_ready, 8 * L + 4)
            for h in range(4):
                for c in range(4):
                    k = 4 * (h % 2) + c
                    last = nc.tensor.transpose(bank[h][:, c * P:(c + 1) * P], x_res[:, k, (h // 2) * P:(h // 2 + 1) * P],
                                               ident[:, :])
                last.then_inc(pre_pe, 1)

        @block.vector
        def _(dve):
            for s in range(RING):
                dve.sem_inc(lo_ready[s], 1)
            dve.sem_inc(params_free, 1)
            V = nc.vector
            n = [0]
            pre = [0]

            def link(l, ins):
                if l is None:
                    pre[0] += 1
                    ins.then_inc(pre_dve, 1)
                    dve.wait_ge(pre_dve, pre[0])
                else:
                    n[0] += 1
                    ins.then_inc(dve_chain, 1)
                    dve.wait_ge(dve_chain, l * DVE_CHAIN_PER_LAYER + n[0])

            def rsqrt(l, o, v, tmp, bits):
                link(l, V.tensor_scalar(bits, v.bitcast(I32), 1, None, ALU.logical_shift_right))
                link(l, V.tensor_scalar(v, v, -0.5, None, ALU.mult))
                link(l, V.tensor_scalar(o.bitcast(I32), bits, -1.0, float(0x5F3759DF), ALU.mult, ALU.add))
                for _ in range(3):
                    link(l, V.tensor_tensor(tmp, o, o, ALU.mult))
                    link(l, V.tensor_tensor(tmp, tmp, v, ALU.mult))
                    link(l, V.scalar_tensor_tensor(o, tmp, 1.5, o, ALU.add, ALU.mult))

            def split(l, slot, use):
                dve.wait_ge(hi_ready[slot], l * USES + use + 1)
                V.tensor_tensor(w_lo[slot][:, :], raw[slot][:, :], w_hi[slot][:, :].bitcast(F32), ALU.subtract)\
                    .then_inc(lo_ready[slot], 1)

            def x_update(l, n, i):
                xv = x_res[:, 2 * i:2 * i + 2, :]
                if n == 0:
                    V.tensor_tensor(xv, low(4 + i), xv, ALU.add).then_inc(x_ready, 1)
                else:
                    V.scalar_tensor_tensor(xv, low(i), 0.5, xv, ALU.mult, ALU.add).then_inc(x_ready, 1)

            def y_wait(l, i):
                if i < 3:
                    dve.wait_ge(ydp_done, l * 3 + (i + 2))
                else:
                    dve.wait_ge(w_used[(UNITS - 1) % RING], l * USES + 1)

            def xg_lo(l, n, i):
                dve.wait_ge(act_hi_ready, l * 12 + (8 * n + i + 1))
                for f in range(2):
                    k = 2 * i + f
                    last = V.scalar_tensor_tensor((act_lo, y_lo)[n][:, k, :], x_res[:, k, :],
                                                  gains[:, bass.ds(l * KT + (n * L * KT + k), 1)],
                                                  (act_hi, y_hi)[n][:, k, :].bitcast(F32), ALU.mult, ALU.subtract)
                last.then_inc(act_lo_ready, 1)

            def square_sum(l, n):
                for i in (0, 2):
                    dve.wait_ge(sq_done, l * 8 + (4 * n + i + 2))
                    a = sq[:, 2 * i:2 * i + 2, :]
                    link(l, V.tensor_tensor(a, a, sq[:, 2 * i + 2:2 * i + 4, :], ALU.add))
                link(l, V.tensor_tensor(sq[:, 0:2, :], sq[:, 0:2, :], sq[:, 4:6, :], ALU.add))
                V.tensor_tensor(sq[:, 0, :], sq[:, 0, :], sq[:, 1, :], ALU.add).then_inc(ssum_ready, 1)

            def norm_scale(l, n):
                b, what = (7, "stat1") if n == 0 else (2, "stat2")
                dve.wait_ge(stat_done, l * 2 + (n + 1))
                V.tensor_scalar(st[:, 0:2], bank[b][:, 0:2], 1.0 / D, EPS, ALU.mult, ALU.add).then_inc(bank_free[b], 1)
                dve.wait_ge(bank_free[b], free_at(l, b, what, True))
                rsqrt(l, rms_t[:, 0:2], st[:, 0:2], st[:, 4:6], ist[:, 0:2])
                for t in range(TT):
                    last = V.tensor_scalar(diag[:, t, :], ident[:, :], rms_t[:, t:t + 1], None, ALU.mult)
                last.then_inc(diag_ready, 1)

            def scaled(out, b, l):
                return V.tensor_tensor(out, low(b), rms_b[:, :, :].to_broadcast([P, 2, S]), ALU.mult)

            def unit_done(l, u):
                dve.wait_ge(w_used[u % RING], l * USES + (u // RING + 2))

            def lo_of(o_lo, src, o_hi, count, l):
                dve.wait_ge(yhi_ready, l * 7 + count)
                return V.tensor_tensor(o_lo, src, o_hi.bitcast(F32), ALU.subtract)

            def conv_taps(l, w0, w1):
                for w in range(w0, w1):
                    for f in range(2):
                        c = ROWS["conv_w"][0] + 2 * w + f
                        src = conv_h[:, f, 32 - (CW - 1) + w:32 - (CW - 1) + w + S]
                        if w == 0:
                            cb = ROWS["conv_b"][0] + f
                            ins = V.tensor_scalar(conv_a[:, f, :], src, par[:, c:c + 1], par[:, cb:cb + 1],
                                                  ALU.mult, ALU.add)
                        else:
                            dve.wait_ge(conv_tap, l * (2 * CW) + (2 * (w - 1) + f + 1))
                            ins = V.scalar_tensor_tensor(conv_a[:, f, :], src, par[:, c:c + 1], conv_a[:, f, :],
                                                         ALU.mult, ALU.add)
                        ins.then_inc(conv_tap, 1)

            def misc(l, u):
                if 2 <= u <= 5:
                    i = u - 2
                    if i == 0:
                        dve.wait_ge(bank_free[6], free_at(l, 6, "R1", True))
                        link(l, V.tensor_tensor(cos_r[:, :, :], cos_t[:, :, :], rms_b[:, :, :], ALU.mult))
                        link(l, V.tensor_tensor(sin_r[:, :, :], sin_t[:, :, :], rms_b[:, :, :], ALU.mult))
                    else:
                        dve.wait_ge(rope_ready, l * 4 + i)
                    r = rot[:, :, :]
                    dst = qk[:, 2 * i:2 * i + 2, :]
                    dve.wait_ge(perm_done, l * 4 + i + 1)
                    V.tensor_tensor(r, low(4 + i), sin_r[:, :, :].to_broadcast([P, 2, S]), ALU.mult)\
                        .then_inc(bank_free[4 + i], 1)
                    link(l, V.tensor_tensor(dst, dst, cos_r[:, :, :].to_broadcast([P, 2, S]), ALU.mult))
                    dve.wait_ge(bank_free[4 + i], free_at(l, 4 + i, f"perm{i}", True))
                    V.tensor_tensor(dst, dst, r, ALU.add).then_inc(rope_ready, 1)
                if u == 5:
                    unit_done(l, 5)
                    scaled(glu_t[:, :, :], 1, l).then_inc(bank_free[1], 1)
                if u == 6:
                    dve.wait_ge(glu_ready, l + 1)
                    link(l, V.tensor_scalar(glu_t[:, :, :], glu_t[:, :, :], 0.5, 0.5, ALU.mult, ALU.add))
                    link(l, V.tensor_tensor(glu_t[:, :, :], glu_t[:, :, :], rms_b[:, :, :].to_broadcast([P, 2, S]),
                                            ALU.mult))
                    unit_done(l, 6)
                    V.tensor_tensor(conv_h[:, :, 32:32 + S], glu_t[:, :, :], low(2), ALU.mult)\
                        .then_inc(bank_free[2], 1)
                    dve.wait_ge(bank_free[2], free_at(l, 2, "unit6", True))
                if u == 9:
                    unit_done(l, 9)
                    scaled(zu, 1, l).then_inc(bank_free[1], 1)
                if u == 10:
                    unit_done(l, 10)
                    scaled(xa[:, :, PAD:PAD + S], 2, l).then_inc(bank_free[2], 1)
                if U_GATE <= u < U_PROJ_A:
                    g, dp = divmod(u - U_GATE, 4)
                    k = GATE_BRANCH[g] * KT + 2 * dp
                    unit_done(l, u)
                    scaled(gates[:, k:k + 2, :], u % 4, l).then_inc(bank_free[u % 4], 1)
                if u == 7:
                    dve.wait_ge(bank_free[0], free_at(l, 0, "unit4", True))
                    for t in range(TT):
                        link(l, V.bn_stats(bn6[:, t, :], zv[:, t, :]))
                        V.memset(st[:, 14:15], 0.0)
                        link(l, V.bn_aggr(mv[:, t, :], bn6[:, t, :]))
                    link(l, V.tensor_scalar(st[:, 8:10], mv[:, :, 1], EPS, None, ALU.add))
                    rsqrt(l, st[:, 10:12], st[:, 8:10], st[:, 12:14], ist[:, 2:4])
                    for t in range(TT):
                        link(l, V.tensor_scalar(zv[:, t, :], zv[:, t, :], mv[:, t, 0:1], st[:, 10 + t:11 + t],
                                                ALU.subtract, ALU.mult))
                    dve.wait_ge(mats_seen, l + 1)
                    link(l, V.tensor_tensor(zv[:, :, :], zv[:, :, :],
                                            ln_g[:, :].unsqueeze(1).to_broadcast([P, TT, 256]), ALU.mult))
                    V.tensor_tensor(zv[:, :, :], zv[:, :, :],
                                    ln_b[:, :].unsqueeze(1).to_broadcast([P, TT, 256]), ALU.add).then_inc(vn_ready, 1)
                if u in TAPS:
                    w0 = sum(TAPS[v] for v in TAPS if v < u)
                    conv_taps(l, w0, w0 + TAPS[u])
                if u in (10, 14, 18, 22):
                    hp = (u - 10) // 4
                    for i in range(2):
                        dve.wait_ge(s_done, l * 2 * HP + 2 * hp + i + 1)
                        V.tensor_reduce(mx[:, i:i + 1], bank[4 + i][:, 0:P], AX.X, ALU.max)
                        last = V.tensor_reduce(mx[:, 2 + i:3 + i], bank[4 + i][:, P:3 * P], AX.X, ALU.max)
                    link(l, last)
                    V.tensor_scalar(nmx[:, :], mx[:, :], -SCALE, None, ALU.mult).then_inc(nmx_ready, 1)
                if u in (11, 15, 19, 23):
                    hp = (u - 11) // 4
                    for i in range(2):
                        dve.wait_ge(bank_free[4 + i], free_at(l, 4 + i, f"S{hp}", True))
                    V.reciprocal(rden[:, :], den[:, :]).then_inc(rden_ready, 1)
                if u == 13:
                    dve.wait_ge(f_done, l + 1)
                    for f in range(2):
                        last = V.tensor_tensor(yc_f[:, f, :].rearrange("p (t s) -> p t s", t=TT),
                                               bank[5][:, f * S:(f + 1) * S].rearrange("p (t s) -> p t s", t=TT),
                                               sgu_bias[:, f:f + 1, :].to_broadcast([P, TT, P]), ALU.add)
                    last.then_inc(bank_free[5], 1)
                    dve.wait_ge(bank_free[5], free_at(l, 5, "F", True))
                    dve.wait_ge(gelu_done, l + 1)
                    V.tensor_tensor(yc_f, yc_f, zu[:, :, :], ALU.mult).then_inc(yc_ready, 1)
                if u in (13, 17, 21, 25):
                    hp = (u - 13) // 4
                    count = (1, 4, 5, 6)[hp]
                    lo_of(y_lo[:, 2 + hp, :], bank[4][:, 0:S], y_hi[:, 2 + hp, :], count, l).then_inc(bank_free[4], 1)
                if u == 15:
                    lo_of(y_lo[:, 6:8, :], yc_f, y_hi[:, 6:8, :], 2, l)
                if u == 16:
                    lo_of(y_lo[:, 0:2, :], ya_f, y_hi[:, 0:2, :], 3, l).then_inc(params_free, 1)
                if u == 20:
                    dve.wait_ge(ct1_done, l + 1)
                    nat = bank[5][:, :].rearrange("p (t c) -> p t c", t=TT)
                    for t in range(TT):
                        link(l, V.bn_stats(bn6[:, t, :], nat[:, t, :]))
                        V.memset(st[:, 14:15], 0.0)
                        link(l, V.bn_aggr(mv[:, t, :], bn6[:, t, :]))
                    link(l, V.tensor_scalar(st[:, 8:10], mv[:, :, 1], EPS, None, ALU.add))
                    rsqrt(l, st[:, 10:12], st[:, 8:10], st[:, 12:14], ist[:, 2:4])
                    for t in range(TT):
                        last = V.tensor_scalar(conv_n[:, t, :], nat[:, t, :], mv[:, t, 0:1], st[:, 10 + t:11 + t],
                                               ALU.subtract, ALU.mult)
                    last.then_inc(bank_free[5], 1)
                if u == 25:
                    dve.wait_ge(swish_ready, l + 1)
                    link(l, V.tensor_scalar(swish_t[:, :, :], swish_t[:, :, :], 0.5, 0.5, ALU.mult, ALU.add))
                    V.tensor_tensor(yd_f[:, :, :], yd_f[:, :, :], swish_t[:, :, :], ALU.mult).then_inc(yd_ready, 1)
                if u == 26:
                    lo_of(y_lo[:, 8:10, :], yd_f[:, :, :], y_hi[:, 8:10, :], 7, l).then_inc(ylo_ready, 1)

            def gated(which, dp, b, o):
                k = {"A": 0, "B": 1, "C": 2, "D": 3}[which] * KT + 2 * dp
                return V.scalar_tensor_tensor(o, gates[:, k:k + 2, :], 1.0, low(b), ALU.add, ALU.mult)

            def merge(l, u):
                if u in (U_PROJ_A, U_PROJ_C, U_PROJ_B + 1, U_PROJ_D):
                    nth, which, b0 = {U_PROJ_A: (0, "A", 0), U_PROJ_C: (1, "C", 4), U_PROJ_B + 1: (2, "B", 0),
                                      U_PROJ_D: (3, "D", 4)}[u]
                    if which == "A":
                        dve.wait_ge(gate_ready, l * 16 + 16)
                    if which == "D":
                        dve.wait_ge(madd_done, l * 8 + 9)
                    for dp in range(4):
                        if dp < 3:
                            dve.wait_ge(pj_done, l * 12 + (3 * nth + dp + 1))
                        else:
                            unit_done(l, u)
                        b, m = b0 + dp, gates[:, 2 * dp:2 * dp + 2, :]
                        tmp = mtmp[:, dp % 2, :].rearrange("p (f s) -> p f s", f=2)
                        if which == "A":
                            gated(which, dp, b, m).then_inc(bank_free[b], 1)
                        elif which in "CB":
                            i = 4 * (nth - 1) + dp
                            if i >= 1:
                                dve.wait_ge(madd_done, l * 8 + i)
                            gated(which, dp, b, tmp).then_inc(bank_free[b], 1)
                        else:
                            if dp >= 2:
                                dve.wait_ge(merged_ready, l * 4 + dp - 1)
                            gated(which, dp, b, tmp).then_inc(bank_free[b], 1)
                            dve.wait_ge(bank_free[b], free_at(l, b, "D", True))
                            V.tensor_tensor(m, m, tmp, ALU.add).then_inc(merged_ready, 1)
                            if dp >= 1:
                                merged_lo(l, dp - 1)
                    if which == "D":
                        merged_lo(l, 3)
                if U_WO <= u < U_FFN:
                    unit_done(l, u)
                    x_update(l, 1, u - U_WO)
                    xg_lo(l, 1, u - U_WO)

            def merged_lo(l, i):
                dve.wait_ge(act_hi_ready, l * 12 + (4 + i + 1))
                V.tensor_tensor(act_lo[:, 2 * i:2 * i + 2, :], gates[:, 2 * i:2 * i + 2, :],
                                act_hi[:, 2 * i:2 * i + 2, :].bitcast(F32), ALU.subtract).then_inc(act_lo_ready, 1)

            def ffn_gate(l, slot, use, even, j):
                b = 0 if even else 2
                if j is not None:
                    dve.wait_ge(ffa_ready, l * FF_STEPS + j)
                dve.wait_ge(w_used[slot], l * USES + (use + 2))
                scaled(ff_g, b, l).then_inc(bank_free[b], 1)

            def ffn_up(l, slot, use, even, j, it):
                b = 1 if even else 3
                dve.wait_ge(w_used[slot], l * USES + (use + 2))
                scaled(ff_u, b, l).then_inc(bank_free[b], 1)
                if j is not None:
                    dve.wait_ge(fflo_ready, l * FF_STEPS + j)
                dve.wait_ge(bank_free[b], l * len(BANKS[b]) + (it + (FFN_FROM[b] + (3 if even else 2))))
                dve.wait_ge(silu_done, l * FF_STEPS + (1 if j is None else j + 1))
                V.tensor_tensor(ff_a, ff_g, ff_u, ALU.mult).then_inc(ffa_ready, 1)

            def ffn_lo(l, even, j):
                e = 0 if even else 1
                dve.wait_ge(ffhi_ready, l * FF_STEPS + (j + 1))
                V.tensor_tensor(ff_lo[:, e, :, :], ff_a, ff_hi[:, e, :, :].bitcast(F32), ALU.subtract)\
                    .then_inc(fflo_ready, 1)

            dve.wait_ge(pos_in, 16 * 2)
            posf, ang, turns = sq[:, 0, :], sq[:, 1, :], sq[:, 2, :]
            magic = 1.5 * 2.0 ** 23
            c1 = 6.28125
            c2 = float(np.float32(np.round((2 * np.pi - c1) * 2 ** 20) / 2 ** 20))
            c3 = float(np.float32(2 * np.pi - c1 - c2))
            link(None, V.tensor_copy(posf, pos_i))
            link(None, V.tensor_scalar(ang, posf, ifreq[:, 0:1], None, ALU.mult))
            for red, quarter in ((red_s, 0.0), (red_c, 0.25)):
                link(None, V.tensor_scalar(turns, ang, 1.0 / (2 * np.pi), quarter, ALU.mult, ALU.add))
                link(None, V.tensor_scalar(turns, turns, magic, None, ALU.add))
                link(None, V.tensor_scalar(turns, turns, magic, None, ALU.subtract))
                link(None, V.scalar_tensor_tensor(red, turns, -c1, ang, ALU.mult, ALU.add))
                link(None, V.scalar_tensor_tensor(red, turns, -c2, red, ALU.mult, ALU.add))
                link(None, V.scalar_tensor_tensor(red, turns, -c3, red, ALU.mult, ALU.add))
                link(None, V.tensor_scalar(red, red, quarter * 2 * np.pi, 3.1415925, ALU.add, ALU.min))
                link(None, V.tensor_scalar(red, red, -3.1415925, None, ALU.max))
            assert pre[0] == PRE_DVE_ROPE
            V.memset(x_res[:, :, :], 0.0).then_inc(pre_x0, 1)
            dve.wait_ge(pre_x0, 1)
            dve.wait_ge(pre_act, 2)
            dve.wait_ge(pre_const, 5)

            with dve.Fori(0, L) as l:
                split(l, 0, 0)
                for i in range(4):
                    y_wait(l, i)
                    x_update(l, 0, i)
                    if i >= 1:
                        xg_lo(l, 0, i - 1)
                xg_lo(l, 0, 3)
                split(l, 1, 0)
                square_sum(l, 0)
                for u in range(U_FFN):
                    split(l, (u + 2) % RING, (u + 2) // RING)
                    if u == 0:
                        norm_scale(l, 0)
                    misc(l, u)
                    merge(l, u)
                square_sum(l, 1)
                split(l, (U_FFN + 2) % RING, (U_FFN + 2) // RING)
                norm_scale(l, 1)
                split(l, (U_FFN + 3) % RING, (U_FFN + 3) // RING)
                dve.wait_ge(bank_free[3], free_at(l, 3, "R2", True))
                ffn_gate(l, U_FFN % RING, U_FFN // RING, True, None)
                ffn_up(l, (U_FFN + 1) % RING, (U_FFN + 1) // RING, True, None, -1)
                ffn_lo(l, True, 0)

                def ffn_unit(l, base_u, use0, it, c):
                    ahead = c + 2
                    split(l, (base_u + ahead) % RING, use0 + ((base_u + ahead) // RING - base_u // RING))
                    use, slot = use0 + ((base_u + c) // RING - base_u // RING), (base_u + c) % RING
                    j = it * 2 + (c // 3 + 1)
                    if c % 3 == 0:
                        ffn_gate(l, slot, use, c == 3, j)
                    if c % 3 == 1:
                        ffn_up(l, slot, use, c == 4, j, it)
                    if c % 3 == 2:
                        ffn_lo(l, c == 5, j)

                with dve.Fori(0, FF_ITERS) as it:
                    for c in range(6):
                        ffn_unit(l, U_LOOP, it * 2 + U_LOOP // RING, it, c)
                for c in range(5):
                    ffn_unit(l, U_TAIL, U_TAIL // RING, FF_ITERS, c)
                ffn_lo(l, True, FF_STEPS - 1)
            assert n[0] == DVE_CHAIN_PER_LAYER, n[0]

            for i in range(4):
                y_wait(L, i)
                x_update(L, 0, i)
            dve.wait_ge(gfin_in, 16)
            dve.wait_ge(pre_act, 6)
            pre[0] = PRE_DVE_ROPE
            link(None, V.tensor_tensor(st[:, 0:2], ssq[:, 0:4:2], ssq[:, 1:4:2], ALU.add))
            link(None, V.tensor_scalar(st[:, 0:2], st[:, 0:2], 1.0 / D, EPS, ALU.mult, ALU.add))
            rsqrt(None, st[:, 2:4], st[:, 0:2], st[:, 4:6], ist[:, 0:2])
            assert pre[0] == PRE_DVE_OUT, pre[0]
            for h in range(4):
                ins = V.scalar_tensor_tensor(o_nat[:, h // 2, 512 * (h % 2):512 * (h % 2) + 512], bank[h][:, :],
                                             st[:, 2 + h // 2:3 + h // 2], g_fin[:, 512 * (h % 2):512 * (h % 2) + 512],
                                             ALU.mult, ALU.mult)
                if h % 2:
                    ins.then_inc(pre_dve, 1)


_INS = ["x", "positions", "norm_mix_g", "w_in", "w_gate", "b_gate", "pool_w", "pool_scale", "sgu_norm_g",
        "sgu_norm_b", "sgu_w", "sgu_b", "conv_w", "conv_b", "conv_norm_g", "conv_norm_b", "w_proj_a",
        "w_proj_b", "w_proj_c", "w_proj_d", "w_o", "norm_ffn_g", "w_ffn_in", "w_ffn_out", "final_norm_g"]


def kernel(**inputs):
    import numpy as _np
    import concourse.bacc as _bacc
    from concourse import mybir as _mybir
    from concourse.bass_utils import run_bass_kernel_spmd as _run

    nc = _bacc.Bacc("TRN2", target_bir_lowering=False, num_devices=1)
    arrays, T = {}, {}
    for name in _INS:
        a = _np.ascontiguousarray(inputs[name])
        arrays[f"in_{name}"] = a
        T[name] = nc.dram_tensor(f"in_{name}", a.shape, _mybir.dt.from_np(a.dtype), kind="ExternalInput").ap()
    S = inputs["x"].shape[1]
    half = HEAD_DIM // 2
    freq = (1.0 / (_np.float32(ROPE_THETA) ** (_np.arange(half, dtype=_np.float32) / half))).astype(_np.float32)
    consts = {
        "inv_freq": _np.tile(freq, P // half).reshape(P, 1),
        "inv_count": _np.stack([_np.repeat([1.0 / _np.minimum(_np.arange(S) + 1, w) for w in WINDOWS[2 * f:2 * f + 2]],
                                           P // 2, axis=0) for f in range(2)], axis=1).astype(_np.float32),
    }
    aps = {}
    for name, a in consts.items():
        arrays[name] = _np.ascontiguousarray(a)
        aps[name] = nc.dram_tensor(name, a.shape, _mybir.dt.float32, kind="ExternalInput").ap()
    out = nc.dram_tensor("out", inputs["x"].shape, _mybir.dt.float32, kind="ExternalOutput").ap()
    build(nc, T, out, aps["inv_freq"], aps["inv_count"])
    r = _run(nc, [arrays], core_ids=[0])
    return r.results[0]["out"]
```

```python
from contextlib import ExitStack

import numpy as np

import concourse.bass as bass
from concourse import mybir

ALU = mybir.AluOpType
ACT = mybir.ActivationFunctionType
AX = mybir.AxisListType
F32 = mybir.dt.float32
F32R = mybir.dt.float32r
BF16 = mybir.dt.bfloat16
I32 = mybir.dt.int32

P = 128
EPS = 1e-6
NEG = -1e30
WINDOWS = (2, 4, 8, 16)
HEAD_DIM = 64
ROPE_THETA = 10000.0
PAD = 16

RING = 3
UC = 256
W_IN_UNITS = (("q", 256), ("q", 512), ("k", 768), ("k", 1024), ("sgu_v", 2048), ("glu_gate", 2560),
              ("glu_in", 2304), ("v", 1280), ("v", 1536), ("sgu_u", 1792), ("pool", 0))
N_IN = len(W_IN_UNITS)
U_GATE = N_IN
GATE_BRANCH = (0, 2, 1, 3)
U_PROJ_A = U_GATE + 12
U_PROJ_C = U_PROJ_A + 1
U_PROJ_B = U_PROJ_A + 2
U_PROJ_D = U_PROJ_A + 4
U_GATE_D = U_PROJ_A + 5
U_WO = U_GATE_D + 4
U_FFN = U_WO + 4
FF_STEPS = 11
UNITS = U_FFN + 3 * FF_STEPS
USES = UNITS // RING
FF_ITERS = 4
U_LOOP = U_FFN + 2
U_TAIL = U_LOOP + 6 * FF_ITERS
J_TAIL = 1 + 2 * FF_ITERS
ORDER_A = tuple((U_PROJ_A + i) % 4 for i in range(4))


def gate_of(u):
    if U_GATE <= u < U_PROJ_A:
        i, dp = divmod(u - U_GATE, 4)
        return GATE_BRANCH[i], dp
    if U_GATE_D <= u < U_WO:
        return 3, u - U_GATE_D
    return None


BANKS = {b: [f"unit{u}" for u in range(U_PROJ_A) if u % 4 == b] + ["A", "B", f"unit{U_GATE_D + b}"] for b in range(4)}
BANKS[2] += ["stat2"]
BANKS[3] += ["R2"]
FFN_FROM = [len(BANKS[b]) for b in range(4)]
for b in range(4):
    BANKS[b] += [f"ffn{j}" for j in range(b // 2, FF_STEPS, 2)]
BANKS[4] = ["perm0", "S0", "S1", "S2", "S3", "C", "D"]
BANKS[5] = ["perm1", "S0", "S1", "S2", "cT1", "S3", "cT2", "C", "D"]
BANKS[6] = ["par", "R1", "perm2", "wsT", "PT0", "PV0", "PT1", "PV1", "PT2", "PV2", "PT3", "PV3", "C", "D"]
BANKS[7] = ["stat1", "perm3", "PT0", "F", "PT1", "pool", "PT2", "PT3", "C", "D"]
ATT = (10, 13, 16, 19)
TAPS = {7: 5, 9: 3, 10: 1, 11: 3, 12: 4, 13: 2, 14: 5, 15: 4, 16: 4}
POOL_TAPS_FIRST = 8

ROWS = {"b_gate": (0, 32), "pool_scale": (32, 2), "conv_b": (34, 2), "conv_norm_g": (36, 2),
        "conv_norm_b": (38, 2), "conv_w": (40, 62)}
N_ROWS = 102
DVE_CHAIN_PER_LAYER = 80
POOL_CHAIN_PER_LAYER = 8
PRE_DVE_ROPE = 10
PRE_DVE_OUT = PRE_DVE_ROPE + 14


def build(nc, T, out, inv_freq, inv_count):
    L, D, IN_DIM = T["w_in"].shape
    S = T["x"].shape[1]
    FF = T["w_ffn_out"].shape[1]
    KT = D // P
    TT = S // P
    CW = T["conv_w"].shape[1]
    HP = 4
    SCALE = float(HEAD_DIM) ** -0.5
    assert FF == FF_STEPS * UC and UNITS % RING == 0 and U_LOOP % RING == 2

    with ExitStack() as ctx:
        def sb(name, shape, dt=F32):
            return ctx.enter_context(nc.sbuf_tensor(name, shape, dt))

        def sem(name):
            return ctx.enter_context(nc.semaphore(name))

        raw = [sb(f"raw{s}", [P, 8 * UC]) for s in range(RING)]
        w_hi = [sb(f"w_hi{s}", [P, 8 * UC], F32R) for s in range(RING)]
        w_lo = [sb(f"w_lo{s}", [P, 8 * UC], F32R) for s in range(RING)]
        x_res = sb("x_res", [P, KT, S])
        sq = sb("sq", [P, KT, S])
        act_hi = sb("act_hi", [P, KT, S], F32R)
        act_lo = sb("act_lo", [P, KT, S], F32R)
        gates = sb("gates", [P, 4 * KT, S])
        qk = sb("qk", [P, 8, S])
        rot = sb("rot", [P, 2, S])
        v_sb = sb("v_sb", [P, TT, 512])
        y_hi = sb("y_hi", [P, 10, S], F32R)
        y_lo = sb("y_lo", [P, 10, S], F32R)
        conv_h = sb("conv_h", [P, 2, 32 + S])
        xa = sb("xa", [P, 2, PAD + S])
        ff_hi = sb("ff_hi", [P, 2, 2, S], F32R)
        ff_lo = sb("ff_lo", [P, 2, 2, S], F32R)
        yd_f = sb("yd_f", [P, 2, S])
        rms_b = sb("rms_b", [P, 1, S])
        cos_r = sb("cos_r", [P, 1, S])
        sin_r = sb("sin_r", [P, 1, S])

        def part(owner, a, shape):
            flat = owner.rearrange("p k s -> p (k s)") if len(owner.shape) == 3 else owner
            n = int(np.prod(shape))
            return flat[:, a:a + n].rearrange("p (i j) -> p i j", j=shape[-1]) if len(shape) == 2 else flat[:, a:a + n]

        conv_a, swish_t = rot, rot
        glu_t = yd_f
        probs = part(sq[:, :, :], 0, [2, 3 * P])
        probsT = part(sq[:, :, :], 6 * P, [2, 3 * P])
        conv_n = part(sq[:, :, :], 12 * P, [TT, 256])
        E = PAD + S
        g_b = gates[:, KT:2 * KT, :]
        s2, s4 = part(g_b, 0, [2, E]), part(g_b, 2 * E, [2, E])
        s8, s16 = part(g_b, 4 * E, [E]), part(g_b, E, [E])
        conv_p = gates[:, 2 * KT - 2:2 * KT, :]
        g_d = gates[:, 3 * KT:4 * KT, :]
        zv, zu = g_d[:, 0:2, :], g_d[:, 2:4, :]
        yc_f, ya_f, pooled = g_d[:, 4:6, :], g_d[:, 0:2, :], g_d[:, 6:8, :]
        mtmp = part(qk[:, :, :], 0, [2, 2 * S])
        ff_g, ff_u, ff_a = (qk[:, 2 * i:2 * i + 2, :] for i in range(3))
        rows = sb("rows", [N_ROWS, P])
        gain_rows = sb("gain_rows", [2 * L * KT, P])
        gains = sb("gains", [P, 2 * L * KT])
        par = sb("par", [P, N_ROWS])
        half_bg = sb("half_bg", [P, 32])
        ln_g = sb("ln_g", [P, 256])
        ln_b = sb("ln_b", [P, 256])
        sgu_bias = sb("sgu_bias", [P, 2, P])
        pool_w = sb("pool_w", [P, 2, P])
        ws_nat = sb("ws_nat", [P, 4, P])
        wsT = sb("wsT", [P, 4, P])
        ident = sb("ident", [P, P])
        ones = sb("ones", [P, P])
        zeros = sb("zeros", [P, 2 * S], BF16)
        rot_perm = sb("rot_perm", [P, P])
        causal = sb("causal", [P, 384], BF16)
        ident16 = sb("ident16", [P, P], BF16)
        angles = sb("angles", [P, 2, S])
        icnt = sb("icnt", [P, 2, S])
        ifreq = sb("ifreq", [P, 1])
        st = sb("st", [P, 16])
        ist = sb("ist", [P, 4], I32)
        rms_t = sb("rms_t", [P, TT])
        diag = sb("diag", [P, TT, P])
        bn6 = sb("bn6", [P, TT, 6])
        mv = sb("mv", [P, TT, 2])
        mx = sb("mx", [P, 4])
        nmx = sb("nmx", [P, 4])
        den = sb("den", [P, 4])
        rden = sb("rden", [P, 4])
        ssq = sb("ssq", [P, 4])

        bank = [ctx.enter_context(nc.psum_tensor(f"bank{b}", [P, 512], F32)) for b in range(8)]

        raw_full = [sem(f"raw_full{s}") for s in range(RING)]
        raw_claimed = sem("raw_claimed")
        hi_ready = [sem(f"hi_ready{s}") for s in range(RING)]
        lo_ready = [sem(f"lo_ready{s}") for s in range(RING)]
        w_used = [sem(f"w_used{s}") for s in range(RING)]
        bank_free = [sem(f"bank_free{b}") for b in range(8)]
        x_ready = sem("x_ready")
        sq_done = sem("sq_done")
        ssum_ready = sem("ssum_ready")
        stat_done = sem("stat_done")
        diag_ready = sem("diag_ready")
        rms_done = sem("rms_done")
        rms_ready = sem("rms_ready")
        table_ready = sem("table_ready")
        glu_ready = sem("glu_ready")
        gelu_done = sem("gelu_done")
        gate_ready = sem("gate_ready")
        rden_ready = sem("rden_ready")
        pj_done = sem("pj_done")
        ydp_done = sem("ydp_done")
        swish_ready = sem("swish_ready")
        silu_done = sem("silu_done")
        ffa_ready = sem("ffa_ready")
        act_hi_ready = sem("act_hi_ready")
        act_lo_ready = sem("act_lo_ready")
        par_done = sem("par_done")
        perm_done = sem("perm_done")
        rope_ready = sem("rope_ready")
        tri_ready = sem("tri_ready")
        wst_done = sem("wst_done")
        vn_ready = sem("vn_ready")
        f_done = sem("f_done")
        yc_ready = sem("yc_ready")
        pooled_ready = sem("pooled_ready")
        pool_done = sem("pool_done")
        conv_tap = sem("conv_tap")
        conv_mul = sem("conv_mul")
        conv_tap2 = sem("conv_tap2")
        ct1_done = sem("ct1_done")
        ct2_done = sem("ct2_done")
        yd_ready = sem("yd_ready")
        s_done = sem("s_done")
        nmx_ready = sem("nmx_ready")
        probs_ready = sem("probs_ready")
        pt_done = sem("pt_done")
        pv_done = sem("pv_done")
        yhi_ready = sem("yhi_ready")
        ylo_ready = sem("ylo_ready")
        merged_ready = sem("merged_ready")
        madd_done = sem("madd_done")
        ffhi_ready = sem("ffhi_ready")
        fflo_ready = sem("fflo_ready")
        mats_seen = sem("mats_seen")
        rows_in = sem("rows_in")
        mats_in = sem("mats_in")
        params_free = sem("params_free")
        dve_chain = sem("dve_chain")
        pool_chain = sem("pool_chain")
        x_in = [sem(f"x_in{i}") for i in range(4)]
        gain_in = sem("gain_in")
        pos_in = sem("pos_in")
        icnt_in = sem("icnt_in")
        gfin_in = sem("gfin_in")
        pre_const = sem("pre_const")
        pre_x0 = sem("pre_x0")
        pre_dve = sem("pre_dve")
        pre_act = sem("pre_act")
        pre_pe = sem("pre_pe")
        out_done = sem("out_done")

        def free_at(l, b, what, after=False):
            return l * len(BANKS[b]) + (BANKS[b].index(what) + (2 if after else 1))

        def kview(t):
            return t[:, :].rearrange("p (k n) -> p k n", n=UC)

        def wide(t):
            return t[:, :].rearrange("p (k n) -> p k n", n=D)

        def low(b):
            return bank[b][:, :].rearrange("p (f s) -> p f s", f=2)

        x_nat = gates[:, 0:8, :].rearrange("p k s -> p (k s)").rearrange("p (t d) -> p t d", t=TT)
        g_fin = gates[:, 8:12, :].rearrange("p k s -> p (k s)")
        o_nat = gates[:, 16:24, :].rearrange("p k s -> p (k s)").rearrange("p (t d) -> p t d", t=TT)
        pos_i = gates[:, 8, :].bitcast(I32)
        junk = gates[:, 24:32, :].rearrange("p k s -> p (k s)").rearrange("p (h n) -> p h n", h=4)

        block = ctx.enter_context(nc.Block())

        @block.sync
        def _(sp):
            for i in range(4):
                cs = slice(i * 2 * P, (i + 1) * 2 * P)
                sp.dma_start(x_nat[:, :, cs], T["x"][0].rearrange("(t p) d -> p t d", p=P)[:, :, cs])\
                    .then_inc(x_in[i], 16)

            def load(l, slot, use, src, n=UC):
                sp.wait_ge(lo_ready[slot], l * USES + use + 1)
                sp.sem_inc(raw_claimed, 1)
                sp.dma_start(raw[slot][:, :].rearrange("p (k n) -> p k n", n=n), src)\
                    .then_inc(raw_full[slot], 16)

            def cols(w, l, c0):
                return w[l].rearrange("(k p) n -> p k n", p=P)[:, :, c0:c0 + UC]

            def down(l, r0):
                return T["w_ffn_out"][l].rearrange("(j k p) n -> j p k n", p=P, k=2)[r0]

            def ffn_load(l, kind, j, slot, use):
                if kind == "G":
                    load(l, slot, use, T["w_ffn_in"][l].rearrange("(k p) (h j n) -> h j p k n", p=P, h=2, n=UC)[0, j])
                elif kind == "U":
                    load(l, slot, use, T["w_ffn_in"][l].rearrange("(k p) (h j n) -> h j p k n", p=P, h=2, n=UC)[1, j])
                else:
                    load(l, slot, use, down(l, j), n=D)

            with sp.Fori(0, L) as l:
                for u in range(U_FFN):
                    slot, use = u % RING, u // RING
                    if u < U_GATE:
                        load(l, slot, use, cols(T["w_in"], l, W_IN_UNITS[u][1]))
                    elif gate_of(u):
                        branch, dp = gate_of(u)
                        load(l, slot, use, cols(T["w_gate"], l, branch * D + dp * UC))
                    elif u in (U_PROJ_A, U_PROJ_C, U_PROJ_D):
                        w = T["w_proj_" + {U_PROJ_A: "a", U_PROJ_C: "c", U_PROJ_D: "d"}[u]]
                        load(l, slot, use, w[l].rearrange("(k p) n -> p k n", p=P), n=D)
                    elif u < U_WO:
                        load(l, slot, use, T["w_proj_b"][l].rearrange("(j k p) n -> j p k n", p=P, k=2)[u - U_PROJ_B],
                             n=D)
                    else:
                        load(l, slot, use, cols(T["w_o"], l, (u - U_WO) * UC))
                ffn_load(l, "G", 0, U_FFN % RING, U_FFN // RING)
                ffn_load(l, "U", 0, (U_FFN + 1) % RING, (U_FFN + 1) // RING)
                with sp.Fori(0, FF_ITERS) as it:
                    for c in range(6):
                        ffn_load(l, "GUO"[c % 3], it * 2 + c // 3 + (c % 3 != 2),
                                 (U_LOOP + c) % RING, it * 2 + (U_LOOP + c) // RING)
                for u in range(U_TAIL, UNITS):
                    c = u - U_TAIL
                    kind = "GUO"[c % 3] if u < UNITS - 1 else "O"
                    j = J_TAIL + c // 3 - (kind == "O") if u < UNITS - 1 else FF_STEPS - 1
                    ffn_load(l, kind, j, u % RING, u // RING)

            sp.wait_ge(x_ready, 8 * L)
            sp.dma_start(g_fin, T["final_norm_g"].partition_broadcast(P)).then_inc(gfin_in, 16)
            for t in range(TT):
                sp.wait_ge(pre_dve, PRE_DVE_OUT + t + 1)
                sp.dma_start(out[0].rearrange("(t p) d -> t p d", p=P)[t], o_nat[:, t, :])\
                    .then_inc(out_done, 16)
            sp.wait_ge(out_done, 16 * TT)

        @block.gpsimd
        def _(pool):
            nc.gpsimd.memset(ident[:, :], 0.0).then_inc(pre_const, 1)
            pool.wait_ge(pre_const, 1)
            nc.gpsimd.affine_select(out=ident[:, :], in_=ident[:, :], compare_op=ALU.not_equal, fill=1.0,
                                    base=0, pattern=[[-1, P]], channel_multiplier=1).then_inc(pre_const, 1)
            nc.gpsimd.memset(ones[:, :], 1.0).then_inc(pre_const, 1)
            nc.gpsimd.memset(rot_perm[:, :], 0.0)
            nc.gpsimd.memset(causal[:, :], 0.0)
            nc.gpsimd.memset(zeros[:, :], 0.0)
            nc.gpsimd.memset(conv_h[:, :, :], 0.0)
            nc.gpsimd.memset(pool_w[:, :, :], 0.0)
            nc.gpsimd.memset(xa[:, :, 0:PAD], 0.0).then_inc(pre_const, 1)
            pool.wait_ge(pre_const, 4)
            nc.gpsimd.tensor_copy(ident16[:, :], ident[:, :])
            for m0 in range(0, P, 32):
                first = m0 % HEAD_DIM == 0
                src0 = m0 + 32 if first else m0 - 32
                blk = rot_perm[:, m0:m0 + 32]
                nc.gpsimd.affine_select(out=blk, in_=blk, compare_op=ALU.not_equal, fill=-1.0 if first else 1.0,
                                        base=-src0, pattern=[[-1, 32]], channel_multiplier=1)
            for c0 in (0, 2 * P):
                blk = causal[:, c0:c0 + P]
                last = nc.gpsimd.affine_select(out=blk, in_=blk, compare_op=ALU.is_ge, fill=NEG,
                                               base=0, pattern=[[-1, P]], channel_multiplier=1)
            last.then_inc(pre_const, 1)
            pool.sem_inc(madd_done, 1)
            pool.dma_start(icnt[:, :, :], inv_count).then_inc(icnt_in, 16)

            n = [0]

            def link(l, ins):
                n[0] += 1
                ins.then_inc(pool_chain, 1)
                pool.wait_ge(pool_chain, l * POOL_CHAIN_PER_LAYER + n[0])

            def conv_taps2(l, w0, w1):
                for w in range(w0, w1):
                    c = ROWS["conv_w"][0] + 2 * w + 1
                    src = conv_h[:, 1, 32 - (CW - 1) + w:32 - (CW - 1) + w + S]
                    if w == 0:
                        ins = nc.gpsimd.tensor_tensor(conv_a[:, 1, :], src, par[:, c:c + 1].to_broadcast([P, S]),
                                                      ALU.mult)
                    else:
                        tmp = conv_p[:, w % 2, :]
                        pool.wait_ge(conv_tap2, l * (CW + 1) + w)
                        nc.gpsimd.tensor_tensor(tmp, src, par[:, c:c + 1].to_broadcast([P, S]), ALU.mult)\
                            .then_inc(conv_mul, 1)
                        pool.wait_ge(conv_mul, l * (CW - 1) + w)
                        ins = nc.gpsimd.tensor_tensor(conv_a[:, 1, :], conv_a[:, 1, :], tmp, ALU.add)
                    ins.then_inc(conv_tap2, 1)

            with pool.Fori(0, L) as l:
                pool.wait_ge(params_free, l + 1)
                for name, (r0, k) in ROWS.items():
                    src = T[name][l]
                    if name == "conv_w":
                        src = src.rearrange("w (c p) -> (w c) p", p=P)
                    else:
                        src = src.rearrange("(r p) -> r p", p=P)
                    pool.dma_start(rows[r0:r0 + k, :], src).then_inc(rows_in, 16)
                pool.dma_start(ws_nat[:, :, :], T["sgu_w"][l].rearrange("g t s -> t g s")).then_inc(mats_in, 16)
                pool.dma_start(ln_g[:, :], T["sgu_norm_g"][l].partition_broadcast(P)).then_inc(mats_in, 16)
                pool.dma_start(ln_b[:, :], T["sgu_norm_b"][l].partition_broadcast(P)).then_inc(mats_in, 16)
                for g in range(4):
                    half = slice(64 * (g % 2), 64 * (g % 2) + 64)
                    pool.dma_start(sgu_bias[half, g // 2, :], T["sgu_b"][l, g].partition_broadcast(64))\
                        .then_inc(mats_in, 16)
                    pool.dma_start(pool_w[half, g // 2, half], T["pool_w"][l, g]).then_inc(mats_in, 16)
                pool.wait_ge(mats_in, l * (16 * 11) + 16 * 11)
                pool.sem_inc(mats_seen, 1)
                nc.gpsimd.affine_select(out=ws_nat[:, :, :], in_=ws_nat[:, :, :], compare_op=ALU.is_ge, fill=0.0,
                                        base=0, pattern=[[0, 4], [-1, P]], channel_multiplier=1).then_inc(tri_ready, 1)
                pool.wait_ge(bank_free[2], free_at(l, 2, "unit6", True))
                conv_taps2(l, 0, POOL_TAPS_FIRST)
                pool.wait_ge(bank_free[2], free_at(l, 2, "unit10", True))
                pool.wait_ge(icnt_in, 16)
                link(l, nc.gpsimd.tensor_tensor(s2[:, :, 1:E], xa[:, :, 1:E], xa[:, :, 0:E - 1], ALU.add))
                link(l, nc.gpsimd.tensor_tensor(s4[:, :, 4:E], s2[:, :, 4:E], s2[:, :, 2:E - 2], ALU.add))
                link(l, nc.gpsimd.tensor_tensor(s8[:, 8:E], s4[:, 1, 8:E], s4[:, 1, 4:E - 4], ALU.add))
                link(l, nc.gpsimd.tensor_tensor(s16[:, 16:E], s8[:, 16:E], s8[:, 8:E - 8], ALU.add))
                for g, total in enumerate((s2[:, 0], s4[:, 0], s8, s16)):
                    half = slice(64 * (g % 2), 64 * (g % 2) + 64)
                    link(l, nc.gpsimd.tensor_tensor(pooled[half, g // 2, :], total[half, PAD:E],
                                                    icnt[half, g // 2, :], ALU.mult))
                nc.gpsimd.tensor_tensor(pooled[:, :, :], pooled[:, :, :], xa[:, :, PAD:E], ALU.subtract)\
                    .then_inc(pooled_ready, 1)
                conv_taps2(l, POOL_TAPS_FIRST, CW)
                cb = ROWS["conv_b"][0] + 1
                pool.wait_ge(conv_tap2, l * (CW + 1) + CW)
                nc.gpsimd.tensor_tensor(conv_a[:, 1, :], conv_a[:, 1, :], par[:, cb:cb + 1].to_broadcast([P, S]), ALU.add)\
                    .then_inc(conv_tap2, 1)
                for i in range(8):
                    dp = i % 4
                    b, which = (4 + dp, "C") if i < 4 else (dp, "B")
                    pool.wait_ge(bank_free[b], free_at(l, b, which, True))
                    m = gates[:, 2 * dp:2 * dp + 2, :].rearrange("p f s -> p (f s)")
                    nc.gpsimd.tensor_tensor(m, m, mtmp[:, i % 2, :], ALU.add).then_inc(madd_done, 1)
            assert n[0] == POOL_CHAIN_PER_LAYER

        @block.scalar
        def _(act):
            act.dma_start(pos_i, T["positions"].to_broadcast([P, S])).then_inc(pos_in, 16)
            act.dma_start(ifreq[:, :], inv_freq).then_inc(pos_in, 16)
            for i, name in enumerate(("norm_mix_g", "norm_ffn_g")):
                act.dma_start(gain_rows[i * L * KT:(i + 1) * L * KT, :], T[name].rearrange("l (r p) -> (l r) p", p=P))\
                    .then_inc(gain_in, 16)
            for s in range(RING):
                act.sem_inc(w_used[s], 1)
            for b in range(8):
                act.sem_inc(bank_free[b], 1)

            def copy(o, i):
                return nc.scalar.activation(o, i, ACT.Copy)

            def split(l, slot, use):
                act.wait_ge(raw_full[slot], (l * USES + use + 1) * 16)
                act.wait_ge(w_used[slot], l * USES + use + 1)
                copy(w_hi[slot][:, :], raw[slot][:, :]).then_inc(hi_ready[slot], 1)

            def xg_hi(l, n, i):
                act.wait_ge(x_ready, l * 8 + (4 * n + i + 1))
                for f in range(2):
                    k = 2 * i + f
                    last = nc.scalar.activation(act_hi[:, k, :], x_res[:, k, :], ACT.Copy,
                                                scale=gains[:, bass.ds(l * KT + (n * L * KT + k), 1)])
                last.then_inc(act_hi_ready, 1)

            def square(l, n, i):
                act.wait_ge(x_ready, l * 8 + (4 * n + i + 1))
                nc.scalar.activation(sq[:, 2 * i:2 * i + 2, :], x_res[:, 2 * i:2 * i + 2, :], ACT.Square)\
                    .then_inc(sq_done, 1)

            def rms_copy(l, n):
                b, what = (6, "R1") if n == 0 else (3, "R2")
                act.wait_ge(rms_done, l * 2 + (n + 1))
                copy(rms_b[:, 0, :], bank[b][:, 0:S]).then_inc(bank_free[b], 1)

            def unit_done(l, u):
                act.wait_ge(w_used[u % RING], l * USES + (u // RING + 2))

            def evac(l, u):
                b = u % 4
                if u < 4:
                    unit_done(l, u)
                    copy(qk[:, 2 * u:2 * u + 2, :], low(b)).then_inc(bank_free[b], 1)
                elif u in (4, 7, 8):
                    unit_done(l, u)
                    act.wait_ge(diag_ready, l * 2 + 1)
                    for t in range(TT):
                        if u == 4:
                            last = nc.scalar.activation(zv[:, t, :], low(b)[:, t, :], ACT.Gelu_apprx_tanh,
                                                        scale=rms_t[:, t:t + 1])
                        else:
                            last = nc.scalar.activation(v_sb[:, t, (u - 7) * UC:(u - 6) * UC], low(b)[:, t, :],
                                                        ACT.Copy, scale=rms_t[:, t:t + 1])
                    last.then_inc(bank_free[b], 1)
                elif u == 5:
                    act.wait_ge(bank_free[b], free_at(l, b, "unit5", True))
                    nc.scalar.activation(glu_t[:, :, :], glu_t[:, :, :], ACT.Tanh, scale=0.5).then_inc(glu_ready, 1)
                elif u == 9:
                    act.wait_ge(bank_free[b], free_at(l, b, "unit9", True))
                    nc.scalar.activation(zu, zu, ACT.Gelu_apprx_tanh).then_inc(gelu_done, 1)
                elif gate_of(u):
                    branch, dp = gate_of(u)
                    act.wait_ge(bank_free[b], free_at(l, b, f"unit{u}", True))
                    for f in range(2):
                        k = branch * KT + 2 * dp + f
                        last = nc.scalar.activation(gates[:, k, :], gates[:, k, :], ACT.Tanh, scale=0.5,
                                                    bias=half_bg[:, k:k + 1])
                    last.then_inc(gate_ready, 1)
                    if branch == 3:
                        act.wait_ge(merged_ready, l * 4 + dp + 1)
                        copy(y_hi[:, 2 * dp:2 * dp + 2, :], gates[:, 2 * dp:2 * dp + 2, :]).then_inc(act_hi_ready, 1)
                elif U_WO <= u < U_FFN:
                    xg_hi(l, 1, u - U_WO)

            def misc(l, u):
                if u == 0:
                    act.wait_ge(par_done, l + 1)
                    copy(par[:, :], bank[6][:, 0:N_ROWS])
                    r0, k = ROWS["b_gate"]
                    nc.scalar.activation(half_bg[:, :], bank[6][:, r0:r0 + k], ACT.Copy, scale=0.5)\
                        .then_inc(bank_free[6], 1)
                    act.wait_ge(bank_free[6], free_at(l, 6, "par", True))
                if u == 2:
                    rms_copy(l, 0)
                if u == 7:
                    act.wait_ge(wst_done, l + 1)
                    copy(wsT[:, :, :], bank[6][:, :].rearrange("p (g s) -> p g s", g=4)).then_inc(bank_free[6], 1)
                if u in ATT:
                    hp = ATT.index(u)
                    act.wait_ge(nmx_ready, l * HP + hp + 1)
                    for i in range(2):
                        for q, (a, b) in enumerate(((0, P), (P, 3 * P))):
                            c = 2 * q + i
                            last = nc.scalar.activation(probs[:, i, a:b], bank[4 + i][:, a:b], ACT.Exp, scale=SCALE,
                                                        bias=nmx[:, c:c + 1], accum_out=den[:, c:c + 1])
                        last.then_inc(bank_free[4 + i], 1)
                if u - 1 in ATT:
                    hp = ATT.index(u - 1)
                    act.wait_ge(rden_ready, l * HP + hp + 1)
                    for i in range(2):
                        for q, (a, b) in enumerate(((0, P), (P, 3 * P))):
                            c = 2 * q + i
                            last = nc.scalar.activation(probs[:, i, a:b], probs[:, i, a:b], ACT.Copy,
                                                        scale=rden[:, c:c + 1])
                    last.then_inc(probs_ready, 1)
                if u - 2 in ATT:
                    hp = ATT.index(u - 2)
                    for i in range(2):
                        act.wait_ge(pt_done, l * 2 * HP + 2 * hp + i + 1)
                        copy(probsT[:, i, :], bank[6 + i][:, 0:3 * P]).then_inc(bank_free[6 + i], 1)
                if u - 3 in ATT:
                    hp = ATT.index(u - 3)
                    act.wait_ge(pv_done, l * HP + hp + 1)
                    copy(y_hi[:, 2 + hp, :], bank[6][:, 0:S]).then_inc(yhi_ready, 1)
                if u == 14:
                    act.wait_ge(yc_ready, l + 1)
                    copy(y_hi[:, 6:8, :], yc_f).then_inc(yhi_ready, 1)
                if u == 16:
                    act.wait_ge(pool_done, l + 1)
                    for f in range(2):
                        c = ROWS["pool_scale"][0] + f
                        last = nc.scalar.activation(ya_f[:, f, :], bank[7][:, f * S:(f + 1) * S], ACT.Copy,
                                                    scale=par[:, c:c + 1])
                    last.then_inc(bank_free[7], 1)
                    act.wait_ge(bank_free[7], free_at(l, 7, "pool", True))
                    copy(y_hi[:, 0:2, :], ya_f).then_inc(yhi_ready, 1)
                if u == 20:
                    act.wait_ge(ct2_done, l + 1)
                    for f in range(2):
                        cg, cb = ROWS["conv_norm_g"][0] + f, ROWS["conv_norm_b"][0] + f
                        last = nc.scalar.activation(yd_f[:, f, :], bank[5][:, f * S:(f + 1) * S], ACT.Identity,
                                                    scale=par[:, cg:cg + 1], bias=par[:, cb:cb + 1])
                    last.then_inc(bank_free[5], 1)
                    act.wait_ge(bank_free[5], free_at(l, 5, "cT2", True))
                    nc.scalar.activation(swish_t[:, :, :], yd_f[:, :, :], ACT.Tanh, scale=0.5).then_inc(swish_ready, 1)
                if u == 22:
                    act.wait_ge(yd_ready, l + 1)
                    copy(y_hi[:, 8:10, :], yd_f[:, :, :]).then_inc(yhi_ready, 1)
                if U_WO <= u < U_FFN:
                    square(l, 1, u - U_WO)

            def ffn_silu(l, even, it):
                b = 0 if even else 2
                act.wait_ge(bank_free[b], l * len(BANKS[b]) + (it + (FFN_FROM[b] + (3 if even else 2))))
                nc.scalar.activation(ff_g, ff_g, ACT.Silu).then_inc(silu_done, 1)

            def ffn_hi(l, even, j):
                act.wait_ge(ffa_ready, l * FF_STEPS + (j + 1))
                copy(ff_hi[:, 0 if even else 1, :, :], ff_a).then_inc(ffhi_ready, 1)

            act.wait_ge(pre_pe, 1)
            copy(gains[:, :], bank[0][:, 0:2 * L * KT]).then_inc(pre_act, 1)
            act.wait_ge(pre_act, 1)

            with act.Fori(0, L) as l:
                split(l, 0, 0)
                split(l, 1, 0)
                for step, i in ((xg_hi, 0), (square, 0), (xg_hi, 1), (square, 1), (xg_hi, 2), (xg_hi, 3),
                                (square, 2), (square, 3)):
                    step(l, 0, i)
                act.wait_ge(pre_dve, PRE_DVE_ROPE)
                nc.scalar.activation(sin_r[:, 0, :], angles[:, 0, :], ACT.Sin)
                nc.scalar.activation(cos_r[:, 0, :], angles[:, 1, :], ACT.Sin).then_inc(table_ready, 1)
                split(l, 2, 0)
                for u in range(U_FFN):
                    urgent = u in (U_WO - 1, U_FFN - 1)
                    if not urgent:
                        split(l, (u + 3) % RING, (u + 3) // RING)
                    evac(l, u)
                    misc(l, u)
                    if urgent:
                        split(l, (u + 3) % RING, (u + 3) // RING)
                split(l, (U_FFN + 3) % RING, (U_FFN + 3) // RING)
                rms_copy(l, 1)
                ffn_silu(l, True, -1)
                ffn_hi(l, True, 0)

                def ffn_unit(l, base_u, use0, it, c):
                    ahead = c + 2
                    split(l, (base_u + ahead) % RING, use0 + ((base_u + ahead) // RING - base_u // RING))
                    if c % 3 == 0:
                        ffn_silu(l, c == 3, it)
                    elif c % 3 == 1:
                        ffn_hi(l, c == 4, it * 2 + (c // 3 + 1))

                with act.Fori(0, FF_ITERS) as it:
                    for c in range(6):
                        ffn_unit(l, U_LOOP, it * 2 + U_LOOP // RING, it, c)
                for c in range(5):
                    ffn_unit(l, U_TAIL, U_TAIL // RING, FF_ITERS, c)

            for n, h in enumerate((0, 2, 1, 3)):
                act.wait_ge(pre_pe, 2 + n)
                nc.scalar.activation(junk[:, h, :], bank[h][:, :], ACT.Square, accum_out=ssq[:, h:h + 1]).then_inc(pre_act, 1)

        @block.tensor
        def _(pe):
            def mm3(o, whi, wlo, ahi, alo, first, last, skip=False):
                nc.tensor.matmul(o, whi, ahi, start=first, stop=False, skip_group_check=skip)
                nc.tensor.matmul(o, whi, alo, start=False, stop=False, skip_group_check=skip)
                return nc.tensor.matmul(o, wlo, ahi, start=False, stop=last, skip_group_check=skip)

            def weights(l, slot, use):
                pe.wait_ge(lo_ready[slot], l * USES + use + 2)

            def bank_wait(l, b, what):
                pe.wait_ge(bank_free[b], free_at(l, b, what))

            def unit(l, slot, b, a_hi=act_hi, a_lo=act_lo):
                hi, lo = kview(w_hi[slot]), kview(w_lo[slot])
                for f in range(2):
                    fs = slice(f * P, f * P + P)
                    for k in range(KT):
                        last = mm3(low(b)[:, f, :], hi[:, k, fs], lo[:, k, fs], a_hi[:, k, :], a_lo[:, k, :],
                                   k == 0, k == KT - 1)
                last.then_inc(w_used[slot], 1)

            def unit_early(l, slot, b, ready, a_hi=act_hi, a_lo=act_lo):
                hi, lo = kview(w_hi[slot]), kview(w_lo[slot])
                for i in range(KT // 2):
                    pe.wait_ge(act_lo_ready, ready + (i + 1))
                    for f in range(2):
                        fs = slice(f * P, f * P + P)
                        for k in (2 * i, 2 * i + 1):
                            last = mm3(low(b)[:, f, :], hi[:, k, fs], lo[:, k, fs], a_hi[:, k, :], a_lo[:, k, :],
                                       k == 0 and f == 0, k == KT - 1, skip=True)
                last.then_inc(w_used[slot], 1)

            def unit_natural(slot, b):
                hi, lo = kview(w_hi[slot]), kview(w_lo[slot])
                for t in range(TT):
                    ts = slice(t * P, t * P + P)
                    for k in range(KT):
                        o = low(b)[:, t, :]
                        nc.tensor.matmul(o, act_hi[:, k, ts], hi[:, k, :], start=(k == 0), stop=False)
                        nc.tensor.matmul(o, act_hi[:, k, ts], lo[:, k, :], start=False, stop=False)
                        last = nc.tensor.matmul(o, act_lo[:, k, ts], hi[:, k, :], start=False, stop=(k == KT - 1))
                last.then_inc(w_used[slot], 1)

            def unit_rows(slot, b0, hi_in, lo_in, first, last_k, done=None, order=range(4), free=None):
                hi, lo = wide(w_hi[slot]), wide(w_lo[slot])
                for nth, dp in enumerate(order):
                    if free is not None:
                        bank_wait(free[0], b0 + dp, free[1])
                    for f in range(2):
                        fs = slice((2 * dp + f) * P, (2 * dp + f + 1) * P)
                        for k in range(2):
                            last = mm3(low(b0 + dp)[:, f, :], hi[:, k, fs], lo[:, k, fs], hi_in[k], lo_in[k],
                                       first and f == 0 and k == 0, last_k and k == 1, skip=True)
                    if done is not None and nth < 3:
                        last.then_inc(done, 1)
                last.then_inc(w_used[slot], 1)

            def norm_stat(l, n):
                b, what = (7, "stat1") if n == 0 else (2, "stat2")
                bank_wait(l, b, what)
                pe.wait_ge(ssum_ready, l * 2 + (n + 1))
                for t in range(TT):
                    last = nc.tensor.matmul(bank[b][:, t:t + 1], sq[:, 0, t * P:t * P + P], ones[:, 0:1],
                                            start=True, stop=True)
                last.then_inc(stat_done, 1)

            def norm_rms(l, n):
                b, what = (6, "R1") if n == 0 else (3, "R2")
                bank_wait(l, b, what)
                pe.wait_ge(diag_ready, l * 2 + (n + 1))
                for t in range(TT):
                    last = nc.tensor.matmul(bank[b][:, t * P:t * P + P], ones[:, :], diag[:, t, :], start=True, stop=True)
                last.then_inc(rms_done, 1)

            def misc(l, u):
                if u == 0:
                    pe.wait_ge(rows_in, l * (16 * len(ROWS)) + 16 * len(ROWS))
                    bank_wait(l, 6, "par")
                    nc.tensor.transpose(bank[6][:, 0:N_ROWS], rows[:, :], ident[0:N_ROWS, 0:N_ROWS])\
                        .then_inc(par_done, 1)
                if u == 1:
                    norm_stat(l, 0)
                if u == 2:
                    norm_rms(l, 0)
                if 3 <= u <= 6:
                    i = u - 3
                    bank_wait(l, 4 + i, f"perm{i}")
                    pe.wait_ge(bank_free[i], free_at(l, i, f"unit{i}", True))
                    nc.tensor.matmul(bank[4 + i][:, :], rot_perm[:, :],
                                     qk[:, 2 * i:2 * i + 2, :].rearrange("p f s -> p (f s)"),
                                     start=True, stop=True).then_inc(perm_done, 1)
                if u == 7:
                    bank_wait(l, 6, "wsT")
                    pe.wait_ge(tri_ready, l + 1)
                    for g in range(4):
                        last = nc.tensor.transpose(bank[6][:, g * P:(g + 1) * P], ws_nat[:, g, :], ident[:, :])
                    last.then_inc(wst_done, 1)
                if u in ATT:
                    hp = ATT.index(u)
                    if hp == 0:
                        pe.wait_ge(rope_ready, l * 4 + 4)
                    for i in range(2):
                        bank_wait(l, 4 + i, f"S{hp}")
                        h = slice(64 * i, 64 * i + 64)
                        s_bank = bank[4 + i]
                        nc.tensor.matmul(s_bank[:, 0:3 * P], ident16[:, :], causal[:, :], start=True, stop=False,
                                         skip_group_check=True)
                        nc.tensor.matmul(s_bank[:, 0:P], qk[h, hp, 0:P], qk[h, 4 + hp, 0:P], start=False, stop=False,
                                         skip_group_check=True)
                        nc.tensor.matmul(s_bank[:, P:3 * P], qk[h, hp, P:2 * P], qk[h, 4 + hp, :],
                                         start=False, stop=True, skip_group_check=True).then_inc(s_done, 1)
                if u - 2 in ATT:
                    hp = ATT.index(u - 2)
                    pe.wait_ge(probs_ready, l * HP + hp + 1)
                    for i in range(2):
                        bank_wait(l, 6 + i, f"PT{hp}")
                        for c in range(3):
                            last = nc.tensor.transpose(bank[6 + i][:, c * P:(c + 1) * P], probs[:, i, c * P:(c + 1) * P],
                                                       ident[:, :])
                        last.then_inc(pt_done, 1)
                if u == 13:
                    bank_wait(l, 7, "F")
                    pe.wait_ge(vn_ready, l + 1)
                    pe.wait_ge(bank_free[6], free_at(l, 6, "wsT", True))
                    for g in range(4):
                        for t in range(TT):
                            c0 = (g // 2) * S + t * P
                            last = nc.tensor.matmul(bank[7][64 * (g % 2):64 * (g % 2) + 64, c0:c0 + P],
                                                    zv[:, t, g * 64:(g + 1) * 64], wsT[:, g, :], start=True, stop=True)
                    last.then_inc(f_done, 1)
                if u - 3 in ATT:
                    hp = ATT.index(u - 3)
                    for i in range(2):
                        pe.wait_ge(bank_free[6 + i], free_at(l, 6 + i, f"PT{hp}", True))
                        o = bank[6][64 * i:64 * i + 64, :]
                        c0 = (2 * hp + i) * HEAD_DIM
                        nc.tensor.matmul(o[:, 0:S], v_sb[:, 0, c0:c0 + HEAD_DIM], probsT[:, i, 0:2 * P],
                                         start=True, stop=False, skip_group_check=True)
                        last = nc.tensor.matmul(o[:, P:S], v_sb[:, 1, c0:c0 + HEAD_DIM], probsT[:, i, 2 * P:3 * P],
                                                start=False, stop=True, skip_group_check=True)
                    last.then_inc(pv_done, 1)
                if u == 16:
                    bank_wait(l, 7, "pool")
                    pe.wait_ge(pooled_ready, l + 1)
                    for f in range(2):
                        last = nc.tensor.matmul(bank[7][:, f * S:(f + 1) * S], pool_w[:, f, :], pooled[:, f, :],
                                                start=True, stop=True)
                    last.then_inc(pool_done, 1)
                if u == 17:
                    bank_wait(l, 5, "cT1")
                    pe.wait_ge(conv_tap, l * CW + CW)
                    pe.wait_ge(conv_tap2, l * (CW + 1) + (CW + 1))
                    for t in range(TT):
                        for f in range(2):
                            last = nc.tensor.transpose(bank[5][:, t * 256 + f * P:t * 256 + (f + 1) * P],
                                                       conv_a[:, f, t * P:(t + 1) * P], ident[:, :])
                    last.then_inc(ct1_done, 1)
                if u == 20:
                    bank_wait(l, 5, "cT2")
                    pe.wait_ge(bank_free[5], free_at(l, 5, "cT1", True))
                    for t in range(TT):
                        for f in range(2):
                            last = nc.tensor.transpose(bank[5][:, f * S + t * P:f * S + (t + 1) * P],
                                                       conv_n[:, t, f * P:(f + 1) * P], ident[:, :])
                    last.then_inc(ct2_done, 1)

            def ffn_in(l, slot, use, b, it):
                weights(l, slot, use)
                pe.wait_ge(bank_free[b], l * len(BANKS[b]) + (it + (FFN_FROM[b] + 1)))
                unit(l, slot, b)

            def ffn_out(l, slot, use, even, j, last_unit=False):
                weights(l, slot, use)
                pe.wait_ge(fflo_ready, l * FF_STEPS + (j + 1))
                e = 0 if even else 1
                unit_rows(slot, 4, [ff_hi[:, e, k, :] for k in range(2)], [ff_lo[:, e, k, :] for k in range(2)],
                          False, last_unit, done=ydp_done if last_unit else None)

            def proj(l, u):
                which, k0, b0, ready = {U_PROJ_A: ("A", 0, 0, 1), U_PROJ_C: ("C", 6, 4, 1), U_PROJ_B: ("B", 2, 0, 2),
                                        U_PROJ_B + 1: ("B", 4, 0, 2), U_PROJ_D: ("D", 8, 4, 3)}[u]
                pe.wait_ge(ylo_ready, l * 3 + ready)
                first, complete = u != U_PROJ_B + 1, u != U_PROJ_B
                unit_rows(u % RING, b0, [y_hi[:, k0 + k, :] for k in range(2)], [y_lo[:, k0 + k, :] for k in range(2)],
                          first, complete, done=pj_done if complete and which != "D" else None,
                          order=ORDER_A if which == "A" else range(4), free=(l, which) if first else None)

            pe.wait_ge(pre_const, 3)
            pe.wait_ge(gain_in, 16 * 2)
            nc.tensor.transpose(bank[0][:, 0:2 * L * KT], gain_rows[:, :], ident[0:2 * L * KT, 0:2 * L * KT])\
                .then_inc(pre_pe, 1)
            for i in range(4):
                pe.wait_ge(x_in[i], 16)
                for f in range(2):
                    for t in range(TT):
                        k = 2 * i + f
                        last = nc.tensor.transpose(low(4 + i)[:, f, t * P:(t + 1) * P], x_nat[:, t, k * P:(k + 1) * P],
                                                   ident[:, :])
                last.then_inc(ydp_done, 1)
            pe.wait_ge(pre_act, 1)
            pe.wait_ge(pre_const, 5)

            with pe.Fori(0, L) as l:
                for u in range(U_WO):
                    weights(l, u % RING, u // RING)
                    if u < U_PROJ_A or u >= U_GATE_D:
                        bank_wait(l, u % 4, f"unit{u}")
                    if u == 0:
                        unit_early(l, u % RING, u % 4, l * 12)
                    elif u < N_IN and W_IN_UNITS[u][0] in ("v", "sgu_v"):
                        unit_natural(u % RING, u % 4)
                    elif u < U_PROJ_A or u >= U_GATE_D:
                        unit(l, u % RING, u % 4)
                    else:
                        proj(l, u)
                    misc(l, u)
                for i in range(4):
                    u = U_WO + i
                    weights(l, u % RING, u // RING)
                    pe.wait_ge(bank_free[i], free_at(l, i, f"unit{U_GATE_D + i}", True))
                    if i == 0:
                        unit_early(l, u % RING, i, l * 12 + 4, y_hi, y_lo)
                    else:
                        unit(l, u % RING, i, y_hi, y_lo)
                pe.wait_ge(x_ready, l * 8 + 6)
                weights(l, U_FFN % RING, U_FFN // RING)
                unit_early(l, U_FFN % RING, 0, l * 12 + 8)
                norm_stat(l, 1)
                ffn_in(l, (U_FFN + 1) % RING, (U_FFN + 1) // RING, 1, 0)
                norm_rms(l, 1)
                for b in range(4, 8):
                    pe.wait_ge(bank_free[b], free_at(l, b, "D", True))
                    nc.tensor.matmul(bank[b][:, :], zeros[:, 0:P], zeros[:, :], start=True, stop=False,
                                     skip_group_check=True)

                def ffn_pair(l, c, use0, it):
                    for h in range(2):
                        b = 0 if h else 2
                        uses = [use0 + ((c + 3 * h + i) // RING - c // RING) for i in range(3)]
                        ffn_in(l, (c + 3 * h) % RING, uses[0], b, it + h)
                        ffn_in(l, (c + 3 * h + 1) % RING, uses[1], b + 1, it + h)
                        ffn_out(l, (c + 3 * h + 2) % RING, uses[2], h == 0, it * 2 + h)

                with pe.Fori(0, FF_ITERS) as it:
                    ffn_pair(l, U_LOOP, it * 2 + U_LOOP // RING, it)
                ffn_pair(l, U_TAIL, U_TAIL // RING, FF_ITERS)
                u = UNITS - 1
                ffn_out(l, u % RING, u // RING, True, FF_STEPS - 1, last_unit=True)

            for n, h in enumerate((0, 2, 1, 3)):
                if n % 2 == 0:
                    pe.wait_ge(x_ready, 8 * L + (2 if n == 0 else 4))
                for c in range(4):
                    k = 4 * (h % 2) + c
                    last = nc.tensor.transpose(bank[h][:, c * P:(c + 1) * P], x_res[:, k, (h // 2) * P:(h // 2 + 1) * P],
                                               ident[:, :])
                last.then_inc(pre_pe, 1)

        @block.vector
        def _(dve):
            for s in range(RING):
                dve.sem_inc(lo_ready[s], 1)
            dve.sem_inc(params_free, 1)
            V = nc.vector
            n = [0]
            pre = [0]

            def link(l, ins):
                if l is None:
                    pre[0] += 1
                    ins.then_inc(pre_dve, 1)
                    dve.wait_ge(pre_dve, pre[0])
                else:
                    n[0] += 1
                    ins.then_inc(dve_chain, 1)
                    dve.wait_ge(dve_chain, l * DVE_CHAIN_PER_LAYER + n[0])

            def rsqrt(l, o, v, tmp, bits):
                link(l, V.tensor_scalar(bits, v.bitcast(I32), 1, None, ALU.logical_shift_right))
                link(l, V.tensor_scalar(v, v, -0.5, None, ALU.mult))
                link(l, V.tensor_scalar(o.bitcast(I32), bits, -1.0, float(0x5F3759DF), ALU.mult, ALU.add))
                for _ in range(3):
                    link(l, V.tensor_tensor(tmp, o, o, ALU.mult))
                    link(l, V.tensor_tensor(tmp, tmp, v, ALU.mult))
                    link(l, V.scalar_tensor_tensor(o, tmp, 1.5, o, ALU.add, ALU.mult))

            def split(l, slot, use):
                dve.wait_ge(hi_ready[slot], l * USES + use + 1)
                V.tensor_tensor(w_lo[slot][:, :], raw[slot][:, :], w_hi[slot][:, :].bitcast(F32), ALU.subtract)\
                    .then_inc(lo_ready[slot], 1)

            def x_update(l, n, i):
                xv = x_res[:, 2 * i:2 * i + 2, :]
                if n == 0:
                    V.tensor_tensor(xv, low(4 + i), xv, ALU.add).then_inc(x_ready, 1)
                else:
                    V.scalar_tensor_tensor(xv, low(i), 0.5, xv, ALU.mult, ALU.add).then_inc(x_ready, 1)

            def y_wait(l, i):
                if i < 3:
                    dve.wait_ge(ydp_done, l * 3 + (i + 2))
                else:
                    dve.wait_ge(w_used[(UNITS - 1) % RING], l * USES + 1)

            def xg_lo(l, n, i):
                dve.wait_ge(act_hi_ready, l * 12 + (8 * n + i + 1))
                for f in range(2):
                    k = 2 * i + f
                    last = V.scalar_tensor_tensor(act_lo[:, k, :], x_res[:, k, :],
                                                  gains[:, bass.ds(l * KT + (n * L * KT + k), 1)],
                                                  act_hi[:, k, :].bitcast(F32), ALU.mult, ALU.subtract)
                last.then_inc(act_lo_ready, 1)

            def square_sum(l, n, i):
                dve.wait_ge(sq_done, l * 8 + (4 * n + i + 1))
                link(l, V.tensor_tensor(sq[:, 0:2, :], sq[:, 0:2, :], sq[:, 2 * i:2 * i + 2, :], ALU.add))
                if i == 3:
                    V.tensor_tensor(sq[:, 0, :], sq[:, 0, :], sq[:, 1, :], ALU.add).then_inc(ssum_ready, 1)

            def norm_scale(l, n):
                b, what = (7, "stat1") if n == 0 else (2, "stat2")
                dve.wait_ge(stat_done, l * 2 + (n + 1))
                V.tensor_scalar(st[:, 0:2], bank[b][:, 0:2], 1.0 / D, EPS, ALU.mult, ALU.add).then_inc(bank_free[b], 1)
                dve.wait_ge(bank_free[b], free_at(l, b, what, True))
                rsqrt(l, rms_t[:, 0:2], st[:, 0:2], st[:, 4:6], ist[:, 0:2])
                for t in range(TT):
                    last = V.tensor_scalar(diag[:, t, :], ident[:, :], rms_t[:, t:t + 1], None, ALU.mult)
                last.then_inc(diag_ready, 1)

            def scaled(out, b, l):
                return V.tensor_tensor(out, low(b), rms_b[:, :, :].to_broadcast([P, 2, S]), ALU.mult)

            def unit_done(l, u):
                dve.wait_ge(w_used[u % RING], l * USES + (u // RING + 2))

            def lo_of(o_lo, src, o_hi, count, l):
                dve.wait_ge(yhi_ready, l * 7 + count)
                return V.tensor_tensor(o_lo, src, o_hi.bitcast(F32), ALU.subtract)

            def conv_taps(l, w0, w1):
                for w in range(w0, w1):
                    c = ROWS["conv_w"][0] + 2 * w
                    src = conv_h[:, 0, 32 - (CW - 1) + w:32 - (CW - 1) + w + S]
                    if w == 0:
                        cb = ROWS["conv_b"][0]
                        ins = V.tensor_scalar(conv_a[:, 0, :], src, par[:, c:c + 1], par[:, cb:cb + 1],
                                              ALU.mult, ALU.add)
                    else:
                        dve.wait_ge(conv_tap, l * CW + w)
                        ins = V.scalar_tensor_tensor(conv_a[:, 0, :], src, par[:, c:c + 1], conv_a[:, 0, :],
                                                     ALU.mult, ALU.add)
                    ins.then_inc(conv_tap, 1)

            def misc(l, u):
                if 3 <= u <= 6:
                    i = u - 3
                    if i == 0:
                        dve.wait_ge(bank_free[6], free_at(l, 6, "R1", True))
                        dve.wait_ge(table_ready, l + 1)
                        link(l, V.tensor_tensor(cos_r[:, :, :], cos_r[:, :, :], rms_b[:, :, :], ALU.mult))
                        link(l, V.tensor_tensor(sin_r[:, :, :], sin_r[:, :, :], rms_b[:, :, :], ALU.mult))
                    else:
                        dve.wait_ge(rope_ready, l * 4 + i)
                    r = rot[:, :, :]
                    dst = qk[:, 2 * i:2 * i + 2, :]
                    dve.wait_ge(perm_done, l * 4 + i + 1)
                    V.tensor_tensor(r, low(4 + i), sin_r[:, :, :].to_broadcast([P, 2, S]), ALU.mult)\
                        .then_inc(bank_free[4 + i], 1)
                    link(l, V.tensor_tensor(dst, dst, cos_r[:, :, :].to_broadcast([P, 2, S]), ALU.mult))
                    dve.wait_ge(bank_free[4 + i], free_at(l, 4 + i, f"perm{i}", True))
                    V.tensor_tensor(dst, dst, r, ALU.add).then_inc(rope_ready, 1)
                if u == 5:
                    unit_done(l, 5)
                    scaled(glu_t[:, :, :], 1, l).then_inc(bank_free[1], 1)
                if u == 6:
                    dve.wait_ge(glu_ready, l + 1)
                    link(l, V.tensor_scalar(glu_t[:, :, :], glu_t[:, :, :], 0.5, 0.5, ALU.mult, ALU.add))
                    link(l, V.tensor_tensor(glu_t[:, :, :], glu_t[:, :, :], rms_b[:, :, :].to_broadcast([P, 2, S]),
                                            ALU.mult))
                    unit_done(l, 6)
                    V.tensor_tensor(conv_h[:, :, 32:32 + S], glu_t[:, :, :], low(2), ALU.mult)\
                        .then_inc(bank_free[2], 1)
                    dve.wait_ge(bank_free[2], free_at(l, 2, "unit6", True))
                if u == 9:
                    unit_done(l, 9)
                    scaled(zu, 1, l).then_inc(bank_free[1], 1)
                if u == 10:
                    unit_done(l, 10)
                    scaled(xa[:, :, PAD:PAD + S], 2, l).then_inc(bank_free[2], 1)
                if gate_of(u):
                    branch, dp = gate_of(u)
                    k = branch * KT + 2 * dp
                    unit_done(l, u)
                    scaled(gates[:, k:k + 2, :], u % 4, l).then_inc(bank_free[u % 4], 1)
                if u == 8:
                    dve.wait_ge(bank_free[0], free_at(l, 0, "unit4", True))
                    for t in range(TT):
                        link(l, V.bn_stats(bn6[:, t, :], zv[:, t, :]))
                        V.memset(st[:, 14:15], 0.0)
                        link(l, V.bn_aggr(mv[:, t, :], bn6[:, t, :]))
                    link(l, V.tensor_scalar(st[:, 8:10], mv[:, :, 1], EPS, None, ALU.add))
                    rsqrt(l, st[:, 10:12], st[:, 8:10], st[:, 12:14], ist[:, 2:4])
                    for t in range(TT):
                        link(l, V.tensor_scalar(zv[:, t, :], zv[:, t, :], mv[:, t, 0:1], st[:, 10 + t:11 + t],
                                                ALU.subtract, ALU.mult))
                    dve.wait_ge(mats_seen, l + 1)
                    link(l, V.tensor_tensor(zv[:, :, :], zv[:, :, :],
                                            ln_g[:, :].unsqueeze(1).to_broadcast([P, TT, 256]), ALU.mult))
                    V.tensor_tensor(zv[:, :, :], zv[:, :, :],
                                    ln_b[:, :].unsqueeze(1).to_broadcast([P, TT, 256]), ALU.add).then_inc(vn_ready, 1)
                if u in ATT:
                    hp = ATT.index(u)
                    for i in range(2):
                        dve.wait_ge(s_done, l * 2 * HP + 2 * hp + i + 1)
                        V.tensor_reduce(mx[:, i:i + 1], bank[4 + i][:, 0:P], AX.X, ALU.max)
                        last = V.tensor_reduce(mx[:, 2 + i:3 + i], bank[4 + i][:, P:3 * P], AX.X, ALU.max)
                    link(l, last)
                    V.tensor_scalar(nmx[:, :], mx[:, :], -SCALE, None, ALU.mult).then_inc(nmx_ready, 1)
                if u - 1 in ATT:
                    hp = ATT.index(u - 1)
                    for i in range(2):
                        dve.wait_ge(bank_free[4 + i], free_at(l, 4 + i, f"S{hp}", True))
                    V.reciprocal(rden[:, :], den[:, :]).then_inc(rden_ready, 1)
                if u == 13:
                    dve.wait_ge(f_done, l + 1)
                    for f in range(2):
                        last = V.tensor_tensor(yc_f[:, f, :].rearrange("p (t s) -> p t s", t=TT),
                                               bank[7][:, f * S:(f + 1) * S].rearrange("p (t s) -> p t s", t=TT),
                                               sgu_bias[:, f:f + 1, :].to_broadcast([P, TT, P]), ALU.add)
                    last.then_inc(bank_free[7], 1)
                    dve.wait_ge(bank_free[7], free_at(l, 7, "F", True))
                    dve.wait_ge(gelu_done, l + 1)
                    V.tensor_tensor(yc_f, yc_f, zu[:, :, :], ALU.mult).then_inc(yc_ready, 1)
                if u - 3 in ATT:
                    hp = ATT.index(u - 3)
                    count = (1, 3, 5, 6)[hp]
                    last = lo_of(y_lo[:, 2 + hp, :], bank[6][:, 0:S], y_hi[:, 2 + hp, :], count, l)
                    last.then_inc(bank_free[6], 1)
                    if hp == HP - 1:
                        dve.wait_ge(bank_free[6], free_at(l, 6, f"PV{hp}", True))
                        dve.sem_inc(ylo_ready, 1)
                if u == 15:
                    lo_of(y_lo[:, 6:8, :], yc_f, y_hi[:, 6:8, :], 2, l)
                if u == 17:
                    lo_of(y_lo[:, 0:2, :], ya_f, y_hi[:, 0:2, :], 4, l).then_inc(ylo_ready, 1)
                    dve.wait_ge(ylo_ready, l * 3 + 1)
                    dve.sem_inc(params_free, 1)
                if u == 17:
                    dve.wait_ge(ct1_done, l + 1)
                    nat = bank[5][:, :].rearrange("p (t c) -> p t c", t=TT)
                    for t in range(TT):
                        link(l, V.bn_stats(bn6[:, t, :], nat[:, t, :]))
                        V.memset(st[:, 14:15], 0.0)
                        link(l, V.bn_aggr(mv[:, t, :], bn6[:, t, :]))
                    link(l, V.tensor_scalar(st[:, 8:10], mv[:, :, 1], EPS, None, ALU.add))
                    rsqrt(l, st[:, 10:12], st[:, 8:10], st[:, 12:14], ist[:, 2:4])
                    for t in range(TT):
                        last = V.tensor_scalar(conv_n[:, t, :], nat[:, t, :], mv[:, t, 0:1], st[:, 10 + t:11 + t],
                                               ALU.subtract, ALU.mult)
                    last.then_inc(bank_free[5], 1)
                if u == 21:
                    dve.wait_ge(swish_ready, l + 1)
                    link(l, V.tensor_scalar(swish_t[:, :, :], swish_t[:, :, :], 0.5, 0.5, ALU.mult, ALU.add))
                    V.tensor_tensor(yd_f[:, :, :], yd_f[:, :, :], swish_t[:, :, :], ALU.mult).then_inc(yd_ready, 1)
                if u == 23:
                    lo_of(y_lo[:, 8:10, :], yd_f[:, :, :], y_hi[:, 8:10, :], 7, l).then_inc(ylo_ready, 1)
                if u in TAPS:
                    w0 = sum(TAPS[v] for v in TAPS if v < u)
                    conv_taps(l, w0, w0 + TAPS[u])

            def gated(which, dp, b, o):
                k = {"A": 0, "B": 1, "C": 2, "D": 3}[which] * KT + 2 * dp
                return V.scalar_tensor_tensor(o, gates[:, k:k + 2, :], 1.0, low(b), ALU.add, ALU.mult)

            def merge(l, u):
                if u in (U_PROJ_A, U_PROJ_C, U_PROJ_B + 1):
                    nth, which, b0 = {U_PROJ_A: (0, "A", 0), U_PROJ_C: (1, "C", 4), U_PROJ_B + 1: (2, "B", 0)}[u]
                    if which == "A":
                        dve.wait_ge(gate_ready, l * 16 + 12)
                    for i, dp in enumerate(ORDER_A if which == "A" else range(4)):
                        if i < 3:
                            dve.wait_ge(pj_done, l * 9 + (3 * nth + i + 1))
                        else:
                            unit_done(l, u)
                        b, m = b0 + dp, gates[:, 2 * dp:2 * dp + 2, :]
                        tmp = mtmp[:, dp % 2, :].rearrange("p (f s) -> p f s", f=2)
                        if which == "A":
                            gated(which, dp, b, m).then_inc(bank_free[b], 1)
                        else:
                            i = 4 * (nth - 1) + dp
                            if i >= 1:
                                dve.wait_ge(madd_done, l * 8 + i)
                            gated(which, dp, b, tmp).then_inc(bank_free[b], 1)
                if U_GATE_D <= u < U_WO:
                    dp = u - U_GATE_D
                    b, m, g = 4 + dp, gates[:, 2 * dp:2 * dp + 2, :], gates[:, 3 * KT + 2 * dp:3 * KT + 2 * dp + 2, :]
                    if dp == 0:
                        dve.wait_ge(madd_done, l * 8 + 9)
                    else:
                        merged_lo(l, dp - 1)
                    if dp < 3:
                        split(l, (u + 3) % RING, (u + 3) // RING)
                    dve.wait_ge(gate_ready, l * 16 + (13 + dp))
                    gated("D", dp, b, g).then_inc(bank_free[b], 1)
                    dve.wait_ge(bank_free[b], free_at(l, b, "D", True))
                    V.tensor_tensor(m, m, g, ALU.add).then_inc(merged_ready, 1)
                    if dp == 3:
                        merged_lo(l, 3)
                if U_WO <= u < U_FFN:
                    i = u - U_WO
                    unit_done(l, u)
                    x_update(l, 1, i)
                    if i >= 1:
                        xg_lo(l, 1, i - 1)
                    if i >= 2:
                        square_sum(l, 1, i - 1)
                    if i == 3:
                        xg_lo(l, 1, 3)
                        square_sum(l, 1, 3)

            def merged_lo(l, i):
                dve.wait_ge(act_hi_ready, l * 12 + (4 + i + 1))
                V.tensor_tensor(y_lo[:, 2 * i:2 * i + 2, :], gates[:, 2 * i:2 * i + 2, :],
                                y_hi[:, 2 * i:2 * i + 2, :].bitcast(F32), ALU.subtract).then_inc(act_lo_ready, 1)

            def ffn_gate(l, slot, use, even, j):
                b = 0 if even else 2
                if j is not None:
                    dve.wait_ge(ffa_ready, l * FF_STEPS + j)
                dve.wait_ge(w_used[slot], l * USES + (use + 2))
                scaled(ff_g, b, l).then_inc(bank_free[b], 1)

            def ffn_up(l, slot, use, even, j, it):
                b = 1 if even else 3
                dve.wait_ge(w_used[slot], l * USES + (use + 2))
                scaled(ff_u, b, l).then_inc(bank_free[b], 1)
                if j is not None:
                    dve.wait_ge(fflo_ready, l * FF_STEPS + j)
                dve.wait_ge(bank_free[b], l * len(BANKS[b]) + (it + (FFN_FROM[b] + (3 if even else 2))))
                dve.wait_ge(silu_done, l * FF_STEPS + (1 if j is None else j + 1))
                V.tensor_tensor(ff_a, ff_g, ff_u, ALU.mult).then_inc(ffa_ready, 1)

            def ffn_lo(l, even, j):
                e = 0 if even else 1
                dve.wait_ge(ffhi_ready, l * FF_STEPS + (j + 1))
                V.tensor_tensor(ff_lo[:, e, :, :], ff_a, ff_hi[:, e, :, :].bitcast(F32), ALU.subtract)\
                    .then_inc(fflo_ready, 1)

            V.memset(x_res[:, :, :], 0.0).then_inc(pre_x0, 1)
            dve.wait_ge(pre_x0, 1)
            dve.wait_ge(pos_in, 16 * 2)
            posf, ang, turns = sq[:, 0, :], sq[:, 1, :], sq[:, 2:4, :]
            angb = sq[:, 1:2, :].to_broadcast([P, 2, S])
            magic = 1.5 * 2.0 ** 23
            c1 = 6.28125
            c2 = float(np.float32(np.round((2 * np.pi - c1) * 2 ** 20) / 2 ** 20))
            c3 = float(np.float32(2 * np.pi - c1 - c2))
            link(None, V.tensor_copy(posf, pos_i))
            link(None, V.tensor_scalar(ang, posf, ifreq[:, 0:1], None, ALU.mult))
            V.tensor_scalar(turns[:, 0, :], ang, 1.0 / (2 * np.pi), None, ALU.mult)
            link(None, V.tensor_scalar(turns[:, 1, :], ang, 1.0 / (2 * np.pi), 0.25, ALU.mult, ALU.add))
            link(None, V.tensor_scalar(turns, turns, magic, None, ALU.add))
            link(None, V.tensor_scalar(turns, turns, magic, None, ALU.subtract))
            link(None, V.scalar_tensor_tensor(angles[:, :, :], turns, -c1, angb, ALU.mult, ALU.add))
            link(None, V.scalar_tensor_tensor(angles[:, :, :], turns, -c2, angles[:, :, :], ALU.mult, ALU.add))
            link(None, V.scalar_tensor_tensor(angles[:, :, :], turns, -c3, angles[:, :, :], ALU.mult, ALU.add))
            V.tensor_scalar(angles[:, 0, :], angles[:, 0, :], 3.1415925, None, ALU.min)
            link(None, V.tensor_scalar(angles[:, 1, :], angles[:, 1, :], 0.5 * np.pi, 3.1415925, ALU.add, ALU.min))
            link(None, V.tensor_scalar(angles[:, :, :], angles[:, :, :], -3.1415925, None, ALU.max))
            assert pre[0] == PRE_DVE_ROPE
            dve.wait_ge(pre_act, 1)
            dve.wait_ge(pre_const, 5)

            with dve.Fori(0, L) as l:
                split(l, 0, 0)
                for i in range(4):
                    y_wait(l, i)
                    x_update(l, 0, i)
                    if i >= 1:
                        xg_lo(l, 0, i - 1)
                xg_lo(l, 0, 3)
                split(l, 1, 0)
                for i in range(1, 4):
                    square_sum(l, 0, i)
                split(l, 2, 0)
                for u in range(U_FFN):
                    if u == 1:
                        norm_scale(l, 0)
                    misc(l, u)
                    merge(l, u)
                    if not U_GATE_D <= u < U_WO - 1:
                        split(l, (u + 3) % RING, (u + 3) // RING)
                norm_scale(l, 1)
                split(l, (U_FFN + 3) % RING, (U_FFN + 3) // RING)
                dve.wait_ge(bank_free[3], free_at(l, 3, "R2", True))
                ffn_gate(l, U_FFN % RING, U_FFN // RING, True, None)
                ffn_up(l, (U_FFN + 1) % RING, (U_FFN + 1) // RING, True, None, -1)
                ffn_lo(l, True, 0)

                def ffn_unit(l, base_u, use0, it, c):
                    ahead = c + 2
                    split(l, (base_u + ahead) % RING, use0 + ((base_u + ahead) // RING - base_u // RING))
                    use, slot = use0 + ((base_u + c) // RING - base_u // RING), (base_u + c) % RING
                    j = it * 2 + (c // 3 + 1)
                    if c % 3 == 0:
                        ffn_gate(l, slot, use, c == 3, j)
                    if c % 3 == 1:
                        ffn_up(l, slot, use, c == 4, j, it)
                    if c % 3 == 2:
                        ffn_lo(l, c == 5, j)

                with dve.Fori(0, FF_ITERS) as it:
                    for c in range(6):
                        ffn_unit(l, U_LOOP, it * 2 + U_LOOP // RING, it, c)
                for c in range(5):
                    ffn_unit(l, U_TAIL, U_TAIL // RING, FF_ITERS, c)
                ffn_lo(l, True, FF_STEPS - 1)
            assert n[0] == DVE_CHAIN_PER_LAYER, n[0]

            for i in range(4):
                y_wait(L, i)
                x_update(L, 0, i)
            dve.wait_ge(gfin_in, 16)
            dve.wait_ge(pre_act, 5)
            pre[0] = PRE_DVE_ROPE
            link(None, V.tensor_tensor(st[:, 0:2], ssq[:, 0:4:2], ssq[:, 1:4:2], ALU.add))
            link(None, V.tensor_scalar(st[:, 0:2], st[:, 0:2], 1.0 / D, EPS, ALU.mult, ALU.add))
            rsqrt(None, st[:, 2:4], st[:, 0:2], st[:, 4:6], ist[:, 0:2])
            assert pre[0] == PRE_DVE_OUT, pre[0]
            for h in range(4):
                ins = V.scalar_tensor_tensor(o_nat[:, h // 2, 512 * (h % 2):512 * (h % 2) + 512], bank[h][:, :],
                                             st[:, 2 + h // 2:3 + h // 2], g_fin[:, 512 * (h % 2):512 * (h % 2) + 512],
                                             ALU.mult, ALU.mult)
                if h % 2:
                    ins.then_inc(pre_dve, 1)


_INS = ["x", "positions", "norm_mix_g", "w_in", "w_gate", "b_gate", "pool_w", "pool_scale", "sgu_norm_g",
        "sgu_norm_b", "sgu_w", "sgu_b", "conv_w", "conv_b", "conv_norm_g", "conv_norm_b", "w_proj_a",
        "w_proj_b", "w_proj_c", "w_proj_d", "w_o", "norm_ffn_g", "w_ffn_in", "w_ffn_out", "final_norm_g"]


def kernel(**inputs):
    import numpy as _np
    import concourse.bacc as _bacc
    from concourse import mybir as _mybir
    from concourse.bass_utils import run_bass_kernel_spmd as _run

    nc = _bacc.Bacc("TRN2", target_bir_lowering=False, num_devices=1)
    arrays, T = {}, {}
    for name in _INS:
        a = _np.ascontiguousarray(inputs[name])
        arrays[f"in_{name}"] = a
        T[name] = nc.dram_tensor(f"in_{name}", a.shape, _mybir.dt.from_np(a.dtype), kind="ExternalInput").ap()
    S = inputs["x"].shape[1]
    half = HEAD_DIM // 2
    freq = (1.0 / (_np.float32(ROPE_THETA) ** (_np.arange(half, dtype=_np.float32) / half))).astype(_np.float32)
    consts = {
        "inv_freq": _np.tile(freq, P // half).reshape(P, 1),
        "inv_count": _np.stack([_np.repeat([1.0 / _np.minimum(_np.arange(S) + 1, w) for w in WINDOWS[2 * f:2 * f + 2]],
                                           P // 2, axis=0) for f in range(2)], axis=1).astype(_np.float32),
    }
    aps = {}
    for name, a in consts.items():
        arrays[name] = _np.ascontiguousarray(a)
        aps[name] = nc.dram_tensor(name, a.shape, _mybir.dt.float32, kind="ExternalInput").ap()
    out = nc.dram_tensor("out", inputs["x"].shape, _mybir.dt.float32, kind="ExternalOutput").ap()
    build(nc, T, out, aps["inv_freq"], aps["inv_count"])
    r = _run(nc, [arrays], core_ids=[0])
    return r.results[0]["out"]
```
